# Optimizing a Trainium2 kernel written in Bass

```python
import jax, jax.numpy as jnp
from jax import lax
import numpy as np
import math
import jax
import jax.numpy as jnp

D_MODEL = 1024
BATCH = 1
SEQ = 256
DEPTH = 2

EPS = 1e-6
GRID_W = 64
D_MIX = D_MODEL
HEAD_DIM = 64
ATT_HEADS = (D_MIX // 2) // HEAD_DIM
ATT_KV_HEADS = 2
ATT_GROUP = ATT_HEADS // ATT_KV_HEADS
ATT_WIDTH = ATT_HEADS * HEAD_DIM
KV_WIDTH = ATT_KV_HEADS * HEAD_DIM
ATT_SCALE = HEAD_DIM ** -0.5
Q_BLOCK = 128
ROPE_THETA = 10000.0
ROPE_AXIS_DIM = HEAD_DIM // 2
HGRN_WIDTH = D_MIX // 4
HGRN_DK = 64
HGRN_DV = 64
HGRN_HEADS = HGRN_WIDTH // HGRN_DV
HGRN_CHUNK = 16
CONV_WIDTH = D_MIX - ATT_WIDTH - HGRN_WIDTH
CONV_KERNEL = 31
CONV_PAD = (CONV_KERNEL - 1) // 2
D_FF = 4 * D_MODEL
IN_COLS = ATT_WIDTH + 2 * KV_WIDTH + 5 * HGRN_WIDTH + 2 * CONV_WIDTH


def _in_split_points():
    sizes = [ATT_WIDTH, KV_WIDTH, KV_WIDTH, HGRN_WIDTH, HGRN_WIDTH, HGRN_WIDTH,
             HGRN_WIDTH, HGRN_WIDTH, CONV_WIDTH, CONV_WIDTH]
    points, acc = [], 0
    for s in sizes[:-1]:
        acc += s
        points.append(acc)
    return points

def rms_norm(x, g):
    xf = x.astype(jnp.float32)
    y = xf * lax.rsqrt(jnp.mean(xf * xf, axis=-1, keepdims=True) + EPS)
    return (y * g.astype(jnp.float32)).astype(x.dtype)

def layer_norm(x, g, b):
    xf = x.astype(jnp.float32)
    mu = jnp.mean(xf, axis=-1, keepdims=True)
    xc = xf - mu
    y = xc * lax.rsqrt(jnp.mean(xc * xc, axis=-1, keepdims=True) + EPS)
    return (y * g.astype(jnp.float32) + b.astype(jnp.float32)).astype(x.dtype)

def _rope_angles(pos):
    inv_freq = ROPE_THETA ** (-jnp.arange(0, ROPE_AXIS_DIM, 2, dtype=jnp.float32) / ROPE_AXIS_DIM)
    ang = pos.astype(jnp.float32)[:, None] * inv_freq[None, :]
    return jnp.cos(ang), jnp.sin(ang)

def _rotate(x, cos, sin):
    half = x.shape[-1] // 2
    x1, x2 = x[..., :half], x[..., half:]
    c, s = cos[None, :, None, :], sin[None, :, None, :]
    return jnp.concatenate([x1 * c - x2 * s, x1 * s + x2 * c], axis=-1)

def apply_axial_rope(x, row_cs, col_cs):
    xf = x.astype(jnp.float32)
    out = jnp.concatenate([_rotate(xf[..., :ROPE_AXIS_DIM], *row_cs),
                           _rotate(xf[..., ROPE_AXIS_DIM:], *col_cs)], axis=-1)
    return out.astype(x.dtype)

def block_attention(q, k, v):
    B, L, H, D = q.shape
    nb = L // Q_BLOCK
    qb = q.reshape(B, nb, Q_BLOCK, ATT_KV_HEADS, ATT_GROUP, D).transpose(1, 0, 2, 3, 4, 5)

    def one_block(q_blk):
        s = jnp.einsum("bqhgd,bkhd->bhgqk", q_blk, k).astype(jnp.float32) * ATT_SCALE
        p = jax.nn.softmax(s, axis=-1)
        return jnp.einsum("bhgqk,bkhd->bqhgd", p.astype(v.dtype), v)

    o = lax.map(one_block, qb)
    return o.transpose(1, 0, 2, 3, 4, 5).reshape(B, L, H * D)

def chunk_gated_recurrence(q, k, v, log_f):
    B, L, H, K = q.shape
    V = v.shape[-1]
    C = HGRN_CHUNK
    N = L // C

    def to_chunks(a):
        return a.reshape(B, N, C, H, a.shape[-1]).transpose(0, 3, 1, 2, 4)

    q, k, v, log_f = (to_chunks(a) for a in (q, k, v, log_f))
    b = jnp.cumsum(log_f, axis=3)
    causal = jnp.tril(jnp.ones((C, C), dtype=bool))[:, :, None]
    diff = b[:, :, :, :, None, :] - b[:, :, :, None, :, :]
    decay = jnp.where(causal, jnp.exp(jnp.where(causal, diff, 0.0)), 0.0)
    scores = jnp.einsum("bhnik,bhnjk,bhnijk->bhnij", q, k, decay)
    o_intra = jnp.einsum("bhnij,bhnjv->bhniv", scores, v)
    b_last = b[:, :, :, -1:, :]
    u = jnp.einsum("bhnjk,bhnjv->bhnkv", k * jnp.exp(b_last - b), v)
    chunk_decay = jnp.exp(b_last[:, :, :, 0, :])

    def step(S, inp):
        dec, uu = inp
        return dec[..., None] * S + uu, S

    S0 = jnp.zeros((B, H, K, V), q.dtype)
    _, S_prev = lax.scan(step, S0, (jnp.moveaxis(chunk_decay, 2, 0), jnp.moveaxis(u, 2, 0)))
    S_prev = jnp.moveaxis(S_prev, 0, 2)
    o_inter = jnp.einsum("bhnik,bhnkv->bhniv", q * jnp.exp(b), S_prev)
    return (o_intra + o_inter).transpose(0, 2, 3, 1, 4).reshape(B, L, H, V)

def _layer_lower_bounds(lb_param):
    p = jax.nn.softmax(lb_param.astype(jnp.float32), axis=0)
    return jnp.cumsum(p, axis=0) - p[0:1]

def _forget_gate(z, lb):
    zf = z.astype(jnp.float32)
    log_f = jax.nn.log_sigmoid(zf) + jnp.log1p(lb * jnp.exp(-zf))
    k = (1.0 - lb) * jax.nn.sigmoid(-zf)
    return log_f, k

def hgrn2_bidirectional(q_h, i_h, f_fw, f_bw, g_h, lb_fw, lb_bw, norm_g):
    B, L, _ = q_h.shape
    heads = lambda a: a.astype(jnp.float32).reshape(B, L, HGRN_HEADS, -1)
    q, v = heads(q_h), heads(i_h)
    lb_fw = lb_fw.reshape(HGRN_HEADS, HGRN_DK)
    lb_bw = lb_bw.reshape(HGRN_HEADS, HGRN_DK)
    logf_fw, k_fw = _forget_gate(heads(f_fw), lb_fw)
    logf_bw, k_bw = _forget_gate(heads(f_bw), lb_bw)
    flip = lambda a: jnp.flip(a, axis=1)
    o_fw = chunk_gated_recurrence(q, k_fw, v, logf_fw)
    o_bw = flip(chunk_gated_recurrence(flip(q), flip(k_bw), flip(v), flip(logf_bw)))
    o = rms_norm(o_fw + o_bw, norm_g.reshape(HGRN_HEADS, HGRN_DV))
    o = o.reshape(B, L, HGRN_WIDTH) * jax.nn.silu(g_h.astype(jnp.float32))
    return o.astype(q_h.dtype)

def conformer_conv(a, gate, w_dw, b_dw, ln_g, ln_b):
    u = a * jax.nn.sigmoid(gate)
    y = lax.conv_general_dilated(u, w_dw[:, None, :], window_strides=(1,),
                                 padding=[(CONV_PAD, CONV_PAD)],
                                 dimension_numbers=("NWC", "WIO", "NWC"),
                                 feature_group_count=CONV_WIDTH)
    y = layer_norm(y + b_dw, ln_g, ln_b)
    return jax.nn.silu(y)

def first_inputs(seed: int = 0) -> dict:
    key = jax.random.key(seed)
    ks = jax.random.split(key, 16)
    n = lambda k, shape: jax.random.normal(k, shape, jnp.float32)
    return {
        "x": n(ks[0], (BATCH, SEQ, D_MODEL)),
        "w_in": n(ks[1], (DEPTH, D_MODEL, IN_COLS)) * D_MODEL ** -0.5,
        "w_out": n(ks[2], (DEPTH, D_MIX, D_MODEL)) * D_MIX ** -0.5,
        "norm_mix": 1.0 + 0.05 * n(ks[3], (DEPTH, D_MODEL)),
        "norm_mlp": 1.0 + 0.05 * n(ks[4], (DEPTH, D_MODEL)),
        "q_norm": 1.0 + 0.05 * n(ks[5], (DEPTH, HEAD_DIM)),
        "k_norm": 1.0 + 0.05 * n(ks[6], (DEPTH, HEAD_DIM)),
        "hgrn_lb_fwd": 0.5 * n(ks[7], (DEPTH, HGRN_WIDTH)),
        "hgrn_lb_bwd": 0.5 * n(ks[8], (DEPTH, HGRN_WIDTH)),
        "hgrn_norm": 1.0 + 0.05 * n(ks[9], (DEPTH, HGRN_WIDTH)),
        "conv_w": n(ks[10], (DEPTH, CONV_KERNEL, CONV_WIDTH)) * CONV_KERNEL ** -0.5,
        "conv_b": 0.02 * n(ks[11], (DEPTH, CONV_WIDTH)),
        "conv_ln_g": 1.0 + 0.05 * n(ks[12], (DEPTH, CONV_WIDTH)),
        "conv_ln_b": 0.02 * n(ks[13], (DEPTH, CONV_WIDTH)),
        "w_mlp_in": n(ks[14], (DEPTH, D_MODEL, D_FF)) * D_MODEL ** -0.5,
        "w_mlp_out": n(ks[15], (DEPTH, D_FF, D_MODEL)) * D_FF ** -0.5,
    }

def first_block(x, w_in, w_out, norm_mix, norm_mlp, q_norm, k_norm, hgrn_lb_fwd, hgrn_lb_bwd,
              hgrn_norm, conv_w, conv_b, conv_ln_g, conv_ln_b, w_mlp_in, w_mlp_out):
    B, L, _ = x.shape
    rows = L // GRID_W
    row_idx = jnp.broadcast_to(jnp.arange(rows)[:, None], (rows, GRID_W)).reshape(L)
    col_idx = jnp.broadcast_to(jnp.arange(GRID_W)[None, :], (rows, GRID_W)).reshape(L)
    row_cs, col_cs = _rope_angles(row_idx), _rope_angles(col_idx)
    lb_fwd = _layer_lower_bounds(hgrn_lb_fwd)
    lb_bwd = _layer_lower_bounds(hgrn_lb_bwd)
    splits = _in_split_points()

    for l in range(DEPTH):
        h = rms_norm(x, norm_mix[l])
        z = h @ w_in[l]
        (q_a, k_a, v_a, q_h, i_h, f_fw, f_bw, g_h, a_c, g_c) = jnp.split(z, splits, axis=-1)

        q_a = rms_norm(q_a.reshape(B, L, ATT_HEADS, HEAD_DIM), q_norm[l])
        k_a = rms_norm(k_a.reshape(B, L, ATT_KV_HEADS, HEAD_DIM), k_norm[l])
        q_a = apply_axial_rope(q_a, row_cs, col_cs)
        k_a = apply_axial_rope(k_a, row_cs, col_cs)
        v_a = v_a.reshape(B, L, ATT_KV_HEADS, HEAD_DIM)
        o_att = block_attention(q_a, k_a, v_a)

        o_hg = hgrn2_bidirectional(q_h, i_h, f_fw, f_bw, g_h,
                                   lb_fwd[l], lb_bwd[l], hgrn_norm[l])

        o_cv = conformer_conv(a_c, g_c, conv_w[l], conv_b[l],
                              conv_ln_g[l], conv_ln_b[l])

        mix = jnp.concatenate([o_att, o_hg.astype(x.dtype), o_cv], axis=-1)
        x = x + mix @ w_out[l]

        h = rms_norm(x, norm_mlp[l])
        x = x + jnp.square(jax.nn.relu(h @ w_mlp_in[l])) @ w_mlp_out[l]
    return x


N_A_LAYERS = DEPTH // 2
N_B_LAYERS = DEPTH - N_A_LAYERS
DN_ALPHA = (2.0 * DEPTH) ** 0.25
DN_BETA = (8.0 * DEPTH) ** -0.25
LN_EPS = 1e-5
HEAD_NORM_EPS = 1e-6
MIX_WIDTH = D_MODEL

MEM_LEN = 256
MEM_HEADS = 4
MEM_HEAD_DIM = D_MODEL // 16
MEM_WIDTH = MEM_HEADS * MEM_HEAD_DIM

GLA_HEADS = 4
GLA_DV = (MIX_WIDTH - MEM_WIDTH) // GLA_HEADS
GLA_DK = GLA_DV // 2
GLA_GATE_RANK = 16
GLA_TAU = 16.0
GLA_CHUNK = 64
GLA_QK_WIDTH = GLA_HEADS * GLA_DK
GLA_V_WIDTH = GLA_HEADS * GLA_DV

DIL_PAIRS = ((128, 1), (512, 4), (2048, 16))
DIL_GROUPS = len(DIL_PAIRS)
DIL_SLOTS = 6
DIL_HEAD_DIM = (MIX_WIDTH - MEM_WIDTH) // DIL_SLOTS
DIL_BLOCK = 128
DIL_Q_WIDTH = DIL_GROUPS * DIL_SLOTS * DIL_HEAD_DIM
DIL_KV_WIDTH = DIL_SLOTS * DIL_HEAD_DIM

PEER_N_KEYS = 128
PEER_EXPERTS = PEER_N_KEYS * PEER_N_KEYS
PEER_HEADS = 8
PEER_TOPK = 16
PEER_QDIM = 256
PEER_HALF = PEER_QDIM // 2
PEER_TOKEN_BLOCK = 128

A_Q0, A_Q1 = 0, GLA_QK_WIDTH
A_K0, A_K1 = A_Q1, A_Q1 + GLA_QK_WIDTH
A_V0, A_V1 = A_K1, A_K1 + GLA_V_WIDTH
A_R0, A_R1 = A_V1, A_V1 + GLA_V_WIDTH
A_G0, A_G1 = A_R1, A_R1 + GLA_GATE_RANK
A_M0, A_M1 = A_G1, A_G1 + MEM_WIDTH
A_IN_WIDTH = A_M1
B_Q0, B_Q1 = 0, DIL_Q_WIDTH
B_M0, B_M1 = B_Q1, B_Q1 + MEM_WIDTH
B_IN_WIDTH = B_M1


def _layer_norm(x, g, b):
    xf = x.astype(jnp.float32)
    mu = jnp.mean(xf, axis=-1, keepdims=True)
    var = jnp.mean(jnp.square(xf - mu), axis=-1, keepdims=True)
    y = (xf - mu) * lax.rsqrt(var + LN_EPS)
    return (y * g.astype(jnp.float32) + b.astype(jnp.float32)).astype(x.dtype)

def _gla(q, k, v, log_a):
    B, S, H, K = q.shape
    nc = S // GLA_CHUNK

    def chunks(t):
        return t.astype(jnp.float32).reshape(B, nc, GLA_CHUNK, H, -1).transpose(1, 0, 3, 2, 4)

    q_c = chunks(q) * (K ** -0.5)
    k_c, v_c, g_c = chunks(k), chunks(v), chunks(log_a)
    b = jnp.cumsum(g_c, axis=3)
    b_last = b[:, :, :, -1:, :]
    q_t = q_c * jnp.exp(b)
    k_t = k_c * jnp.exp(-b)
    k_end = k_c * jnp.exp(b_last - b)
    causal = jnp.tril(jnp.ones((GLA_CHUNK, GLA_CHUNK), dtype=bool))
    attn = jnp.where(causal, jnp.einsum('nbhck,nbhsk->nbhcs', q_t, k_t), 0.0)
    o_intra = jnp.einsum('nbhcs,nbhsv->nbhcv', attn, v_c)

    def step(state, inp):
        qt, ke, vc, dec = inp
        o = jnp.einsum('bhck,bhkv->bhcv', qt, state)
        state = dec[..., None] * state + jnp.einsum('bhck,bhcv->bhkv', ke, vc)
        return state, o

    s0 = jnp.zeros((B, H, K, v.shape[-1]), jnp.float32)
    _, o_inter = lax.scan(step, s0, (q_t, k_end, v_c, jnp.exp(b_last[:, :, :, 0, :])))
    return (o_intra + o_inter).transpose(1, 0, 3, 2, 4).reshape(B, S, H, -1)

def _dilated_group(q, k, v, window, dilation):
    B, S, H, E = q.shape
    L = S // dilation
    nb = -(-L // DIL_BLOCK)
    Lp = nb * DIL_BLOCK
    span = window // dilation

    def sub(t):
        return t.reshape(B, L, dilation, H, E).transpose(0, 2, 3, 1, 4)

    qs = jnp.pad(sub(q), ((0, 0), (0, 0), (0, 0), (0, Lp - L), (0, 0)))
    qs = qs.reshape(B, dilation, H, nb, DIL_BLOCK, E)

    def kv_blocks(t):
        tp = jnp.pad(sub(t), ((0, 0), (0, 0), (0, 0), (DIL_BLOCK, Lp - L), (0, 0)))
        prev = tp[:, :, :, :Lp].reshape(B, dilation, H, nb, DIL_BLOCK, E)
        cur = tp[:, :, :, DIL_BLOCK:].reshape(B, dilation, H, nb, DIL_BLOCK, E)
        return jnp.concatenate([prev, cur], axis=4)

    kb, vb = kv_blocks(k), kv_blocks(v)
    s = jnp.einsum('bdhnqe,bdhnke->bdhnqk', qs, kb,
                   preferred_element_type=jnp.float32) * (E ** -0.5)
    qi = jnp.arange(DIL_BLOCK)[:, None]
    kj = jnp.arange(2 * DIL_BLOCK)[None, :]
    rel = DIL_BLOCK + qi - kj
    band = (rel >= 0) & (rel <= span)
    not_front = (jnp.arange(nb)[:, None, None] > 0) | (kj[None] >= DIL_BLOCK)
    mask = band[None] & not_front
    s = jnp.where(mask, s, -jnp.inf)
    lse = jax.nn.logsumexp(s, axis=-1)
    p = jnp.exp(s - lse[..., None])
    o = jnp.einsum('bdhnqk,bdhnke->bdhnqe', p.astype(vb.dtype), vb,
                   preferred_element_type=jnp.float32)
    o = o.reshape(B, dilation, H, Lp, E)[:, :, :, :L].transpose(0, 3, 1, 2, 4).reshape(B, S, H, E)
    lse = lse.reshape(B, dilation, H, Lp)[..., :L].transpose(0, 3, 1, 2).reshape(B, S, H)
    return o, lse

def _dilated_attention(q_all, k, v):
    outs, lses = [], []
    for g, (window, dilation) in enumerate(DIL_PAIRS):
        o, l = _dilated_group(q_all[:, :, g], k, v, window, dilation)
        outs.append(o)
        lses.append(l)
    wts = jax.nn.softmax(jnp.stack(lses, axis=0), axis=0)
    return jnp.einsum('gbsh,gbshe->bshe', wts, jnp.stack(outs, axis=0))

def _mem_attn(qm, km, vm):
    s = jnp.einsum('bshe,bmhe->bhsm', qm, km,
                   preferred_element_type=jnp.float32) * (qm.shape[-1] ** -0.5)
    p = jax.nn.softmax(s, axis=-1)
    return jnp.einsum('bhsm,bmhe->bshe', p.astype(vm.dtype), vm)

def _peer(x, w_q, sub_keys, u, v):
    B, S, D = x.shape
    T = B * S
    xt = x.reshape(T, D)
    q = (xt @ w_q).reshape(T, PEER_HEADS, 2, PEER_HALF)
    s = jnp.einsum('thpe,pne->thpn', q, sub_keys, preferred_element_type=jnp.float32)
    top_s, top_i = lax.top_k(s, PEER_TOPK)
    cand = (top_s[:, :, 0, :, None] + top_s[:, :, 1, None, :]).reshape(
        T, PEER_HEADS, PEER_TOPK * PEER_TOPK)
    best_s, best_j = lax.top_k(cand, PEER_TOPK)
    idx_a = jnp.take_along_axis(top_i[:, :, 0], best_j // PEER_TOPK, axis=-1)
    idx_b = jnp.take_along_axis(top_i[:, :, 1], best_j % PEER_TOPK, axis=-1)
    expert = idx_a * PEER_N_KEYS + idx_b
    gate = jax.nn.softmax(best_s, axis=-1)
    nblk = T // PEER_TOKEN_BLOCK

    def block(args):
        xb, eb, gb = args
        h = jnp.einsum('td,thkd->thk', xb, u[eb], preferred_element_type=jnp.float32)
        a = (jax.nn.gelu(h, approximate=False) * gb).astype(xb.dtype)
        return jnp.einsum('thk,thkd->td', a, v[eb])

    out = lax.map(block, (xt.reshape(nblk, PEER_TOKEN_BLOCK, D),
                          expert.reshape(nblk, PEER_TOKEN_BLOCK, PEER_HEADS, PEER_TOPK),
                          gate.reshape(nblk, PEER_TOKEN_BLOCK, PEER_HEADS, PEER_TOPK)))
    return out.reshape(B, S, D).astype(x.dtype)

def second_inputs(seed: int = 0) -> dict:
    key = jax.random.key(seed)
    ks = jax.random.split(key, 20)
    n = jax.random.normal
    D = D_MODEL
    return {
        'x': n(ks[0], (BATCH, SEQ, D), jnp.float32),
        'mem': n(ks[1], (BATCH, MEM_LEN, D), jnp.float32),
        'a_w_in': n(ks[2], (N_A_LAYERS, D, A_IN_WIDTH), jnp.float32) * D ** -0.5,
        'a_w_gate2': n(ks[3], (N_A_LAYERS, GLA_GATE_RANK, GLA_QK_WIDTH), jnp.float32) * GLA_GATE_RANK ** -0.5,
        'a_b_gate': 0.02 * n(ks[4], (N_A_LAYERS, GLA_QK_WIDTH), jnp.float32),
        'a_norm_g': 1.0 + 0.02 * n(ks[5], (N_A_LAYERS, GLA_V_WIDTH), jnp.float32),
        'b_w_in': n(ks[6], (N_B_LAYERS, D, B_IN_WIDTH), jnp.float32) * D ** -0.5,
        'shared_w_kv': n(ks[7], (D, 2 * DIL_KV_WIDTH), jnp.float32) * D ** -0.5,
        'w_mem_kv': n(ks[8], (DEPTH, D, 2 * MEM_WIDTH), jnp.float32) * D ** -0.5,
        'w_out': n(ks[9], (DEPTH, MIX_WIDTH, D), jnp.float32) * (MIX_WIDTH ** -0.5 * DN_BETA),
        'ln_mix_g': 1.0 + 0.02 * n(ks[10], (DEPTH, D), jnp.float32),
        'ln_mix_b': 0.02 * n(ks[11], (DEPTH, D), jnp.float32),
        'ln_ffn_g': 1.0 + 0.02 * n(ks[12], (DEPTH, D), jnp.float32),
        'ln_ffn_b': 0.02 * n(ks[13], (DEPTH, D), jnp.float32),
        'peer_w_q': n(ks[14], (DEPTH, D, PEER_HEADS * PEER_QDIM), jnp.float32) * D ** -0.5,
        'peer_sub_keys': n(ks[15], (DEPTH, 2, PEER_N_KEYS, PEER_HALF), jnp.float32) * PEER_HALF ** -0.5,
        'peer_u': n(ks[16], (DEPTH, PEER_EXPERTS, D), jnp.float32) * D ** -0.5,
        'peer_v': n(ks[17], (DEPTH, PEER_EXPERTS, D), jnp.float32) * (DN_BETA * PEER_HEADS ** -0.5),
    }

def second_block(x, mem, a_w_in, a_w_gate2, a_b_gate, a_norm_g, b_w_in, shared_w_kv,
              w_mem_kv, w_out, ln_mix_g, ln_mix_b, ln_ffn_g, ln_ffn_b,
              peer_w_q, peer_sub_keys, peer_u, peer_v):
    B, S, _ = x.shape
    shared_k = None
    shared_v = None
    for l in range(DEPTH):
        mkv = (mem @ w_mem_kv[l]).reshape(B, MEM_LEN, 2, MEM_HEADS, MEM_HEAD_DIM)
        if l < N_A_LAYERS:
            h = x @ a_w_in[l]
            q = h[..., A_Q0:A_Q1].reshape(B, S, GLA_HEADS, GLA_DK)
            k = h[..., A_K0:A_K1].reshape(B, S, GLA_HEADS, GLA_DK)
            v = h[..., A_V0:A_V1].reshape(B, S, GLA_HEADS, GLA_DV)
            r = h[..., A_R0:A_R1]
            g_pre = (h[..., A_G0:A_G1] @ a_w_gate2[l] + a_b_gate[l]).astype(jnp.float32)
            log_a = (jax.nn.log_sigmoid(g_pre) / GLA_TAU).reshape(B, S, GLA_HEADS, GLA_DK)
            o = _gla(q, k, v, log_a)
            o = o * lax.rsqrt(jnp.mean(jnp.square(o), axis=-1, keepdims=True) + HEAD_NORM_EPS)
            o = o.reshape(B, S, GLA_V_WIDTH) * a_norm_g[l].astype(jnp.float32)
            mix = (jax.nn.silu(r.astype(jnp.float32)) * o).astype(x.dtype)
            qm = h[..., A_M0:A_M1]
        else:
            h = x @ b_w_in[l - N_A_LAYERS]
            qd = h[..., B_Q0:B_Q1].reshape(B, S, DIL_GROUPS, DIL_SLOTS, DIL_HEAD_DIM)
            mix = _dilated_attention(qd, shared_k, shared_v).reshape(B, S, DIL_KV_WIDTH).astype(x.dtype)
            qm = h[..., B_M0:B_M1]
        mo = _mem_attn(qm.reshape(B, S, MEM_HEADS, MEM_HEAD_DIM),
                       mkv[:, :, 0], mkv[:, :, 1]).reshape(B, S, MEM_WIDTH).astype(x.dtype)
        y = jnp.concatenate([mix, mo], axis=-1) @ w_out[l]
        x = _layer_norm(DN_ALPHA * x + y, ln_mix_g[l], ln_mix_b[l])
        f = _peer(x, peer_w_q[l], peer_sub_keys[l], peer_u[l], peer_v[l])
        x = _layer_norm(DN_ALPHA * x + f, ln_ffn_g[l], ln_ffn_b[l])
        if l == N_A_LAYERS - 1:
            kv = (x @ shared_w_kv).reshape(B, S, 2, DIL_SLOTS, DIL_HEAD_DIM)
            shared_k = kv[:, :, 0]
            shared_v = kv[:, :, 1]
    return x


def setup_inputs(seed=0):
    out = dict(first_inputs(seed))
    for name, value in second_inputs(seed + 1).items():
        if name != "x":
            out[name + "_2"] = value
    return out


def reference(
    x, w_in, w_out, norm_mix, norm_mlp, q_norm, k_norm, hgrn_lb_fwd, hgrn_lb_bwd, hgrn_norm,
    conv_w, conv_b, conv_ln_g, conv_ln_b, w_mlp_in, w_mlp_out, mem_2, a_w_in_2, a_w_gate2_2,
    a_b_gate_2, a_norm_g_2, b_w_in_2, shared_w_kv_2, w_mem_kv_2, w_out_2, ln_mix_g_2,
    ln_mix_b_2, ln_ffn_g_2, ln_ffn_b_2, peer_w_q_2, peer_sub_keys_2, peer_u_2, peer_v_2,
):
    x = first_block(
        x, w_in, w_out, norm_mix, norm_mlp, q_norm, k_norm, hgrn_lb_fwd, hgrn_lb_bwd, hgrn_norm,
        conv_w, conv_b, conv_ln_g, conv_ln_b, w_mlp_in, w_mlp_out,
    )
    return second_block(
        x, mem_2, a_w_in_2, a_w_gate2_2, a_b_gate_2, a_norm_g_2, b_w_in_2, shared_w_kv_2,
        w_mem_kv_2, w_out_2, ln_mix_g_2, ln_mix_b_2, ln_ffn_g_2, ln_ffn_b_2, peer_w_q_2,
        peer_sub_keys_2, peer_u_2, peer_v_2,
    )


_drawn_inputs = setup_inputs


def setup_inputs(seed=0):
    import zlib

    import numpy as np

    out = dict(_drawn_inputs(seed))
    spreads = {}
    factors = {'q_norm': 5.952,
     'k_norm': 6.797,
     'conv_ln_b': 4.442,
     'a_b_gate_2': 8.0,
     'a_norm_g_2': 21.918}
    for name, (base, spread) in spreads.items():
        noise = np.random.default_rng([zlib.crc32(name.encode()), seed]).standard_normal(out[name].shape)
        drawn = base * np.exp(spread * noise) if base else spread * noise
        out[name] = jnp.asarray(drawn.astype(out[name].dtype))
    for name, factor in factors.items():
        out[name] = (out[name] * factor).astype(out[name].dtype)
    return out
```

```python
from contextlib import ExitStack

import numpy as np
import concourse.bass as bass
from concourse import mybir

F32 = mybir.dt.float32
BF16 = mybir.dt.bfloat16
F32R = mybir.dt.float32r
I32 = mybir.dt.int32
U32 = mybir.dt.uint32
ALU = mybir.AluOpType
ACT = mybir.ActivationFunctionType
AX = mybir.AxisListType

P = 128
TOK = 256
TT = TOK // P
D = 1024
KT = D // P
DEPTH = 2
HP = 2048
SLOTS = 4
HEAD = 64
EPS = 1e-6
LN_EPS = 1e-5
CHUNK = 16
NCH = TOK // CHUNK
CONV_K = 31
CONV_PAD = 15
D_FF = 4096
GLA_H, GLA_K, GLA_V, GLA_C = 4, 96, 192, 64
SLOT_H = 6
GROUPS = 3
DN_ALPHA = (2.0 * DEPTH) ** 0.25
NEG = -1.0e30
KEYS = 128
PH = 8
TOPK = 16
PAIRS = KEYS // 2
CHUNKS = 4
BC = KEYS // CHUNKS
STEPS = PAIRS // CHUNKS
TPS = TOK // STEPS

N_MEM = 2 * DEPTH
N_IN, N_OUT, N_UP, N_DOWN = 10, 4, 16, 16
N_FIRST = N_IN + N_OUT + N_UP + N_DOWN
N_MIX2, N_WQ, N_DENSE, N_SHARED = [11, 10], 8, 2 * PAIRS, 6
N_SECOND = [m + N_OUT + N_WQ + N_DENSE for m in N_MIX2]
HP_FIRST = [N_MEM + l * N_FIRST for l in range(DEPTH)]
HP_SHARED = N_MEM + DEPTH * N_FIRST + N_SECOND[0]
HP_SECOND = [N_MEM + DEPTH * N_FIRST, HP_SHARED + N_SHARED]
HP_DENSE = [HP_SECOND[l] + N_MIX2[l] + N_OUT + N_WQ for l in range(DEPTH)]
N_HP = HP_SECOND[1] + N_SECOND[1]

CONST = {}
_c = 0
for _n, _w in (("ident", 128), ("iota", 128), ("zero", 128), ("blk", 128), ("ones", 128), ("rot", 128),
               ("cos", 256), ("sin", 256), ("chunkmask", 8), ("notfirst", 16), ("first", 16),
               ("notlast", 16), ("last", 16), ("gscan", 64), ("causal", 64)):
    CONST[_n] = (_c, _c + _w)
    _c += _w
N_CONST = _c
PAR = {}
_c = 0
for _n, _w in (("norm_mix", 8), ("norm_mlp", 8), ("qg", 1), ("kg", 1), ("ng", 2), ("cw", 62), ("cb", 2),
               ("lng", 2), ("lnb", 2)):
    PAR[_n] = (_c, _c + _w)
    _c += _w
N_PAR = _c


class Steps:

    def __init__(self, eng, own):
        self.eng, self.own, self.count = eng, own, {}

    def mark(self, ins, s=None, n=1):
        s = self.own if s is None else s
        self.count[s.name] = self.count.get(s.name, 0) + n
        ins.then_inc(s, n)
        return self.count[s.name]

    def step(self, ins, s=None):
        s = self.own if s is None else s
        self.eng.wait_ge(s, self.mark(ins, s))


def build(nc, stream, x_in, mem_in, const_in, par_in, lb_in, par2_in, wg2_in, mask_in, rows_in, sk_in, out):
    ctx = ExitStack()
    with ctx:
        sems = {}

        def sem(name):
            if name not in sems:
                sems[name] = ctx.enter_context(nc.semaphore(name))
            return sems[name]

        cursor = [(nc.sbuf_base + 63) // 64 * 64]
        end = nc.sbuf_usable_end // 64 * 64

        def at(name, shape, dt=F32, off=None):
            size = int(np.prod(shape[1:])) * (2 if dt == BF16 else 4)
            o = cursor[0] if off is None else off
            if off is None:
                cursor[0] += (size + 63) // 64 * 64
            assert o + size <= end, (name, o + size, end)
            return nc.alloc_sbuf_tensor_at(name, list(shape), dt, offset=o)

        RAW = at("raw", [P, SLOTS, HP])
        HI = [at(f"hi{i}", [P, HP], F32R) for i in range(SLOTS)]
        LO = [at(f"lo{i}", [P, HP], F32R) for i in range(SLOTS)]
        XH = at("xh", [P, KT, TOK], F32R)
        XL = at("xl", [P, KT, TOK], F32R)
        CST = at("cst", [P, N_CONST])
        SMALL = at("small", [P, 64])
        X = at("x", [P, TT, D])
        mix0 = cursor[0]
        LBS = at("lbs", [P, 16], off=end - 64)
        PR = at("pr", [P, DEPTH, N_PAR], off=end - 64 - 704)
        LB = at("lb", [P, DEPTH, 2, 2, 2], off=end - 64 - 704 - 64)
        top = end - 64 - 704 - 64

        E = at("e", [P, 2, 2 * TOK])
        F = at("f", [P, 2, 2 * TOK])
        KG = at("kg", [P, 2, 2 * TOK])
        MIXF = at("mixf", [P, KT, TOK], off=cursor[0] - 8192)
        Q = at("q", [P, 2 * TOK])
        VR = at("vr", [P, TT, 256])
        VT = at("vt", [P, 2 * TOK])
        GT = at("gt", [P, 2 * TOK])
        AC = at("ac", [P, 2 * TOK])
        EG = at("eg", [P, 2 * TOK])
        UP = at("up", [P, 2, TOK + 2 * CONV_PAD])
        W = at("w", [P, 2 * TOK])
        XX = at("xx", [P, 2, 2 * TOK])
        TB = at("tb", [P, 2 * TOK])
        ACC = at("acc", [P, 2 * TOK])
        SCN = at("scn", [P, 2 * TOK])
        QB = at("qb", [P, 2, 2 * TOK])
        ST = at("st", [P, 2, NCH, HEAD])
        DG = at("dg", [P, 4, P])
        QK = at("qk", [P, 5, TOK])
        VA = at("va", [P, TT, P])
        r1 = cursor[0]
        VX = at("vx", [P, TT, 4, 8, HEAD])
        assert cursor[0] <= top, (cursor[0], top)
        XS = at("xs", [P, TT, D], off=r1)
        QK2 = at("qk2", [P, 5, TOK], off=r1)
        QK3 = at("qk3", [P, 5, TOK], off=r1 + 5 * TOK * 4)
        PM = at("pm", [P, 2, 2, TOK], off=r1)
        PT = at("pt", [P, 2, 2, TOK], off=r1 + 4096)
        KVM = at("kvm", [P, 1024], off=r1)
        HH = at("hh", [P, 32, TOK], F32R, off=mix0)
        HL = at("hl", [P, 32, TOK], F32R, off=mix0 + 32768)
        RB = at("rb", [P, 2, 2 * TOK], off=mix0 + 65536)
        SQ = at("sq", [P, 2 * TOK], off=mix0 + 65536 + 4096)
        XS2 = at("xs2", [P, TT, D], off=mix0 + 65536 + 6144)
        assert mix0 + 65536 + 6144 + 8192 <= top

        def cst(name):
            a, b = CONST[name]
            return CST[:, a:b]

        def par(l, name, i=0, n=1):
            c = PAR[name][0] + i
            return PR[:, l, c:c + n]

        def flat(t):
            return t.rearrange("p a b -> p (a b)")

        def v16(t):
            return t.rearrange("p (a c) -> p a c", c=CHUNK)

        cursor[0] = mix0
        ROWS = at("rows", [P, 2, D])
        MIX2 = at("mix2", [P, KT, TOK])
        KVL = at("kvl", [P, 1024])
        QM = at("qm", [P, 2, TOK])
        PM2 = at("pm2", [P, 2, 2, TOK])
        PT2 = at("pt2", [P, 2, 2, TOK])
        both = cursor[0]
        GO2 = at("go2", [P, TT, 768], off=both)
        GQ = at("gq", [P, 4, TOK])
        GK = at("gk", [P, 4, TOK])
        GV = at("gv", [P, TT, 768])
        GR = at("gr", [P, TT, 768])
        LG = at("lg", [P, 4, TOK])
        KTD = at("ktd", [P, 4, TOK], off=cursor[0] - 4096)
        GO = at("go", [P, TT, 768], off=cursor[0] - 4096)
        RG = at("rg", [P, TT, 768], off=cursor[0] + 2048)
        B = at("b", [P, 4, TOK])
        KE = at("ke", [P, 4, TOK])
        SM = at("sm", [P, 4, TOK], off=cursor[0] - 4096)
        QTD = at("qtd", [P, 4, TOK])
        KER = at("ker", [P, TT, 4 * GLA_K])
        ATT = at("att", [P, 8, GLA_C])
        STA = at("sta", [P, 4, GLA_V])
        WG2 = at("wg2", [P, 4 * GLA_K])
        P2 = at("p2", [P, 16])
        BL = at("bl", [P, 16])
        assert cursor[0] <= end
        EXA = at("exa", [P, 4, TOK], off=both - 8192)
        EXB = at("exb", [P, 4, TOK], off=both - 4096)
        cursor[0] = both
        QD = at("qd", [P, GROUPS * SLOT_H, TOK])
        KD = at("kd", [P, SLOT_H, TOK])
        VD = at("vd", [P, TT, 768])
        DM = at("dm", [P, TT, GROUPS * TOK])
        S3 = at("s3", [P, 2, GROUPS * TOK])
        PD = at("pd", [P, 2, 2, TOK])
        PTD = at("ptd", [P, 2, TOK])
        assert cursor[0] <= end
        cursor[0] = mix0
        EQ = at("eq", [P, PH, TOPK, TOPK], off=mix0)
        QP = at("qp", [P, 2 * PH, TOK])
        CD2 = at("cd2", [P, PH, TOPK * TOPK], off=cursor[0])
        SC = at("sc", [P, TT, 2 * PH, KEYS])
        S2 = at("s2", [P, 2 * PH, KEYS], off=cursor[0])
        CD = at("cd", [P, TT, PH, TOPK * TOPK])
        TS = at("ts", [P, TT, 2 * PH, TOPK])
        TI = at("ti", [P, TT, 2 * PH, TOPK], U32)
        TF = at("tf", [P, TT, 2 * PH, TOPK])
        BS = at("bs", [P, TT * PH, TOPK])
        GX = at("gx", [P, TT * PH, TOPK])
        BJ = at("bj", [P, TT, PH, TOPK], U32)
        BK = at("bk", [P, 2, TT * PH * TOPK], U32)
        JF = at("jf", [P, 2, TT, PH, TOPK])
        GSUM = at("gsum", [P, TT * PH])
        SEL = at("sel", [P, 3, TT, PH * TOPK])
        SK = at("sk", [P, 2, KEYS])
        assert cursor[0] <= end
        x0 = mix0 - 8192
        PF = at("pf", [P, 3, TOK], off=x0)
        EQB = at("eqb", [P, TPS, BC], BF16, off=x0 + 3072)
        OB = at("ob", [P, 3, TPS, BC], BF16, off=x0 + 4096)
        cursor[0] = mix0
        G = [at(f"g{i}", [P, BC, TOK]) for i in range(2)]
        GE = at("ge", [P, 2, 512])
        AH = [at(f"ah{i}", [P, 512], F32R) for i in range(2)]
        AL = [at(f"al{i}", [P, 512], F32R) for i in range(2)]
        OA = at("oa", [P, TPS, KEYS], BF16)
        GS = at("gs", [P, 3, TOK], BF16)
        assert cursor[0] <= end
        x_scr = nc.dram_tensor("x_scratch", [P, TT, D], F32).ap()
        PS = [ctx.enter_context(nc.psum_tensor(f"lin{i}", [P, 512], F32)) for i in range(4)]
        M = [ctx.enter_context(nc.psum_tensor(f"m{i}", [P, 512], F32)) for i in range(4)]
        mem_scr = nc.dram_tensor("mem_kv_scratch", [DEPTH, P, 1024], F32).ap()

        raw_loaded = [sem(f"raw_loaded{i}") for i in range(SLOTS)]
        bank_free = [sem(f"bank_free{i}") for i in range(4)]
        hi_ready, lo_ready, hp_used = sem("hi_ready"), sem("lo_ready"), sem("hp_used")

        read_out = [True] * N_HP
        for l in range(DEPTH):
            for i in range(N_DOWN - 4):
                read_out[HP_FIRST[l] + N_IN + N_OUT + N_UP + i] = False
            for i in range(N_DENSE):
                read_out[HP_DENSE[l] + i] = False

        def reads_before(i):
            return sum(read_out[j] for j in range(i % 4, i, 4))

        def evicted(eng, i, it=0):
            eng.wait_ge(bank_free[i % 4], reads_before(i) + 1 + it)

        block = ctx.enter_context(nc.Block())

        @block.sync
        def _(sp):
            sp.dma_start(X[:], mem_in.rearrange("(t p) d -> p t d", p=P)).then_inc(sem("mem_loaded"), 16)
            for i in range(SLOTS):
                sp.dma_start(RAW[:, i, :], stream[i]).then_inc(raw_loaded[i], 16)
            rounds = N_HP // SLOTS
            with sp.Fori(1, rounds) as g:
                for i in range(SLOTS):
                    sp.wait_ge(lo_ready, g * SLOTS + (i + 1 - SLOTS))
                    sp.dma_start(RAW[:, i, :], stream[g * SLOTS + i]).then_inc(raw_loaded[i], 16)
            for i in range(SLOTS * rounds, N_HP):
                sp.wait_ge(lo_ready, i + 1 - SLOTS)
                sp.dma_start(RAW[:, i % SLOTS, :], stream[i]).then_inc(raw_loaded[i % SLOTS], 16)
            sp.wait_ge(sem("x_final"), 1)
            sp.dma_start(out.rearrange("(t p) d -> p t d", p=P), X[:]).then_inc(sem("out_stored"), 16)
            sp.wait_ge(sem("out_stored"), 16)

        def attention_act(act, a, g0, heads, scale, dst, part, PM=PM, PT=PT):
            def tail(n):
                g = g0 + n
                act.wait_ge(sem("pt_done"), g + 1)
                a.mark(act.activation(flat(PT[:, g % 2, :, :]), M[2][:], ACT.Copy), sem("pt_ready"))
                act.wait_ge(sem("pv_done"), g + 1)
                o = part(n)
                a.mark(act.activation(dst(n), M[3][o:o + 64, 0:256], ACT.Copy), sem("o_ready"))

            for n in range(heads):
                g = g0 + n
                act.wait_ge(sem("nb_ready"), g + 1)
                if n >= 2:
                    act.wait_ge(sem("pt_done"), g - 1)
                c = 16 + 8 * (g % 2)
                for qt in range(2):
                    ins = act.activation(PM[:, g % 2, qt, :], M[g % 2][:, 256 * qt:256 * qt + 256], ACT.Exp,
                                         scale=scale, bias=SMALL[:, c + 2 + qt:c + 3 + qt], accum_out=SMALL[:, c + 4 + qt:c + 5 + qt])
                a.mark(ins, sem("exp_ready"))
                if n >= 1:
                    tail(n - 1)
            tail(heads - 1)
            act.wait_ge(sem("o_ready"), g0 + heads)

        @block.scalar
        def _(act):
            a = Steps(act, sem("act_step"))
            nxt = [0]

            def hi(i, it=0):
                act.wait_ge(raw_loaded[i % SLOTS], 16 * (i // SLOTS + 1) + it * 16)
                if i >= SLOTS:
                    act.wait_ge(hp_used, i + 1 - SLOTS + it * SLOTS)
                act.activation(HI[i % SLOTS][:], RAW[:, i % SLOTS, :], ACT.Copy).then_inc(hi_ready, 1)

            def hi_to(n):
                while nxt[0] < min(n, N_HP):
                    hi(nxt[0])
                    nxt[0] += 1

            def xh_evict(inst, gain=None):
                for kp in range(4):
                    act.wait_ge(sem("t_done"), 4 * inst + kp + 1)
                    if gain is None:
                        ins = act.activation(flat(XH[:, 2 * kp:2 * kp + 2, :]), M[kp][:], ACT.Copy)
                    else:
                        act.activation(XH[:, 2 * kp, :], M[kp][:, 0:256], ACT.Copy, scale=gain(2 * kp))
                        ins = act.activation(XH[:, 2 * kp + 1, :], M[kp][:, 256:512], ACT.Copy, scale=gain(2 * kp + 1))
                    a.mark(ins, sem("xh_ready"))

            def rstd(out_, in_, n, eps, signal=None):
                a.step(act.activation(out_, in_, ACT.Ln, scale=1.0 / n, bias=eps))
                a.step(act.activation(out_, out_, ACT.Exp, scale=-0.5), signal)

            def rms_rows(junk):
                for tt in range(TT):
                    a.step(act.activation(junk[:, tt, :], X[:, tt, :], ACT.Square, accum_out=SMALL[:, tt:tt + 1]))
                rstd(SMALL[:, 2:4], SMALL[:, 0:2], D, EPS, sem("row_rstd"))

            act.dma_start(CST[:], const_in).then_inc(sem("cst_loaded"), 16)
            act.dma_start(LBS[:], lb_in).then_inc(sem("cst_loaded"), 16)
            act.dma_start(PR[:], par_in.rearrange("l p n -> p l n")).then_inc(sem("cst_loaded"), 16)
            act.preload_act_table_set("natural_log_exp_and_others")
            act.wait_ge(sem("lb_shifted"), 1)
            a.step(act.activation(LBS[:, 0:8], LBS[:, 0:8], ACT.Exp), sem("lb_exp"))
            hi_to(2)
            xh_evict(0)
            for l in range(DEPTH):
                hi_to(2 * l + 4)
                if l > 0:
                    act.wait_ge(sem("kvm_stored"), 16 * l)
                for i in (2 * l, 2 * l + 1):
                    act.wait_ge(hp_used, i + 1)
                    act.activation(KVM[:, 512 * (i % 2):512 * (i % 2) + 512], PS[i % 4][:], ACT.Copy).then_inc(bank_free[i % 4], 1)
                evicted(act, 2 * l)
                evicted(act, 2 * l + 1)
                act.dma_start(mem_scr[l], KVM[:]).then_inc(sem("kvm_stored"), 16)
            act.wait_ge(sem("t_done"), 4)
            act.dma_start(X[:], x_in.rearrange("(t p) d -> p t d", p=P)).then_inc(sem("x_loaded"), 16)
            act.wait_ge(sem("x_loaded"), 16)
            act.wait_ge(sem("kvm_stored"), 16 * DEPTH)

            for l in range(DEPTH):
                h0 = HP_FIRST[l]
                if l > 0:
                    for u in range(4):
                        evicted(act, h0 - 4 + u)
                rms_rows(XS)
                act.wait_ge(hp_used, h0)
                xh_evict(1 + 2 * l, lambda k: par(l, "norm_mix", k))
                dst = [VR, Q, (E, 0), (E, 1), GT, AC, EG, None, (QK, 0), (QK, 2)]
                for u in range(N_IN):
                    hi_to(h0 + u + 4)
                    i = h0 + u
                    act.wait_ge(hp_used, i + 1)
                    b = PS[i % 4]
                    if u == 7:
                        act.activation(QK[:, 4, :], b[:, 0:256], ACT.Copy)
                        ins = act.activation(flat(VA[:]), b[:, 256:512], ACT.Copy)
                    elif u in (2, 3):
                        ins = act.activation(E[:, u - 2, :], b[:], ACT.Exp, scale=-1.0)
                    elif u == 6:
                        ins = act.activation(EG[:], b[:], ACT.Exp, scale=-1.0)
                    elif u >= 8:
                        ins = act.activation(flat(QK[:, 2 * u - 16:2 * u - 14, :]), b[:], ACT.Copy)
                    else:
                        ins = act.activation(flat(VR[:]) if u == 0 else dst[u][:], b[:], ACT.Copy)
                    ins.then_inc(bank_free[i % 4], 1)
                hi_to(h0 + N_IN + N_OUT)
                act.wait_ge(sem("vt_done"), l + 1)
                a.step(act.activation(VT[:], M[0][:], ACT.Copy), sem("vt_ready"))
                for d in range(2):
                    act.wait_ge(sem("kt_done"), 2 * l + d + 1)
                    a.step(act.activation(XX[:, 1, :], M[2][:], ACT.Copy), sem("kr_ready"))
                act.wait_ge(sem("hss_done"), l + 1)
                rstd(TB[:], M[1][:], HEAD, EPS)
                a.step(act.activation(SCN[:], GT[:], ACT.Exp, scale=-1.0), sem("hrs_ready"))
                act.wait_ge(sem("cvar_done"), l + 1)
                rstd(TB[:, 0:256], M[3][:, 256:512], 256, EPS, sem("crs_ready"))
                act.wait_ge(sem("cy_ready"), l + 1)
                a.step(act.activation(EG[:], AC[:], ACT.Exp, scale=-1.0), sem("ceg_ready"))
                for j in range(3):
                    n = 512 if j < 2 else 256
                    act.wait_ge(sem("qss_done"), 3 * l + j + 1)
                    rstd(flat(QK3[:])[:, 512 * j:512 * j + n], M[j][:, 0:n], HEAD, EPS, sem("qrs_ready"))
                attention_act(act, a, 8 * l, 8, HEAD ** -0.5, lambda n: MIXF[64 * (n // 4):64 * (n // 4) + 64, n % 4, :],
                              lambda n: 64 * (n // 4))
                act.wait_ge(sem("mix_ready"), l + 1)
                a.step(act.activation(flat(XH[:]), flat(MIXF[:]), ACT.Copy), sem("mixh_ready"))
                h1 = h0 + N_IN + N_OUT
                for u in range(4):
                    evicted(act, h1 - 4 + u)
                rms_rows(XS2)
                hi_to(h1 + 3)
                xh_evict(2 + 2 * l, lambda k: par(l, "norm_mlp", k))
                with act.Fori(0, N_UP // 4) as it:
                    for u in range(4):
                        hi(h1 + u + 3, it)
                        act.wait_ge(hp_used, h1 + u + 1 + it * 4)
                        act.wait_ge(sem("hid_ready"), 16 * l + u + 1 + it * 4)
                        act.activation(RB[:, u % 2, :], PS[(h1 + u) % 4][:], ACT.Relu).then_inc(bank_free[(h1 + u) % 4], 1)
                        evicted(act, h1 + u, it)
                        act.activation(flat(HH[:, bass.ds(it * 8 + 2 * u, 2), :]), RB[:, u % 2, :],
                                       ACT.Square).then_inc(sem("sq_ready"), 1)
                nxt[0] = h1 + N_UP + 3
                hi_to(h1 + N_UP + N_DOWN + 2)
            for l in range(DEPTH):
                s0 = HP_SECOND[l]
                act.wait_ge(sem("x_ready"), 2 * l + 1)
                act.wait_ge(hp_used, HP_SHARED if l > 0 else s0)
                for dst_, src_ in [(ROWS[:], rows_in[2 * l].partition_broadcast(P)), (KVL[:], mem_scr[l])] + \
                        ([(WG2[96:112, :], wg2_in), (P2[:], par2_in)] if l == 0 else [(DM[:], mask_in)]):
                    act.dma_start(dst_, src_).then_inc(sem(f"mix_loaded{l}"), 16)
                hi_to(HP_SHARED + 2 if l > 0 else s0 + 3)
                xh_evict(5 + 2 * l)
                if l > 0:
                    for u in range(N_SHARED):
                        hi_to(HP_SHARED + u + 4)
                        i = HP_SHARED + u
                        act.wait_ge(hp_used, i + 1)
                        b = PS[i % 4]
                        if u < 3:
                            ins = act.activation(flat(KD[:, 2 * u:2 * u + 2, :]), b[:], ACT.Copy)
                        else:
                            ins = act.activation(VD[:, :, 256 * (u - 3):256 * (u - 2)], b[:].rearrange("p (t n) -> p t n", t=2), ACT.Copy)
                        ins.then_inc(bank_free[i % 4], 1)
                for u in range(N_MIX2[l]):
                    hi_to(s0 + u + 4)
                    i = s0 + u
                    act.wait_ge(hp_used, i + 1)
                    b = PS[i % 4]
                    if l == 0 and u >= 5:
                        t, j = (GV, u - 5) if u < 8 else (GR, u - 8)
                        ins = act.activation(t[:, :, 256 * j:256 * j + 256], b[:].rearrange("p (t n) -> p t n", t=2), ACT.Copy)
                    else:
                        t = (QM if u == (4 if l == 0 else 9) else GQ[:, 2 * u:2 * u + 2, :] if u < 2 else GK[:, 2 * u - 4:2 * u - 2, :]) if l == 0 \
                            else QM if u == 9 else QD[:, 2 * u:2 * u + 2, :]
                        ins = act.activation(flat(t[:] if t is QM else t), b[:], ACT.Copy)
                    ins.then_inc(bank_free[i % 4], 1)
                hi_to(s0 + N_MIX2[l] + 3)
                k96 = slice(0, GLA_K)
                if l == 0:
                    act.wait_ge(sem("gpre_read"), 1)
                    act.wait_ge(sem("mix_loaded0"), 64)
                    for h in range(4):
                        ins = act.activation(EXA[k96, h, :], M[h // 2][k96, 256 * (h % 2):256 * (h % 2) + 256], ACT.Abs, bias=P2[k96, h:h + 1])
                    a.step(ins)
                    a.step(act.activation(flat(EXB[k96]), flat(EXA[k96]), ACT.Exp, scale=-1.0))
                    a.step(act.activation(flat(EXA[k96]), flat(EXB[k96]), ACT.Ln, bias=1.0), sem("lsig_ready"))
                    act.wait_ge(sem("cum_ready"), 1)
                    a.mark(act.activation(flat(EXA[k96]), flat(B[k96]), ACT.Exp, scale=1.0 / 16))
                    a.mark(act.activation(flat(EXB[k96]), flat(B[k96]), ACT.Exp, scale=-1.0 / 16))
                    a.mark(act.activation(flat(KE[k96]), flat(KE[k96]), ACT.Exp, scale=1.0 / 16))
                    a.step(act.activation(BL[k96], B[k96].rearrange("p h (n c) -> p (h n) c", c=GLA_C)[:, :, GLA_C - 1], ACT.Exp, scale=1.0 / 16), sem("gexp_ready"))
                    act.wait_ge(sem("ket_done"), 1)
                    for tt in range(TT):
                        ins = act.activation(KER[:, tt, :], M[2 + tt][:, 0:384], ACT.Copy)
                    a.step(ins, sem("ker_ready"))
                    a.step(act.activation(flat(RG[:]), flat(GR[:]), ACT.Exp, scale=-1.0), sem("rexp_ready"))
                    for ch in range(4):
                        rows = slice(64 * (ch % 2), 64 * (ch % 2) + 64)
                        act.wait_ge(sem("oc_done"), ch + 1)
                        for j in range(2):
                            ins = act.activation(GO[rows, ch // 2, 384 * j:384 * j + 384], M[2 + j][rows, 0:384], ACT.Copy)
                        a.step(ins, sem("go_ready"))
                    act.wait_ge(sem("gss_ready"), 1)
                    rstd(SMALL[:, 48:56], SMALL[:, 48:56], GLA_V, EPS, sem("grs_ready"))
                    act.wait_ge(sem("got_done"), 1)
                    for kt in range(6):
                        ins = act.activation(MIX2[:, kt, :], M[kt // 2][:, 256 * (kt % 2):256 * (kt % 2) + 256], ACT.Copy, scale=P2[:, 4 + kt:5 + kt])
                    a.step(ins, sem("glamix_ready"))
                else:
                    def slot_out(sl):
                        act.wait_ge(sem("dpt_done"), sl + 1)
                        a.mark(act.activation(flat(PTD[:]), M[2][:], ACT.Copy), sem("dpt_ready"))
                        act.wait_ge(sem("dpv_done"), sl + 1)
                        a.mark(act.activation(MIX2[:, sl, :], M[3][:, 0:256], ACT.Copy), sem("do_ready"))

                    for n in range(2 * SLOT_H):
                        act.wait_ge(sem("dnb_ready"), n + 1)
                        c = 48 + 2 * (n % 2)
                        a.mark(act.activation(S3[:, n % 2, :], S3[:, n % 2, :], ACT.Exp, scale=KEYS ** -0.5, bias=SMALL[:, c:c + 1],
                                              accum_out=SMALL[:, c + 1:c + 2]), sem("dexp_ready"))
                        if n >= 3 and n % 2 == 1:
                            slot_out(n // 2 - 1)
                    slot_out(SLOT_H - 1)
                    act.wait_ge(sem("do_ready"), SLOT_H)
                attention_act(act, a, 16 + 4 * l, 4, HEAD ** -0.5, lambda n: MIX2[64 * (n % 2):64 * (n % 2) + 64, 6 + n // 2, :],
                              lambda n: 64 * (n % 2), PM2, PT2)
                a.step(act.activation(flat(XH[:]), flat(MIX2[:]), ACT.Copy), sem("mix2h_ready"))
                w0 = s0 + N_MIX2[l] + N_OUT
                hi_to(w0)
                act.wait_ge(sem("ln_var"), 2 * l + 1)
                rstd(SMALL[:, 60:62], SMALL[:, 56:60].rearrange("p (t k) -> p t k", k=2)[:, :, 1], 1, LN_EPS, sem("ln_rstd"))
                act.wait_ge(sem("x_ready"), 2 * l + 2)
                act.dma_start(x_scr, X[:]).then_inc(sem("x_spilled"), 16)
                act.dma_start(SK[:], sk_in[l]).then_inc(sem("keys_loaded"), 16)
                hi_to(w0 + 3)
                xh_evict(6 + 2 * l)
                for u in range(N_WQ):
                    hi_to(w0 + u + 4)
                    i = w0 + u
                    act.wait_ge(hp_used, i + 1)
                    act.activation(flat(QP[:, 2 * u:2 * u + 2, :]), PS[i % 4][:], ACT.Copy).then_inc(bank_free[i % 4], 1)
                d0 = w0 + N_WQ
                hi_to(d0 + 3)
                for j in range(8):
                    act.wait_ge(sem("keysc_done"), 8 * l + j + 1)
                    a.mark(act.activation(SC[:, j // 4, 4 * (j % 4):4 * (j % 4) + 4, :].rearrange("p a b -> p (a b)"), M[j % 4][:], ACT.Copy), sem("keysc_ready"))
                act.wait_ge(sem("gx_shifted"), l + 1)
                a.step(act.activation(flat(GX[:]), flat(GX[:]), ACT.Exp), sem("gx_ready"))
                act.wait_ge(sem("selt_done"), l + 1)
                act.wait_ge(sem("x_spilled"), 16 * (l + 1))
                a.mark(act.activation(flat(PF[:, 0:2, :]), M[0][:], ACT.Copy))
                a.step(act.activation(PF[:, 2, :], M[1][:, 0:256], ACT.Copy), sem("pf_ready"))

                t0, s00 = (CHUNKS * STEPS) * l, PAIRS * l

                def table_copy(q, k, it=0):
                    n = t0 + STEPS * q + k
                    act.wait_ge(sem("table_done"), n + 1 + it * 2)
                    act.activation(G[q % 2][:, :, bass.ds(it * (2 * TPS) + TPS * k, TPS)].rearrange("p b t -> p t b"),
                                   PS[2 + k % 2][:].rearrange("p (t b) -> p t b", b=BC), ACT.Copy).then_inc(sem("table_ready"), 1)

                def gelu(s, it=0):
                    act.wait_ge(hp_used, d0 + max(2 * s, 1) + it * 4)
                    if s >= 1:
                        act.wait_ge(sem("al_ready"), s00 + s - 1 + it * 2)
                    act.activation(GE[:, s % 2, :], PS[s % 2][:], ACT.Gelu).then_inc(sem("ge_ready"), 1)

                def act_high(s, it=0):
                    act.wait_ge(sem("a_ready"), s00 + s + 1 + it * 2)
                    if s >= 1:
                        act.wait_ge(hp_used, d0 + 2 * s - 1 + it * 4)
                    act.activation(AH[s % 2][:], GE[:, s % 2, :], ACT.Copy).then_inc(sem("ah_ready"), 1)

                def dense_step(q, j, it=0):
                    s = STEPS * q + j
                    for n in (3, 4):
                        if not isinstance(it, int) or d0 + 2 * s + n < d0 + N_DENSE:
                            hi(d0 + 2 * s + n, it)
                    if s + 1 < PAIRS:
                        gelu(s + 1, it)
                    if q + 1 < CHUNKS:
                        table_copy(q + 1, j, it)
                    if s + 1 < PAIRS:
                        act_high(s + 1, it)

                for k in range(STEPS):
                    table_copy(0, k)
                gelu(0)
                act_high(0)
                for q in range(CHUNKS):
                    with act.Fori(0, STEPS // 2 - 1) as it:
                        for j in range(2):
                            dense_step(q, j, it)
                    for j in (STEPS - 2, STEPS - 1):
                        dense_step(q, j)
                nxt[0] = d0 + N_DENSE
                act.wait_ge(sem("f_done"), l + 1)
                act.wait_ge(sem("picks_used"), l + 1)
                act.dma_start(X[:], x_scr).then_inc(sem("x_back"), 16)
                act.dma_start(ROWS[:], rows_in[2 * l + 1].partition_broadcast(P)).then_inc(sem("x_back"), 16)
                act.wait_ge(sem("ln_var"), 2 * l + 2)
                rstd(SMALL[:, 60:62], SMALL[:, 56:60].rearrange("p (t k) -> p t k", k=2)[:, :, 1], 1, LN_EPS, sem("ln_rstd"))

        def attention_dve(dve, v, g0, heads, scale, PM=PM):
            def head_max(n):
                g = g0 + n
                c = 16 + 8 * (g % 2)
                dve.wait_ge(sem("sc_done"), g + 1)
                v.step(dve.tensor_reduce(SMALL[:, c:c + 2], M[g % 2][:].rearrange("p (q k) -> p q k", q=2), AX.X, ALU.max))
                v.step(dve.tensor_scalar(SMALL[:, c + 2:c + 4], SMALL[:, c:c + 2], -scale, None, ALU.mult), sem("nb_ready"))

            def head_scale(n):
                g = g0 + n
                c = 16 + 8 * (g % 2)
                dve.wait_ge(sem("exp_ready"), g + 1)
                v.step(dve.reciprocal(SMALL[:, c + 6:c + 8], SMALL[:, c + 4:c + 6]))
                for qt in range(2):
                    ins = dve.tensor_scalar(PM[:, g % 2, qt, :], PM[:, g % 2, qt, :], SMALL[:, c + 6 + qt:c + 7 + qt], None, ALU.mult)
                v.step(ins, sem("sm_ready"))

            head_max(0)
            for n in range(heads):
                if n + 1 < heads:
                    head_max(n + 1)
                head_scale(n)

        @block.vector
        def _(dve):
            v = Steps(dve, sem("dve_step"))
            nxt = [0]

            def lo(i, it=0):
                dve.wait_ge(hi_ready, i + 1 + it * 4)
                dve.tensor_tensor(LO[i % SLOTS][:], RAW[:, i % SLOTS, :], HI[i % SLOTS][:].bitcast(F32), ALU.subtract).then_inc(lo_ready, 1)

            def lo_to(n):
                while nxt[0] < min(n, N_HP):
                    lo(nxt[0])
                    nxt[0] += 1

            def xl_evict(inst, gain=None):
                for kp in range(4):
                    dve.wait_ge(sem("xh_ready"), 4 * inst + kp + 1)
                    hi_ = XH[:, 2 * kp:2 * kp + 2, :].bitcast(F32)
                    if gain is None:
                        ins = dve.tensor_tensor(flat(XL[:, 2 * kp:2 * kp + 2, :]), M[kp][:], flat(hi_), ALU.subtract)
                    else:
                        for j in range(2):
                            ins = dve.scalar_tensor_tensor(out=XL[:, 2 * kp + j, :], in0=M[kp][:, 256 * j:256 * j + 256],
                                                           scalar=gain(2 * kp + j), in1=hi_[:, j, :], op0=ALU.mult, op1=ALU.subtract)
                    v.mark(ins, sem("xl_ready"))

            def norm_rows(dst, inst):
                dve.wait_ge(sem("row_rstd"), inst)
                for tt in range(TT):
                    ins = dve.tensor_scalar(dst[:, tt, :], X[:, tt, :], SMALL[:, 2 + tt:3 + tt], None, ALU.mult)
                v.mark(ins, sem("rows_ready"))

            def residual(h):
                for u in range(4):
                    i = h + u
                    dve.wait_ge(hp_used, i + 1)
                    xv = X[:, :, 256 * u:256 * u + 256]
                    dve.tensor_tensor(xv, xv, PS[i % 4][:].rearrange("p (t n) -> p t n", t=2), ALU.add).then_inc(bank_free[i % 4], 1)
                for u in range(4):
                    evicted(dve, h + u)

            dve.wait_ge(sem("cst_loaded"), 48)
            v.step(dve.tensor_tensor(LBS[:, 8:12], LBS[:, 0:4], LBS[:, 4:8], ALU.max))
            v.step(dve.tensor_tensor(LBS[:, 0:4], LBS[:, 0:4], LBS[:, 8:12], ALU.subtract))
            v.step(dve.tensor_tensor(LBS[:, 4:8], LBS[:, 4:8], LBS[:, 8:12], ALU.subtract), sem("lb_shifted"))
            dve.wait_ge(sem("lb_exp"), 1)
            v.step(dve.tensor_tensor(LBS[:, 8:12], LBS[:, 0:4], LBS[:, 4:8], ALU.add))
            v.step(dve.reciprocal(LBS[:, 8:12], LBS[:, 8:12]))
            v.step(dve.tensor_tensor(LBS[:, 0:4], LBS[:, 0:4], LBS[:, 8:12], ALU.mult))
            v.step(dve.tensor_tensor(LBS[:, 4:8], LBS[:, 4:8], LBS[:, 8:12], ALU.mult))
            v.step(dve.tensor_tensor(LBS[:, 4:8], LBS[:, 4:8], LBS[:, 0:4], ALU.add))
            lb4 = [LB[:, l, :, :, 0].rearrange("p a b -> p a b") for l in range(DEPTH)]
            p4 = [LBS[:, 4 * l:4 * l + 4].rearrange("p (a b) -> p a b", b=2) for l in range(DEPTH)]
            for l in range(DEPTH):
                v.step(dve.tensor_tensor(lb4[l], p4[l], p4[0], ALU.subtract))
                v.step(dve.tensor_scalar(LB[:, l, :, :, 1], lb4[l], -1.0, 1.0, ALU.mult, ALU.add))
            dve.memset(UP[:], 0.0).then_inc(sem("hid_ready"), 2)

            lo_to(2)
            xl_evict(0)
            lo_to(4)
            for l in range(DEPTH):
                h0 = HP_FIRST[l]
                norm_rows(XS, 2 * l + 1)
                xl_evict(1 + 2 * l, lambda k: par(l, "norm_mix", k))
                lo_to(h0 + 8)
                evicted(dve, h0 + 2)
                evicted(dve, h0 + 3)
                v.step(dve.tensor_scalar(flat(E[:]), flat(E[:]), 1.0, None, ALU.add))
                v.step(dve.reciprocal(flat(E[:]), flat(E[:])))
                for d in range(2):
                    for ht in range(2):
                        c = slice(256 * ht, 256 * ht + 256)
                        lb, om = LB[:, l, d, ht, 0:1], LB[:, l, d, ht, 1:2]
                        v.mark(dve.tensor_scalar(F[:, d, c], E[:, d, c], om, lb, ALU.mult, ALU.add))
                        v.step(dve.tensor_scalar(KG[:, d, c], E[:, d, c], -1.0, 1.0, ALU.mult, ALU.add))
                        v.step(dve.tensor_scalar(KG[:, d, c], KG[:, d, c], om, None, ALU.mult))
                lo_to(h0 + N_IN)
                evicted(dve, h0 + 1)
                dve.wait_ge(sem("vt_ready"), l + 1)
                v.step(dve.memset(ACC[:], 0.0))

                def lag_value(n):
                    d, g = divmod(n, CHUNK)
                    dve.wait_ge(sem("lag_done"), 2 * CHUNK * l + n + 1)
                    here, there = (slice(g, 16), slice(0, 16 - g)) if d == 0 else (slice(0, 16 - g), slice(g, 16))
                    v.step(dve.tensor_tensor(v16(TB[:])[:, :, here], v16(M[n % 2][:])[:, :, here], v16(VT[:])[:, :, there], ALU.mult))
                    v.step(dve.tensor_tensor(v16(ACC[:])[:, :, here], v16(ACC[:])[:, :, here], v16(TB[:])[:, :, here], ALU.add))

                for n in range(2 * CHUNK):
                    d, g = divmod(n, CHUNK)
                    f, k, w = v16(F[:, d, :]), v16(KG[:, d, :]), v16(W[:])
                    here, there = (slice(g, 16), slice(0, 16 - g)) if d == 0 else (slice(0, 16 - g), slice(g, 16))
                    if g == 0:
                        v.step(dve.tensor_copy(W[:], Q[:]))
                    else:
                        fs = slice(1, 17 - g) if d == 0 else slice(g - 1, 15)
                        v.step(dve.tensor_tensor(w[:, :, here], w[:, :, here], f[:, :, fs], ALU.mult))
                    v.step(dve.tensor_tensor(v16(XX[:, n % 2, :])[:, :, here], w[:, :, here], k[:, :, there], ALU.mult), sem("lagx_ready"))
                    if n >= 1:
                        lag_value(n - 1)
                    if g == CHUNK - 1:
                        e = f[:, :, 0:1] if d == 0 else f[:, :, 15:16]
                        v.step(dve.tensor_tensor(v16(QB[:, d, :]), w, e.to_broadcast([P, 32, 16]), ALU.mult))
                lag_value(2 * CHUNK - 1)
                for d in range(2):
                    f, k, ke = v16(F[:, d, :]), v16(KG[:, d, :]), v16(XX[:, 0, :])
                    keep, edge = ("notlast", "last") if d == 0 else ("notfirst", "first")
                    bc = [P, 32, 16]
                    v.mark(dve.tensor_tensor(v16(E[:, 0, :]), f, cst(keep).unsqueeze(1).to_broadcast(bc), ALU.mult))
                    v.step(dve.tensor_tensor(v16(E[:, 1, :]), f, cst(edge).unsqueeze(1).to_broadcast(bc), ALU.mult))
                    if d == 0:
                        pp = E[:].ap[0]
                        back = [bass.AP(E, 2 * TOK * j + 2 * TOK - 1, [list(pp), [-1, 2 * TOK]]) for j in range(2)]
                        o = bass.AP(SCN, 2 * TOK - 1, [list(SCN[:].ap[0]), [-1, 2 * TOK]])
                    else:
                        back, o = [E[:, 0, :], E[:, 1, :]], SCN[:]
                    v.step(dve.tensor_tensor_scan(o, back[0], back[1], 0.0, ALU.mult, ALU.add))
                    s = v16(SCN[:])
                    if d == 1:
                        dve.wait_ge(sem("u_done"), 8 * l + 4)
                    if d == 0:
                        v.mark(dve.tensor_tensor(ke[:, :, 0:15], k[:, :, 0:15], s[:, :, 1:16], ALU.mult))
                        v.step(dve.tensor_copy(ke[:, :, 15:16], k[:, :, 15:16]), sem("ke_ready"))
                    else:
                        v.mark(dve.tensor_tensor(ke[:, :, 1:16], k[:, :, 1:16], s[:, :, 0:15], ALU.mult))
                        v.step(dve.tensor_copy(ke[:, :, 0:1], k[:, :, 0:1]), sem("ke_ready"))
                        dve.wait_ge(sem("inter_done"), 2 * l + 1)
                    first = 0 if d == 0 else NCH - 1
                    v.step(dve.memset(ST[:, :, first, :], 0.0))
                    dec = SCN[:].rearrange("p (h n c) -> p h n c", h=2, c=CHUNK)[:, :, :, 0 if d == 0 else 15]
                    n = 0
                    for tt in (0, 1) if d == 0 else (1, 0):
                        for ht in range(2):
                            dve.wait_ge(sem("u_done"), 8 * l + 4 * d + n + 1)
                            bank = M[3 - n % 2]
                            for c in range(8) if d == 0 else range(7, -1, -1):
                                ch = 8 * tt + c
                                to = ch + 1 if d == 0 else ch - 1
                                if 0 <= to < NCH:
                                    v.step(dve.scalar_tensor_tensor(out=ST[:, ht, to, :], in0=ST[:, ht, ch, :], scalar=dec[:, ht, ch:ch + 1],
                                                                    in1=bank[:, 64 * c:64 * c + 64], op0=ALU.mult, op1=ALU.add))
                            v.step(dve.memset(SMALL[:, 40:41], 0.0), sem("u_read"))
                            n += 1
                    v.step(dve.memset(SMALL[:, 41:42], 0.0), sem("state_ready"))
                dve.wait_ge(sem("inter_done"), 2 * l + 2)
                v.step(dve.tensor_tensor(ACC[:], ACC[:], M[0][:], ALU.add))
                v.step(dve.tensor_tensor(W[:], ACC[:], ACC[:], ALU.mult), sem("hsq_ready"))
                dve.wait_ge(sem("hrs_ready"), l + 1)
                v.step(dve.tensor_scalar(SCN[:], SCN[:], 1.0, None, ALU.add))
                v.step(dve.reciprocal(SCN[:], SCN[:]))
                v.step(dve.tensor_tensor(SCN[:], SCN[:], GT[:], ALU.mult))
                for ht in range(2):
                    c = slice(256 * ht, 256 * ht + 256)
                    v.step(dve.scalar_tensor_tensor(out=ACC[:, c], in0=ACC[:, c], scalar=par(l, "ng", ht), in1=TB[:, c], op0=ALU.mult, op1=ALU.mult))
                v.step(dve.tensor_tensor(flat(MIXF[:, 4:6, :]), ACC[:], SCN[:], ALU.mult))
                evicted(dve, h0 + 5)
                evicted(dve, h0 + 6)
                v.step(dve.tensor_scalar(EG[:], EG[:], 1.0, None, ALU.add))
                v.step(dve.reciprocal(EG[:], EG[:]))
                if l > 0:
                    v.step(dve.memset(UP[:], 0.0))
                v.step(dve.tensor_tensor(UP[:, :, CONV_PAD:CONV_PAD + TOK], AC[:].rearrange("p (a t) -> p a t", a=2),
                                         EG[:].rearrange("p (a t) -> p a t", a=2), ALU.mult), sem("up_ready"))
                dve.wait_ge(sem("diag_used"), 2 * CONV_K * (l + 1))
                for ct in range(2):
                    c = slice(256 * ct, 256 * ct + 256)
                    v.step(dve.tensor_scalar(AC[:, c], M[2][:, c], par(l, "cb", ct), None, ALU.add), sem("cy0_ready"))
                dve.wait_ge(sem("csum_done"), l + 1)
                for ct in range(2):
                    c = slice(256 * ct, 256 * ct + 256)
                    v.step(dve.scalar_tensor_tensor(out=W[:, c], in0=M[3][:, 0:256], scalar=-1.0 / 256, in1=AC[:, c], op0=ALU.mult, op1=ALU.add))
                    v.step(dve.tensor_tensor(SCN[:, c], W[:, c], W[:, c], ALU.mult), sem("csq_ready"))
                dve.wait_ge(sem("crs_ready"), l + 1)
                for ct in range(2):
                    c = slice(256 * ct, 256 * ct + 256)
                    v.step(dve.scalar_tensor_tensor(out=W[:, c], in0=W[:, c], scalar=par(l, "lng", ct), in1=TB[:, 0:256], op0=ALU.mult, op1=ALU.mult))
                    ins = dve.tensor_scalar(AC[:, c], W[:, c], par(l, "lnb", ct), None, ALU.add)
                    if ct == 0:
                        v.step(ins)
                    else:
                        v.step(ins, sem("cy_ready"))
                dve.wait_ge(sem("ceg_ready"), l + 1)
                v.step(dve.tensor_scalar(EG[:], EG[:], 1.0, None, ALU.add))
                v.step(dve.reciprocal(EG[:], EG[:]))
                v.step(dve.tensor_tensor(flat(MIXF[:, 6:8, :]), AC[:], EG[:], ALU.mult))
                for i in (7, 8, 9):
                    evicted(dve, h0 + i)
                v.step(dve.tensor_tensor(flat(QK2[:]), flat(QK[:]), flat(QK[:]), ALU.mult), sem("qsq_ready"))
                dve.wait_ge(sem("qrs_ready"), 3 * l + 3)
                v.mark(dve.scalar_tensor_tensor(out=flat(QK2[:, 0:4, :]), in0=flat(QK[:, 0:4, :]), scalar=par(l, "qg"), in1=flat(QK3[:, 0:4, :]),
                                                op0=ALU.mult, op1=ALU.mult))
                v.step(dve.scalar_tensor_tensor(out=QK2[:, 4, :], in0=QK[:, 4, :], scalar=par(l, "kg"), in1=QK3[:, 4, :],
                                                op0=ALU.mult, op1=ALU.mult), sem("qn_ready"))
                v.step(dve.tensor_tensor(QK3[:], QK2[:], cst("cos").unsqueeze(1).to_broadcast([P, 5, TOK]), ALU.mult))
                for j in range(3):
                    n = 2 if j < 2 else 1
                    dve.wait_ge(sem("rot_done"), 3 * l + j + 1)
                    v.step(dve.tensor_tensor(QK[:, 2 * j:2 * j + n, :], M[j][:, 0:256 * n].rearrange("p (a t) -> p a t", t=TOK),
                                             cst("sin").unsqueeze(1).to_broadcast([P, n, TOK]), ALU.mult))
                v.step(dve.tensor_tensor(flat(QK[:]), flat(QK[:]), flat(QK3[:]), ALU.add), sem("qk_ready"))
                v.mark(dve.memset(SMALL[:, 42:43], 0.0), sem("mix_ready"))
                lo_to(h0 + N_IN + N_OUT)
                attention_dve(dve, v, 8 * l, 8, HEAD ** -0.5)
                dve.wait_ge(sem("mixh_ready"), l + 1)
                v.step(dve.tensor_tensor(flat(XL[:]), flat(MIXF[:]), flat(XH[:].bitcast(F32)), ALU.subtract), sem("mixl_ready"))
                residual(h0 + N_IN)
                h1 = h0 + N_IN + N_OUT
                norm_rows(XS2, 2 * l + 2)
                lo_to(h1 + 3)
                xl_evict(2 + 2 * l, lambda k: par(l, "norm_mlp", k))
                with dve.Fori(0, N_UP // 4) as it:
                    for u in range(4):
                        lo(h1 + u + 3, it)
                        dve.wait_ge(bank_free[(h1 + u) % 4], reads_before(h1 + u) + 1 + it)
                        dve.tensor_tensor(SQ[:], RB[:, u % 2, :], RB[:, u % 2, :], ALU.mult).then_inc(sem("hsq2"), 1)
                        dve.wait_ge(sem("hsq2"), 16 * l + u + 1 + it * 4)
                        dve.wait_ge(sem("sq_ready"), 16 * l + u + 1 + it * 4)
                        at_ = bass.ds(it * 8 + 2 * u, 2)
                        dve.tensor_tensor(flat(HL[:, at_, :]), SQ[:], flat(HH[:, at_, :].bitcast(F32)), ALU.subtract)\
                           .then_inc(sem("hid_ready"), 1)
                        dve.wait_ge(sem("hid_ready"), 16 * l + u + 3 + it * 4)
                nxt[0] = h1 + N_UP + 3
                lo_to(h1 + N_UP + N_DOWN + 2)
                residual(h1 + N_UP + N_DOWN - 4)
            def layer_norm(n):
                for tt in range(TT):
                    st = SMALL[:, 4:16].rearrange("p (a b) -> p a b", b=6)
                    for j in range(2):
                        ins = dve.bn_stats(st[:, j, :], X[:, tt, 512 * j:512 * j + 512])
                    v.step(ins)
                    ins = dve.bn_aggr(SMALL[:, 56 + 2 * tt:58 + 2 * tt], st)
                    v.step(ins) if tt == 0 else v.step(ins, sem("ln_var"))
                dve.wait_ge(sem("ln_rstd"), n)
                for tt in range(TT):
                    ins = dve.tensor_scalar(X[:, tt, :], X[:, tt, :], SMALL[:, 56 + 2 * tt:57 + 2 * tt], SMALL[:, 60 + tt:61 + tt],
                                            ALU.subtract, ALU.mult)
                v.step(ins)
                v.step(dve.tensor_tensor(X[:], X[:], ROWS[:, 0, :].unsqueeze(1).to_broadcast([P, TT, D]), ALU.mult))
                v.step(dve.tensor_tensor(X[:], X[:], ROWS[:, 1, :].unsqueeze(1).to_broadcast([P, TT, D]), ALU.add), sem("x_ready"))

            def best16(values, spare, top_, idx, groups):
                for g in range(groups):
                    ins = dve.max(top_(g)[:, 0:8], values(g))
                v.step(ins)
                for g in range(groups):
                    dve.max_index(idx(g)[:, 0:8], top_(g)[:, 0:8], values(g))
                    ins = dve.match_replace(spare(g), top_(g)[:, 0:8], values(g), -3.0e38)
                v.step(ins)
                for g in range(groups):
                    ins = dve.max(top_(g)[:, 8:16], spare(g))
                v.step(ins)
                for g in range(groups):
                    ins = dve.max_index(idx(g)[:, 8:16], top_(g)[:, 8:16], spare(g))
                v.step(ins)

            k96 = slice(0, GLA_K)
            v.mark(dve.memset(SMALL[:, 43:44], 0.0), sem("x_ready"))
            for l in range(DEPTH):
                s0 = HP_SECOND[l]
                lo_to(HP_SHARED + 2 if l > 0 else s0 + 3)
                xl_evict(5 + 2 * l)
                if l == 0:
                    lo_to(s0 + N_MIX2[l])
                    dve.wait_ge(sem("mix_loaded0"), 64)
                    dve.wait_ge(sem("gpre_done"), 1)
                    for h in range(4):
                        ins = dve.tensor_scalar(LG[k96, h, :], M[h // 2][k96, 256 * (h % 2):256 * (h % 2) + 256], P2[k96, h:h + 1], 0.0, ALU.add, ALU.min)
                    v.step(ins, sem("gpre_read"))
                    v.step(dve.tensor_copy(flat(SM[:]).rearrange("p (n c) -> p n c", c=GLA_C), cst("gscan").unsqueeze(1).to_broadcast([P, 16, GLA_C])))
                    dve.wait_ge(sem("lsig_ready"), 1)
                    v.step(dve.tensor_tensor(flat(LG[k96]), flat(LG[k96]), flat(EXA[k96]), ALU.subtract))
                    v.step(dve.tensor_tensor_scan(flat(B[k96]), flat(SM[k96]), flat(LG[k96]), 0.0, ALU.mult, ALU.add))
                    bc = B[k96].rearrange("p h (n c) -> p (h n) c", c=GLA_C)
                    v.step(dve.tensor_tensor(KE[k96].rearrange("p h (n c) -> p (h n) c", c=GLA_C),
                                             bc[:, :, GLA_C - 1].unsqueeze(2).to_broadcast([GLA_K, 16, GLA_C]), bc, ALU.subtract), sem("cum_ready"))
                    dve.wait_ge(sem("gexp_ready"), 1)
                    v.mark(dve.tensor_tensor(flat(KE[k96]), flat(KE[k96]), flat(GK[k96]), ALU.mult))
                    v.mark(dve.tensor_tensor(flat(KTD[k96]), flat(EXB[k96]), flat(GK[k96]), ALU.mult))
                    v.step(dve.scalar_tensor_tensor(out=flat(QTD[k96]), in0=flat(GQ[k96]), scalar=GLA_K ** -0.5, in1=flat(EXA[k96]),
                                                    op0=ALU.mult, op1=ALU.mult), sem("gqk_ready"))
                    dve.wait_ge(sem("gatt_done"), 1)
                    cm = cst("causal").unsqueeze(1).to_broadcast([P, 8, GLA_C])
                    v.step(dve.scalar_tensor_tensor(out=ATT[:], in0=cm, scalar=3.0e38, in1=M[0][:].rearrange("p (a c) -> p a c", c=GLA_C),
                                                    op0=ALU.mult, op1=ALU.min))
                    v.step(dve.scalar_tensor_tensor(out=ATT[:], in0=cm, scalar=-3.0e38, in1=ATT[:], op0=ALU.mult, op1=ALU.max), sem("gattm_ready"))
                    for ch in range(3):
                        dve.wait_ge(sem("uc_done"), ch + 1)
                        for h in range(4):
                            u_ = M[h // 2][k96, GLA_V * (h % 2):GLA_V * (h % 2) + GLA_V]
                            if ch == 0:
                                ins = dve.tensor_copy(STA[k96, h, :], u_)
                            else:
                                ins = dve.scalar_tensor_tensor(out=STA[k96, h, :], in0=STA[k96, h, :], scalar=BL[k96, 4 * h + ch:4 * h + ch + 1],
                                                               in1=u_, op0=ALU.mult, op1=ALU.add)
                        v.step(ins, sem("sta_ready"))
                    dve.wait_ge(sem("rexp_ready"), 1)
                    v.step(dve.tensor_scalar(flat(RG[:]), flat(RG[:]), 1.0, None, ALU.add))
                    v.step(dve.reciprocal(flat(RG[:]), flat(RG[:])))
                    v.step(dve.tensor_tensor(flat(RG[:]), flat(RG[:]), flat(GR[:]), ALU.mult))
                    dve.wait_ge(sem("go_ready"), 4)
                    v.step(dve.tensor_tensor(flat(GO2[:]), flat(GO[:]), flat(GO[:]), ALU.mult))
                    v.step(dve.tensor_reduce(SMALL[:, 48:56], GO2[:].rearrange("p t (h c) -> p (t h) c", h=4), AX.X, ALU.add), sem("gss_ready"))
                    dve.wait_ge(sem("grs_ready"), 1)
                    v.step(dve.tensor_tensor(flat(GO[:]), flat(GO[:]), flat(RG[:]), ALU.mult))
                    go = GO[:].rearrange("p t (h c) -> p (t h) c", h=4)
                    v.step(dve.tensor_tensor(go, go, SMALL[:, 48:56].unsqueeze(2).to_broadcast([P, 8, GLA_V]), ALU.mult), sem("gon_ready"))
                else:
                    lo_to(s0 + N_MIX2[l])
                    dve.wait_ge(sem("mix_loaded1"), 48)

                    def slot_max(n):
                        dve.wait_ge(sem("dsc_done"), n + 1)
                        b2 = [M[0], M[1]] if n % 2 == 0 else [PS[0], PS[1]]
                        c = 48 + 2 * (n % 2)
                        for g in range(2):
                            w = slice(0, 512) if g == 0 else slice(512, 768)
                            ins = dve.tensor_tensor(S3[:, n % 2, w], b2[g][:, 0:w.stop - w.start], DM[:, n % 2, w], ALU.add)
                        v.step(ins, sem("dsc_read"))
                        v.step(dve.tensor_reduce(SMALL[:, 52:53], S3[:, n % 2, :], AX.X, ALU.max))
                        v.step(dve.tensor_scalar(SMALL[:, c:c + 1], SMALL[:, 52:53], -KEYS ** -0.5, None, ALU.mult), sem("dnb_ready"))

                    def slot_sum(n):
                        dve.wait_ge(sem("dexp_ready"), n + 1)
                        if n >= 4 and n % 2 == 0:
                            dve.wait_ge(sem("dpt_done"), n // 2 - 1)
                        c = 49 + 2 * (n % 2)
                        o = PD[:, (n // 2) % 2, n % 2, :]
                        v.mark(dve.reciprocal(SMALL[:, 53:54], SMALL[:, c:c + 1]))
                        v.step(dve.tensor_tensor(S3[:, n % 2, 0:256], S3[:, n % 2, 0:256], S3[:, n % 2, 256:512], ALU.add))
                        v.step(dve.tensor_tensor(S3[:, n % 2, 0:256], S3[:, n % 2, 0:256], S3[:, n % 2, 512:768], ALU.add))
                        v.step(dve.tensor_scalar(o, S3[:, n % 2, 0:256], SMALL[:, 53:54], None, ALU.mult), sem("dsm_ready"))

                    slot_max(0)
                    for n in range(2 * SLOT_H):
                        if n + 1 < 2 * SLOT_H:
                            slot_max(n + 1)
                        slot_sum(n)
                lo_to(s0 + N_MIX2[l] + 3)
                attention_dve(dve, v, 16 + 4 * l, 4, HEAD ** -0.5, PM2)
                dve.wait_ge(sem("mix2h_ready"), l + 1)
                v.step(dve.tensor_tensor(flat(XL[:]), flat(MIX2[:]), flat(XH[:].bitcast(F32)), ALU.subtract), sem("mix2l_ready"))
                w0 = s0 + N_MIX2[l] + N_OUT
                lo_to(w0)
                for u in range(4):
                    i = s0 + N_MIX2[l] + u
                    dve.wait_ge(hp_used, i + 1)
                    xv = X[:, :, 256 * u:256 * u + 256]
                    dve.scalar_tensor_tensor(out=xv, in0=xv, scalar=DN_ALPHA, in1=PS[i % 4][:].rearrange("p (t n) -> p t n", t=2),
                                             op0=ALU.mult, op1=ALU.add).then_inc(bank_free[i % 4], 1)
                for u in range(4):
                    evicted(dve, s0 + N_MIX2[l] + u)
                layer_norm(2 * l + 1)
                lo_to(w0 + 3)
                xl_evict(6 + 2 * l)
                d0 = w0 + N_WQ
                lo_to(d0 + 3)
                for tt in range(TT):
                    dve.wait_ge(sem("keysc_ready"), 8 * l + 4 * tt + 4)
                    best16(lambda g: SC[:, tt, g, :], lambda g: S2[:, g, :], lambda g: TS[:, tt, g, :], lambda g: TI[:, tt, g, :], 2 * PH)
                v.mark(dve.tensor_copy(TF[:].rearrange("p a b c -> p (a b c)"), TI[:].rearrange("p a b c -> p (a b c)")))
                bc4 = [P, PH, TOPK, TOPK]
                for tt in range(TT):
                    two = TS[:, tt].rearrange("p (h s) k -> p h s k", s=2)
                    ins = dve.tensor_tensor(CD[:, tt].rearrange("p h (i j) -> p h i j", j=TOPK), two[:, :, 0, :].unsqueeze(3).to_broadcast(bc4),
                                            two[:, :, 1, :].unsqueeze(2).to_broadcast(bc4), ALU.add)
                v.step(ins)
                for tt in range(TT):
                    best16(lambda g: CD[:, tt, g, :], lambda g: CD2[:, g, :], lambda g: BS[:, PH * tt + g, :], lambda g: BJ[:, tt, g, :], PH)
                v.step(dve.tensor_tensor(GX[:], BS[:], BS[:, :, 0:1].to_broadcast([P, TT * PH, TOPK]), ALU.subtract), sem("gx_shifted"))
                bj = BJ[:].rearrange("p a b c -> p (a b c)")
                v.mark(dve.tensor_scalar(BK[:, 0, :], bj, 4, None, ALU.logical_shift_right))
                v.step(dve.tensor_scalar(BK[:, 1, :], bj, TOPK - 1, None, ALU.bitwise_and))
                v.step(dve.tensor_copy(JF[:].rearrange("p s a b c -> p (s a b c)"), flat(BK[:])))
                for side in range(2):
                    for tt in range(TT):
                        v.step(dve.tensor_tensor(EQ[:], cst("iota")[:, 0:TOPK].unsqueeze(1).unsqueeze(1).to_broadcast(bc4),
                                                 JF[:, side, tt].unsqueeze(3).to_broadcast(bc4), ALU.is_equal))
                        v.step(dve.tensor_tensor(EQ[:], EQ[:], TF[:, tt].rearrange("p (h s) k -> p h s k", s=2)[:, :, side, :].unsqueeze(2).to_broadcast(bc4), ALU.mult))
                        v.step(dve.tensor_reduce(SEL[:, side, tt, :].rearrange("p (h k) -> p h k", k=TOPK), EQ[:], AX.X, ALU.add))
                dve.wait_ge(sem("gx_ready"), l + 1)
                v.step(dve.tensor_reduce(GSUM[:], GX[:], AX.X, ALU.add))
                v.step(dve.reciprocal(GSUM[:], GSUM[:]))
                v.step(dve.tensor_tensor(SEL[:, 2].rearrange("p t (h k) -> p (t h) k", k=TOPK), GX[:],
                                         GSUM[:].unsqueeze(2).to_broadcast([P, TT * PH, TOPK]), ALU.mult), sem("sel_ready"))
                dve.wait_ge(sem("pf_ready"), l + 1)
                for c in range(3):
                    v.step(dve.tensor_copy(GS[:, c, :], PF[:, 2, :]))
                    if c < 2:
                        v.step(dve.tensor_tensor(PF[:, 2, :], PF[:, 2, :], GS[:, c, :], ALU.subtract))

                t0, s00 = (CHUNKS * STEPS) * l, PAIRS * l

                def one_hots(q, k, it=0):
                    n = t0 + STEPS * q + k
                    if n > 0:
                        dve.wait_ge(sem("table_done"), n + it * 2)
                    t = bass.ds(it * (2 * TPS) + TPS * k, TPS)
                    dve.tensor_tensor(EQB[:], cst("iota")[:, BC * q:BC * q + BC].unsqueeze(1).to_broadcast([P, TPS, BC]),
                                      PF[:, 1, t].unsqueeze(2).to_broadcast([P, TPS, BC]), ALU.is_equal).then_inc(sem("eqb_ready"), 1)
                    dve.tensor_tensor(OA[:], cst("iota").unsqueeze(1).to_broadcast([P, TPS, KEYS]),
                                      PF[:, 0, t].unsqueeze(2).to_broadcast([P, TPS, KEYS]), ALU.is_equal).then_inc(sem("oa_ready"), 1)
                    dve.wait_ge(sem("eqb_ready"), n + 1 + it * 2)
                    dve.tensor_tensor(OB[:], EQB[:].unsqueeze(1).to_broadcast([P, 3, TPS, BC]),
                                      GS[:, :, t].unsqueeze(3).to_broadcast([P, 3, TPS, BC]), ALU.mult).then_inc(sem("ob_ready"), 1)
                    dve.wait_ge(sem("ob_ready"), n + 1 + it * 2)

                def product(s, q, k, it=0):
                    dve.wait_ge(sem("ge_ready"), s00 + s + 1 + it * 2)
                    if isinstance(it, int):
                        dve.wait_ge(sem("table_ready"), t0 + STEPS * (q + 1))
                    dve.tensor_tensor(GE[:, s % 2, :], GE[:, s % 2, :], flat(G[q % 2][:, bass.ds(it * 4 + 2 * k, 2), :]), ALU.mult)\
                       .then_inc(sem("a_ready"), 1)
                    dve.wait_ge(sem("ah_ready"), s00 + s + 1 + it * 2)
                    dve.wait_ge(sem("a_ready"), s00 + s + 1 + it * 2)
                    dve.tensor_tensor(AL[s % 2][:], GE[:, s % 2, :], AH[s % 2][:].bitcast(F32), ALU.subtract).then_inc(sem("al_ready"), 1)

                def dense_step(q, j, it=0):
                    s = STEPS * q + j
                    for n in (3, 4):
                        if not isinstance(it, int) or d0 + 2 * s + n < d0 + N_DENSE:
                            lo(d0 + 2 * s + n, it)
                    if s + 1 < PAIRS:
                        product(s + 1, q + (j + 1) // STEPS, (j + 1) % STEPS, it)
                    nq = q + 1 + (j + 1) // STEPS
                    if nq < CHUNKS:
                        one_hots(nq, (j + 1) % STEPS, it)

                for k in range(STEPS + 1):
                    one_hots(k // STEPS, k % STEPS)
                product(0, 0, 0)
                for q in range(CHUNKS):
                    with dve.Fori(0, STEPS // 2 - 1) as it:
                        for j in range(2):
                            dense_step(q, j, it)
                    for j in (STEPS - 2, STEPS - 1):
                        dense_step(q, j)
                nxt[0] = d0 + N_DENSE
                dve.wait_ge(sem("al_ready"), PAIRS * (l + 1))
                v.mark(dve.memset(SMALL[:, 44:45], 0.0), sem("picks_used"))
                dve.wait_ge(sem("f_done"), l + 1)
                dve.wait_ge(sem("x_back"), 32 * (l + 1))
                for tt in range(TT):
                    for n in range(2):
                        xv = X[:, tt, 512 * n:512 * n + 512]
                        ins = dve.scalar_tensor_tensor(out=xv, in0=xv, scalar=DN_ALPHA, in1=M[2 * tt + n][:], op0=ALU.mult, op1=ALU.add)
                v.step(ins)
                layer_norm(2 * l + 2)
            v.step(dve.memset(SMALL[:, 45:46], 0.0), sem("x_final"))

        @block.gpsimd
        def _(pool):
            p = Steps(pool, sem("pool_step"))
            pool.wait_ge(sem("cst_loaded"), 48)
            for l in range(DEPTH):
                h0 = HP_FIRST[l]
                evicted(pool, h0)
                pool.wait_ge(sem("t_done"), 4 * (2 * l + 2))
                for tt in range(TT):
                    for h in range(4):
                        ins = pool.tensor_tensor(VX[:, tt, h, :, :], VR[:, tt, 64 * h:64 * h + 64].unsqueeze(1).to_broadcast([P, 8, HEAD]),
                                                 cst("chunkmask").unsqueeze(2).to_broadcast([P, 8, HEAD]), ALU.mult)
                p.mark(ins, sem("vx_ready"))
                for n in range(2 * CONV_K):
                    m = 2 * CONV_K * l + n
                    if n >= 4:
                        pool.wait_ge(sem("diag_used"), m - 3)
                    p.mark(pool.tensor_scalar(DG[:, n % 4, :], cst("ident"), par(l, "cw", n), None, ALU.mult), sem("diag_ready"))
        @block.tensor
        def _(pe):
            def transposes(inst, src, ready):
                ready()
                for kp in range(4):
                    for j in range(2):
                        for tt in range(TT):
                            k = 2 * kp + j
                            ins = pe.transpose(M[kp][:, 256 * j + P * tt:256 * j + P * tt + P], src[:, tt, P * k:P * k + P], cst("ident"))
                    ins.then_inc(sem("t_done"), 1)

            def three(out_, ah, al, bh, bl, first, last, **kw):
                pe.matmul(out_, ah, bh, start=first, stop=False, **kw)
                pe.matmul(out_, ah, bl, start=False, stop=False, **kw)
                return pe.matmul(out_, al, bh, start=False, stop=last, **kw)

            def hp_wait(i, it=0, bank=True):
                pe.wait_ge(lo_ready, i + 1 + it * 4)
                if bank and reads_before(i) > 0:
                    pe.wait_ge(bank_free[i % 4], reads_before(i) + it)

            def half(i, modes, it=0, hh=XH, hl=XL, k0=0, first=True, last=True):
                hp_wait(i, it, first)
                s, b = i % SLOTS, PS[i % 4]
                wh, wl = (t[s][:].rearrange("p (k n) -> p k n", k=KT) for t in (HI, LO))
                if modes == "rr":
                    for tt in range(TT):
                        for k in range(KT):
                            ins = three(b[:, 256 * tt:256 * tt + 256], hh[:, k0 + k, P * tt:P * tt + P], hl[:, k0 + k, P * tt:P * tt + P],
                                        wh[:, k, :], wl[:, k, :], first and k == 0 and (last or tt == 0), last and k == KT - 1, skip_group_check=not (first and last))
                else:
                    for c, mode in enumerate(modes):
                        n = slice(P * c, P * c + P)
                        if mode == "c":
                            for k in range(KT):
                                ins = three(b[:, 256 * c:256 * c + 256], wh[:, k, n], wl[:, k, n], hh[:, k, :], hl[:, k, :], k == 0, k == KT - 1)
                        else:
                            for tt in range(TT):
                                for k in range(KT):
                                    ins = three(b[:, 256 * c + P * tt:256 * c + P * tt + P], hh[:, k, P * tt:P * tt + P], hl[:, k, P * tt:P * tt + P],
                                                wh[:, k, n], wl[:, k, n], k == 0, k == KT - 1)
                ins.then_inc(hp_used, 1)

            def attention_pe(g0, heads, q, k, val, part, PM=PM, PT=PT):
                def scores(n):
                    g = g0 + n
                    if n >= 2:
                        pe.wait_ge(sem("exp_ready"), g - 1)
                    for qt in range(2):
                        ins = pe.matmul(M[g % 2][:, 256 * qt:256 * qt + 256], q(n)[:, P * qt:P * qt + P], k(n), start=True, stop=True)
                    ins.then_inc(sem("sc_done"), 1)

                scores(0)
                scores(1)
                for n in range(heads):
                    g = g0 + n
                    pe.wait_ge(sem("sm_ready"), g + 1)
                    if n >= 1:
                        pe.wait_ge(sem("pt_ready"), g)
                    for kt in range(2):
                        for qt in range(2):
                            ins = pe.transpose(M[2][:, 256 * kt + P * qt:256 * kt + P * qt + P], PM[:, g % 2, qt, P * kt:P * kt + P], cst("ident"))
                    ins.then_inc(sem("pt_done"), 1)
                    if n + 2 < heads:
                        scores(n + 2)
                    pe.wait_ge(sem("pt_ready"), g + 1)
                    if n >= 1:
                        pe.wait_ge(sem("o_ready"), g)
                    o = part(n)
                    for kt in range(2):
                        ins = pe.matmul(M[3][o:o + 64, 0:256], val(n, kt), PT[:, g % 2, kt, :], start=(kt == 0), stop=(kt == 1))
                    ins.then_inc(sem("pv_done"), 1)

            pe.wait_ge(sem("cst_loaded"), 48)
            transposes(0, X, lambda: pe.wait_ge(sem("mem_loaded"), 16))
            pe.wait_ge(sem("xl_ready"), 4)
            for i in range(N_MEM):
                half(i, "cc" if i % 2 == 0 else "rr")
            for l in range(DEPTH):
                h0 = HP_FIRST[l]
                transposes(1 + 2 * l, XS, lambda: pe.wait_ge(sem("rows_ready"), 2 * l + 1))
                pe.wait_ge(sem("xl_ready"), 4 * (2 * l + 2))
                for u in range(N_IN):
                    half(h0 + u, "rr" if u == 0 else "cr" if u == 7 else "cc")
                evicted(pe, h0)
                for ht in range(2):
                    for tt in range(TT):
                        ins = pe.transpose(M[0][:, 256 * ht + P * tt:256 * ht + P * tt + P], VR[:, tt, P * ht:P * ht + P], cst("ident"))
                ins.then_inc(sem("vt_done"), 1)
                pe.wait_ge(sem("vt_ready"), l + 1)
                for n in range(2 * CHUNK):
                    d, g = divmod(n, CHUNK)
                    here = slice(g, 16) if d == 0 else slice(0, 16 - g)
                    pe.wait_ge(sem("lagx_ready"), 2 * CHUNK * l + n + 1)
                    pe.matmul(v16(M[n % 2][:])[:, :, here], cst("blk"), v16(XX[:, n % 2, :])[:, :, here], start=True, stop=True)\
                      .then_inc(sem("lag_done"), 1)
                started = set()
                for d in range(2):
                    pe.wait_ge(sem("ke_ready"), 2 * l + d + 1)
                    if d == 1:
                        pe.wait_ge(sem("u_read"), 8 * l + 4)
                    for tt in range(TT):
                        for ht in range(2):
                            ins = pe.transpose(M[2][:, 256 * tt + P * ht:256 * tt + P * ht + P], XX[:, 0, 256 * ht + P * tt:256 * ht + P * tt + P], cst("ident"))
                    ins.then_inc(sem("kt_done"), 1)
                    pe.wait_ge(sem("kr_ready"), 2 * l + d + 1)
                    pe.wait_ge(sem("vx_ready"), l + 1)
                    n = 0
                    for tt in (0, 1) if d == 0 else (1, 0):
                        for ht in range(2):
                            if n >= 2:
                                pe.wait_ge(sem("u_read"), 8 * l + 4 * d + n - 1)
                            for j in range(2):
                                c = 256 * tt + P * ht + 64 * j
                                ins = pe.matmul(M[3 - n % 2][64 * j:64 * j + 64, :], XX[:, 1, c:c + 64],
                                                VX[:, tt, 2 * ht + j, :, :].rearrange("p a b -> p (a b)"), start=True, stop=True)
                            ins.then_inc(sem("u_done"), 1)
                            n += 1
                    pe.wait_ge(sem("state_ready"), 2 * l + d + 1)
                    for ht in range(2):
                        for ch in range(NCH):
                            for j in range(2):
                                o = slice(64 * j, 64 * j + 64)
                                c = 256 * ht + CHUNK * ch
                                ins = pe.matmul(M[0][o, c:c + CHUNK], ST[o, ht, ch, :], QB[o, d, c:c + CHUNK],
                                                start=j not in started, stop=(d == 1), skip_group_check=True)
                                started.add(j)
                    ins.then_inc(sem("inter_done"), 1)
                pe.wait_ge(sem("hsq_ready"), l + 1)
                pe.matmul(M[1][:], cst("blk"), W[:], start=True, stop=True).then_inc(sem("hss_done"), 1)
                pe.wait_ge(sem("up_ready"), l + 1)
                for n in range(2 * CONV_K):
                    ct, k = divmod(n, CONV_K)
                    pe.wait_ge(sem("diag_ready"), 2 * CONV_K * l + n + 1)
                    ins = pe.matmul(M[2][:, 256 * ct:256 * ct + 256], DG[:, n % 4, :], UP[:, ct, k:k + TOK], start=(k == 0), stop=(k == CONV_K - 1))
                    ins.then_inc(sem("diag_used"), 1)
                for name, src, c0, done in (("cy0_ready", AC, 0, "csum_done"), ("csq_ready", SCN, 256, "cvar_done")):
                    pe.wait_ge(sem(name), 2 * (l + 1))
                    for ct in range(2):
                        ins = pe.matmul(M[3][:, c0:c0 + 256], cst("ones"), src[:, 256 * ct:256 * ct + 256], start=(ct == 0), stop=(ct == 1))
                    ins.then_inc(sem(done), 1)
                for name, lhs, done in (("qsq_ready", "blk", "qss_done"), ("qn_ready", "rot", "rot_done")):
                    pe.wait_ge(sem(name), l + 1)
                    for j in range(3):
                        n = 512 if j < 2 else 256
                        pe.matmul(M[j][:, 0:n], cst(lhs), flat(QK2[:])[:, 512 * j:512 * j + n], start=True, stop=True).then_inc(sem(done), 1)
                pe.wait_ge(sem("qk_ready"), l + 1)
                attention_pe(8 * l, 8, lambda n: QK[64 * (n // 4):64 * (n // 4) + 64, n % 4, :],
                             lambda n: QK[64 * (n // 4):64 * (n // 4) + 64, 4, :],
                             lambda n, kt: VA[:, kt, 64 * (n // 4):64 * (n // 4) + 64], lambda n: 64 * (n // 4))
                pe.wait_ge(sem("mixl_ready"), l + 1)
                for u in range(N_OUT):
                    half(h0 + N_IN + u, "rr")
                h1 = h0 + N_IN + N_OUT
                transposes(2 + 2 * l, XS2, lambda: pe.wait_ge(sem("rows_ready"), 2 * l + 2))
                pe.wait_ge(sem("xl_ready"), 4 * (2 * l + 3))
                with pe.Fori(0, N_UP // 4) as it:
                    for u in range(4):
                        half(h1 + u, "cc", it)
                h2 = h1 + N_UP
                pe.wait_ge(sem("hid_ready"), 16 * (l + 1) + 2)
                for u in range(N_DOWN):
                    half(h2 + u, "rr", 0, HH, HL, 8 * (u // 4), u < 4, u >= N_DOWN - 4)
            k96 = slice(0, GLA_K)
            for l in range(DEPTH):
                s0 = HP_SECOND[l]
                transposes(5 + 2 * l, X, lambda: pe.wait_ge(sem("x_ready"), 2 * l + 1))
                pe.wait_ge(sem("xl_ready"), 4 * (6 + 2 * l))
                if l > 0:
                    for u in range(N_SHARED):
                        half(HP_SHARED + u, "cc" if u < 3 else "rr")
                for u in range(N_MIX2[l]):
                    half(s0 + u, "rr" if l == 0 and u >= 5 else "cc")
                for u in range(4):
                    evicted(pe, s0 + N_MIX2[l] - 4 + u)
                pe.wait_ge(sem(f"mix_loaded{l}"), 64 if l == 0 else 48)
                if l == 0:
                    for h in range(4):
                        ins = pe.matmul(M[h // 2][k96, 256 * (h % 2):256 * (h % 2) + 256], WG2[96:112, GLA_K * h:GLA_K * h + GLA_K],
                                        GQ[96:112, 0, :], start=True, stop=True, tile_position=(96, 0))
                    ins.then_inc(sem("gpre_done"), 1)
                    pe.wait_ge(sem("gqk_ready"), 1)
                    for tt in range(TT):
                        for h in range(4):
                            ins = pe.transpose(M[2 + tt][:, GLA_K * h:GLA_K * h + GLA_K], KE[k96, h, P * tt:P * tt + P], cst("ident")[k96, k96])
                    ins.then_inc(sem("ket_done"), 1)
                    for h in range(4):
                        for ch in range(4):
                            c = slice(GLA_C * ch, GLA_C * ch + GLA_C)
                            a_ = GLA_C * (2 * h + ch // 2)
                            ins = pe.matmul(M[0][64 * (ch % 2):64 * (ch % 2) + 64, a_:a_ + GLA_C], KTD[k96, h, c], QTD[k96, h, c], start=True, stop=True)
                    ins.then_inc(sem("gatt_done"), 1)
                    pe.wait_ge(sem("gattm_ready"), 1)
                    pe.wait_ge(sem("ker_ready"), 1)
                    for ch in range(4):
                        r, tt = slice(64 * (ch % 2), 64 * (ch % 2) + 64), ch // 2
                        if ch >= 1:
                            pe.wait_ge(sem("sta_ready"), ch)
                            pe.wait_ge(sem("go_ready"), ch)
                        for h in range(4):
                            o = M[2 + h // 2][r, GLA_V * (h % 2):GLA_V * (h % 2) + GLA_V]
                            ins = pe.matmul(o, ATT[r, 2 * h + tt, :], GV[r, tt, GLA_V * h:GLA_V * h + GLA_V], start=True, stop=(ch == 0))
                            if ch > 0:
                                ins = pe.matmul(o, QTD[k96, h, GLA_C * ch:GLA_C * ch + GLA_C], STA[k96, h, :], start=False, stop=True)
                        ins.then_inc(sem("oc_done"), 1)
                        if ch < 3:
                            for h in range(4):
                                ins = pe.matmul(M[h // 2][k96, GLA_V * (h % 2):GLA_V * (h % 2) + GLA_V], KER[r, tt, GLA_K * h:GLA_K * h + GLA_K],
                                                GV[r, tt, GLA_V * h:GLA_V * h + GLA_V], start=True, stop=True)
                            ins.then_inc(sem("uc_done"), 1)
                    pe.wait_ge(sem("gon_ready"), 1)
                    for kt in range(6):
                        for tt in range(TT):
                            c = 256 * (kt % 2) + P * tt
                            ins = pe.transpose(M[kt // 2][:, c:c + P], GO[:, tt, P * kt:P * kt + P], cst("ident"))
                    ins.then_inc(sem("got_done"), 1)
                    pe.wait_ge(sem("glamix_ready"), 1)
                else:
                    def slot_scores(n):
                        if n >= 2:
                            pe.wait_ge(sem("dsc_read"), n - 1)
                        sl, qt = divmod(n, 2)
                        b2 = [M[0], M[1]] if n % 2 == 0 else [PS[0], PS[1]]
                        for g in range(GROUPS):
                            ins = pe.matmul(b2[g // 2][:, 256 * (g % 2):256 * (g % 2) + 256], QD[:, SLOT_H * g + sl, P * qt:P * qt + P],
                                            KD[:, sl, :], start=True, stop=True)
                        ins.then_inc(sem("dsc_done"), 1)

                    slot_scores(0)
                    slot_scores(1)
                    for sl in range(SLOT_H):
                        if sl + 1 < SLOT_H:
                            slot_scores(2 * sl + 2)
                            slot_scores(2 * sl + 3)
                        pe.wait_ge(sem("dsm_ready"), 2 * sl + 2)
                        if sl >= 1:
                            pe.wait_ge(sem("dpt_ready"), sl)
                        for kt in range(2):
                            for qt in range(2):
                                ins = pe.transpose(M[2][:, 256 * kt + P * qt:256 * kt + P * qt + P], PD[:, sl % 2, qt, P * kt:P * kt + P], cst("ident"))
                        ins.then_inc(sem("dpt_done"), 1)
                        pe.wait_ge(sem("dpt_ready"), sl + 1)
                        if sl >= 1:
                            pe.wait_ge(sem("do_ready"), sl)
                        for kt in range(2):
                            ins = pe.matmul(M[3][:, 0:256], VD[:, kt, P * sl:P * sl + P], PTD[:, kt, :], start=(kt == 0), stop=(kt == 1))
                        ins.then_inc(sem("dpv_done"), 1)
                    pe.wait_ge(sem("do_ready"), SLOT_H)
                    pe.wait_ge(sem("dsc_read"), 2 * SLOT_H)
                attention_pe(16 + 4 * l, 4, lambda n: QM[64 * (n % 2):64 * (n % 2) + 64, n // 2, :],
                             lambda n: KVL[64 * (n % 2):64 * (n % 2) + 64, 256 * (n // 2):256 * (n // 2) + 256],
                             lambda n, kt: KVL[:, 512 + 256 * kt + 64 * n:512 + 256 * kt + 64 * n + 64], lambda n: 64 * (n % 2), PM2, PT2)
                pe.wait_ge(sem("mix2l_ready"), l + 1)
                for u in range(N_OUT):
                    half(s0 + N_MIX2[l] + u, "rr")
                w0 = s0 + N_MIX2[l] + N_OUT
                transposes(6 + 2 * l, X, lambda: pe.wait_ge(sem("x_ready"), 2 * l + 2))
                pe.wait_ge(sem("xl_ready"), 4 * (7 + 2 * l))
                for u in range(N_WQ):
                    half(w0 + u, "cc")
                for u in range(4):
                    evicted(pe, w0 + N_WQ - 4 + u)
                pe.wait_ge(sem("keys_loaded"), 16 * (l + 1))
                for j in range(8):
                    if j >= 4:
                        pe.wait_ge(sem("keysc_ready"), 8 * l + j - 3)
                    for g in range(4):
                        q_ = 4 * (j % 4) + g
                        ins = pe.matmul(M[j % 4][:, P * g:P * g + P], QP[:, q_, P * (j // 4):P * (j // 4) + P], SK[:, q_ % 2, :], start=True, stop=True)
                    ins.then_inc(sem("keysc_done"), 1)
                pe.wait_ge(sem("keysc_ready"), 8 * l + 8)
                pe.wait_ge(sem("sel_ready"), l + 1)
                for c in range(3):
                    for tt in range(TT):
                        ins = pe.transpose(M[c // 2][:, 256 * (c % 2) + P * tt:256 * (c % 2) + P * tt + P], SEL[:, c, tt, :], cst("ident"))
                ins.then_inc(sem("selt_done"), 1)
                pe.wait_ge(sem("pf_ready"), l + 1)
                for n in range(4):
                    for j in range(4):
                        pe.matmul(M[n][:, P * j:P * j + P], cst("zero"), cst("zero"), start=(j == 0), stop=False, skip_group_check=True)
                d0 = w0 + N_WQ
                t0, s00 = (CHUNKS * STEPS) * l, PAIRS * l

                def table(q, k, it=0):
                    n = t0 + STEPS * q + k
                    pe.wait_ge(sem("oa_ready"), n + 1 + it * 2)
                    pe.wait_ge(sem("ob_ready"), n + 1 + it * 2)
                    if n >= 2:
                        pe.wait_ge(sem("table_ready"), n - 1 + it * 2)
                    for t in range(TPS):
                        for c in range(3):
                            ins = pe.matmul(PS[2 + k % 2][:, BC * t:BC * t + BC], OA[:, t, :], OB[:, c, t, :], start=(c == 0), stop=(c == 2))
                    ins.then_inc(sem("table_done"), 1)

                def expert_in(i, s, it=0):
                    pe.wait_ge(lo_ready, i + 1 + it * 4)
                    if s >= 1:
                        pe.wait_ge(sem("ge_ready"), s00 + s - 1 + it * 2)
                    wh, wl = (t[i % SLOTS][:].rearrange("p (k n) -> p k n", k=KT) for t in (HI, LO))
                    for c in range(2):
                        n = slice(P * c, P * c + P)
                        for k in range(KT):
                            ins = three(PS[s % 2][:, 256 * c:256 * c + 256], wh[:, k, n], wl[:, k, n], XH[:, k, :], XL[:, k, :], k == 0, k == KT - 1)
                    ins.then_inc(hp_used, 1)

                def expert_out(i, s, it=0):
                    pe.wait_ge(lo_ready, i + 1 + it * 4)
                    pe.wait_ge(sem("al_ready"), s00 + s + 1 + it * 2)
                    vh, vl = (t[i % SLOTS][:].rearrange("p (b n) -> p b n", b=2) for t in (HI, LO))
                    for bi in range(2):
                        for tt in range(TT):
                            for n in range(2):
                                c = slice(512 * n, 512 * n + 512)
                                m = slice(256 * bi + P * tt, 256 * bi + P * tt + P)
                                ins = three(M[2 * tt + n][:], AH[s % 2][:, m], AL[s % 2][:, m], vh[:, bi, c], vl[:, bi, c], False, False, skip_group_check=True)
                    ins.then_inc(hp_used, 1)

                def dense_step(q, j, it=0):
                    s = STEPS * q + j
                    if s + 1 < PAIRS:
                        expert_in(d0 + 2 * s + 1, s + 1, it)
                    if q + 1 < CHUNKS:
                        table(q + 1, j, it)
                    expert_out(d0 + (2 * s + 2 if s + 1 < PAIRS else 2 * s + 1), s, it)

                for k in range(STEPS):
                    table(0, k)
                expert_in(d0, 0)
                for q in range(CHUNKS):
                    with pe.Fori(0, STEPS // 2 - 1) as it:
                        for j in range(2):
                            dense_step(q, j, it)
                    for j in (STEPS - 2, STEPS - 1):
                        dense_step(q, j)
                for n in range(4):
                    ins = pe.matmul(M[n][:, 0:P], cst("zero"), cst("zero"), start=False, stop=True, skip_group_check=True)
                ins.then_inc(sem("f_done"), 1)



def _half_panels(w):
    n = w.shape[1]
    return w.reshape(KT, P, n // 256, 256).transpose(2, 1, 0, 3).reshape(n // 256, P, HP)


def _constants():
    c = np.zeros((P, N_CONST), np.float32)
    i = np.arange(P)

    def put(name, v):
        a, b = CONST[name]
        c[:, a:b] = v

    put("ident", np.eye(P))
    put("iota", i[None, :])
    put("blk", (i[:, None] // HEAD) == (i[None, :] // HEAD))
    put("ones", 1.0)
    rot = np.zeros((P, P))
    for m in range(P):
        if m % 32 < 16:
            rot[m + 16, m] = -1.0
        else:
            rot[m - 16, m] = 1.0
    put("rot", rot)
    tok = np.arange(TOK)
    inv = (np.float32(10000.0) ** (-np.arange(0, 32, 2, dtype=np.float32) / np.float32(32)))
    pos = np.where(((i % 64) // 32 == 0)[:, None], (tok // 64)[None, :], (tok % 64)[None, :]).astype(np.float32)
    ang = pos * inv[i % 16][:, None]
    put("cos", np.cos(ang))
    put("sin", np.sin(ang))
    put("chunkmask", (i[:, None] // CHUNK) == np.arange(8)[None, :])
    j = np.arange(16)
    for name, v in (("first", j == 0), ("notfirst", j > 0), ("last", j == 15), ("notlast", j < 15)):
        put(name, v)
    put("gscan", (np.arange(64) > 0))
    put("causal", (i % 64)[:, None] <= np.arange(64)[None, :])
    return c


def _order_in():
    sizes = [512, 128, 128, 256, 256, 256, 256, 256, 256, 256]
    at = np.concatenate([[0], np.cumsum(sizes)])
    qa, ka, va, qh, ih, ff, fb, gh, ac, gc = [np.arange(at[n], at[n + 1]) for n in range(10)]
    heads = qa.reshape(8, HEAD)
    q = np.concatenate([heads[[c, c + 4]].reshape(-1) for c in range(4)])
    return np.concatenate([ih, qh, ff, fb, gh, ac, gc, ka, va, q])


def _order_out():
    heads = np.arange(512).reshape(8, HEAD)
    return np.concatenate([heads[[c, c + 4]].reshape(-1) for c in range(4)] + [np.arange(512, 1024)])


def _columns(v):
    return v.reshape(v.shape[0], -1, P).transpose(0, 2, 1)


def layout_first(inp):
    f = lambda n: np.asarray(inp[n])
    parts = []
    wm = f("w_mem_kv_2")
    for l in range(DEPTH):
        parts.append(_half_panels(wm[l]))
    oi, oo = _order_in(), _order_out()
    for l in range(DEPTH):
        parts.append(_half_panels(f("w_in")[l][:, oi]))
        parts.append(_half_panels(f("w_out")[l][oo]))
        parts.append(_half_panels(f("w_mlp_in")[l]))
        for kc in range(4):
            parts.append(_half_panels(f("w_mlp_out")[l][1024 * kc:1024 * kc + 1024]))
    par = np.concatenate([
        _columns(f("norm_mix")), _columns(f("norm_mlp")),
        np.tile(f("q_norm"), (1, 2))[:, :, None], np.tile(f("k_norm"), (1, 2))[:, :, None],
        _columns(f("hgrn_norm")),
        f("conv_w").reshape(DEPTH, CONV_K, 2, P).transpose(0, 3, 2, 1).reshape(DEPTH, P, 62),
        _columns(f("conv_b")), _columns(f("conv_ln_g")), _columns(f("conv_ln_b"))], axis=2)
    lb = np.stack([f("hgrn_lb_fwd"), f("hgrn_lb_bwd")], 1).reshape(DEPTH, 2, 2, P).transpose(3, 0, 1, 2).reshape(P, 8)
    lb = np.concatenate([lb, np.zeros((P, 8), np.float32)], 1)
    return parts, par, lb


def layout_second(inp):
    f = lambda n: np.asarray(inp[n])
    parts = []
    qk = np.arange(GLA_H * GLA_K).reshape(GLA_H, GLA_K)
    wa = f("a_w_in_2")[0]
    n_qk, n_v = GLA_H * GLA_K, GLA_H * GLA_V
    gate0 = 2 * n_qk + 2 * n_v
    pad = np.zeros((D, 2 * GLA_H, P), np.float32)
    pad[:, :, :GLA_K] = wa[:, :2 * n_qk].reshape(D, 2 * GLA_H, GLA_K)
    pad[:, 0, GLA_K:GLA_K + 16] = wa[:, gate0:gate0 + 16]
    a_in = np.concatenate([pad.reshape(D, -1), wa[:, gate0 + 16:], wa[:, 2 * n_qk:gate0]], axis=1)
    for l, w_in in enumerate([a_in, f("b_w_in_2")[0]]):
        if l > 0:
            parts.append(_half_panels(f("shared_w_kv_2")))
        parts.append(_half_panels(w_in))
        parts.append(_half_panels(f("w_out_2")[l]))
        parts.append(_half_panels(f("peer_w_q_2")[l]))
        u = f("peer_u_2")[l].reshape(KEYS, PAIRS, 2, KT, P).transpose(1, 4, 3, 2, 0).reshape(PAIRS, P, HP)
        v = f("peer_v_2")[l].reshape(KEYS, PAIRS, 2, D).transpose(1, 0, 2, 3).reshape(PAIRS, P, HP)
        dense = np.empty((2 * PAIRS, P, HP), np.float32)
        dense[0], dense[-1] = u[0], v[-1]
        dense[1:-1:2], dense[2:-1:2] = u[1:], v[:-1]
        parts.append(dense)
    par2 = np.zeros((P, 16), np.float32)
    par2[:GLA_K, 0:GLA_H] = f("a_b_gate_2")[0].reshape(GLA_H, GLA_K).T
    par2[:, 4:10] = f("a_norm_g_2")[0].reshape(6, P).T
    rows = np.stack([np.stack([f(f"ln_{n}_g_2")[l], f(f"ln_{n}_b_2")[l]]) for l in range(DEPTH) for n in ("mix", "ffn")])
    keys = np.ascontiguousarray(f("peer_sub_keys_2").transpose(0, 3, 1, 2))
    return parts, par2, np.ascontiguousarray(f("a_w_gate2_2")[0]), rows, keys


def _dilated_mask():
    i, j = np.arange(TOK)[:, None], np.arange(TOK)[None, :]
    groups = [(i >= j) & (i - j <= w) & ((i - j) % d == 0) for w, d in ((128, 1), (512, 4), (2048, 16))]
    m = np.where(np.stack(groups, 1), 0.0, NEG).astype(np.float32)
    return np.ascontiguousarray(m.reshape(TT, P, GROUPS * TOK).transpose(1, 0, 2))


def kernel(**inputs):
    import concourse.bacc as _bacc
    from concourse.bass_utils import run_bass_kernel_spmd

    parts, par, lb = layout_first(inputs)
    more, par2, wg2, rows, keys = layout_second(inputs)
    f = lambda n: np.asarray(inputs[n])
    arrays = {"stream": np.concatenate(parts + more, 0), "x": f("x")[0], "mem": f("mem_2")[0], "consts": _constants(),
              "par": np.ascontiguousarray(par), "lb": np.ascontiguousarray(lb), "par2": par2, "wg2": wg2,
              "mask": _dilated_mask(), "rows": rows, "keys": keys}
    nc = _bacc.Bacc("TRN2", target_bir_lowering=False, num_devices=1)
    aps = {k: nc.dram_tensor(k, v.shape, F32, kind="ExternalInput").ap() for k, v in arrays.items()}
    out = nc.dram_tensor("out", (TOK, D), F32, kind="ExternalOutput").ap()
    build(nc, aps["stream"], aps["x"], aps["mem"], aps["consts"], aps["par"], aps["lb"], aps["par2"], aps["wg2"], aps["mask"],
          aps["rows"], aps["keys"], out)
    r = run_bass_kernel_spmd(nc, [arrays], core_ids=[0])
    return np.asarray(r.results[0]["out"]).reshape(1, TOK, D)
```

```python
from contextlib import ExitStack

import numpy as np
import concourse.bass as bass
from concourse import mybir

F32 = mybir.dt.float32
BF16 = mybir.dt.bfloat16
F32R = mybir.dt.float32r
I32 = mybir.dt.int32
U32 = mybir.dt.uint32
ALU = mybir.AluOpType
ACT = mybir.ActivationFunctionType
AX = mybir.AxisListType

P = 128
TOK = 256
TT = TOK // P
D = 1024
KT = D // P
DEPTH = 2
HP = 2048
SLOTS = 4
HEAD = 64
EPS = 1e-6
LN_EPS = 1e-5
CHUNK = 16
NCH = TOK // CHUNK
CONV_K = 31
CONV_PAD = 15
D_FF = 4096
GLA_H, GLA_K, GLA_V, GLA_C = 4, 96, 192, 64
SLOT_H = 6
GROUPS = 3
DN_ALPHA = (2.0 * DEPTH) ** 0.25
NEG = -1.0e30
KEYS = 128
PH = 8
TOPK = 16
PAIRS = KEYS // 2
CHUNKS = 4
BC = KEYS // CHUNKS
STEPS = PAIRS // CHUNKS
AHEAD = 8
TPS = TOK // STEPS

N_MEM = 2 * DEPTH
N_IN, N_OUT, N_UP, N_DOWN = 10, 4, 16, 16
N_FIRST = N_IN + N_OUT + N_UP + N_DOWN
N_MIX2, N_WQ, N_DENSE, N_SHARED = [11, 10], 8, 2 * PAIRS, 6
N_SECOND = [m + N_OUT + N_WQ + N_DENSE for m in N_MIX2]
HP_FIRST = [N_MEM + l * N_FIRST for l in range(DEPTH)]
HP_SHARED = N_MEM + DEPTH * N_FIRST + N_SECOND[0]
HP_SECOND = [N_MEM + DEPTH * N_FIRST, HP_SHARED + N_SHARED]
HP_DENSE = [HP_SECOND[l] + N_MIX2[l] + N_OUT + N_WQ for l in range(DEPTH)]
N_HP = HP_SECOND[1] + N_SECOND[1]



def u_at(s):
    return s if s < AHEAD else 2 * s - 1


def v_at(s):
    return AHEAD + s if s < AHEAD - 1 else min(2 * s + 2, N_DENSE - 1)


CONST = {}
_c = 0
for _n, _w in (("ident", 128), ("iota", 128), ("zero", 128), ("blk", 128), ("ones", 128), ("rot", 128),
               ("cos", 256), ("sin", 256), ("chunkmask", 8), ("notfirst", 16), ("first", 16),
               ("notlast", 16), ("last", 16), ("gscan", 64), ("causal", 64)):
    CONST[_n] = (_c, _c + _w)
    _c += _w
N_CONST = _c
PAR = {}
_c = 0
for _n, _w in (("norm_mix", 8), ("norm_mlp", 8), ("qg", 1), ("kg", 1), ("ng", 2), ("cw", 62), ("cb", 2),
               ("lng", 2), ("lnb", 2)):
    PAR[_n] = (_c, _c + _w)
    _c += _w
N_PAR = _c


class Steps:

    def __init__(self, eng, own):
        self.eng, self.own, self.count = eng, own, {}

    def mark(self, ins, s=None, n=1):
        s = self.own if s is None else s
        self.count[s.name] = self.count.get(s.name, 0) + n
        ins.then_inc(s, n)
        return self.count[s.name]

    def step(self, ins, s=None):
        s = self.own if s is None else s
        self.eng.wait_ge(s, self.mark(ins, s))


def build(nc, stream, x_in, mem_in, const_in, par_in, lb_in, par2_in, wg2_in, mask_in, rows_in, sk_in, out):
    ctx = ExitStack()
    with ctx:
        sems = {}

        def sem(name):
            if name not in sems:
                sems[name] = ctx.enter_context(nc.semaphore(name))
            return sems[name]

        cursor = [(nc.sbuf_base + 63) // 64 * 64]
        end = nc.sbuf_usable_end // 64 * 64

        def at(name, shape, dt=F32, off=None):
            size = int(np.prod(shape[1:])) * (2 if dt == BF16 else 4)
            o = cursor[0] if off is None else off
            if off is None:
                cursor[0] += (size + 63) // 64 * 64
            assert o + size <= end, (name, o + size, end)
            return nc.alloc_sbuf_tensor_at(name, list(shape), dt, offset=o)

        RAW = at("raw", [P, SLOTS, HP])
        HI = [at(f"hi{i}", [P, HP], F32R) for i in range(SLOTS)]
        LO = [at(f"lo{i}", [P, HP], F32R) for i in range(SLOTS)]
        XH = at("xh", [P, KT, TOK], F32R)
        XL = at("xl", [P, KT, TOK], F32R)
        cst0 = cursor[0]
        CST = at("cst", [P, N_CONST])
        SMALL = at("small", [P, 64])
        X = at("x", [P, TT, D])
        mix0 = cursor[0]
        LBS = at("lbs", [P, 16], off=end - 64)
        PR = at("pr", [P, DEPTH, N_PAR], off=end - 64 - 704)
        LB = at("lb", [P, DEPTH, 2, 2, 2], off=end - 64 - 704 - 64)
        top = end - 64 - 704 - 64

        E = at("e", [P, 2, 2 * TOK])
        F = at("f", [P, 2, 2 * TOK])
        KG = at("kg", [P, 2, 2 * TOK])
        MIXF = at("mixf", [P, KT, TOK], off=cursor[0] - 8192)
        Q = at("q", [P, 2 * TOK])
        VR = at("vr", [P, TT, 256])
        VT = at("vt", [P, 2 * TOK])
        GT = at("gt", [P, 2 * TOK])
        AC = at("ac", [P, 2 * TOK])
        EG = at("eg", [P, 2 * TOK])
        UP = at("up", [P, 2, TOK + 2 * CONV_PAD])
        W = at("w", [P, 2 * TOK])
        XX = at("xx", [P, 2, 2 * TOK])
        TB = at("tb", [P, 2 * TOK])
        ACC = at("acc", [P, 2 * TOK])
        SCN = at("scn", [P, 2 * TOK])
        QB = at("qb", [P, 2, 2 * TOK])
        ST = [at("st0", [P, 2, NCH, HEAD]), at("st1", [P, 2, NCH, HEAD], off=mix0)]
        DG = at("dg", [P, 4, P])
        QK = at("qk", [P, 5, TOK])
        VA = at("va", [P, TT, P])
        r1 = cursor[0]
        VX = at("vx", [P, TT, 4, 8, HEAD])
        assert cursor[0] <= top, (cursor[0], top)
        XS = at("xs", [P, TT, D], off=r1)
        QK2 = at("qk2", [P, 5, TOK], off=r1)
        QK3 = at("qk3", [P, 5, TOK], off=r1 + 5 * TOK * 4)
        PM = at("pm", [P, 2, 2, TOK], off=r1)
        PT = at("pt", [P, 2, 2, TOK], off=r1 + 4096)
        KVM = at("kvm", [P, 1024], off=r1)
        HH = at("hh", [P, 32, TOK], F32R, off=mix0)
        HL = at("hl", [P, 32, TOK], F32R, off=mix0 + 32768)
        RB = at("rb", [P, 2, 2 * TOK], off=mix0 + 65536)
        SQ = at("sq", [P, 2 * TOK], off=mix0 + 65536 + 4096)
        XS2 = at("xs2", [P, TT, D], off=mix0 + 65536 + 6144)
        assert mix0 + 65536 + 6144 + 8192 <= top

        def cst(name):
            a, b = CONST[name]
            return CST[:, a:b]

        def par(l, name, i=0, n=1):
            c = PAR[name][0] + i
            return PR[:, l, c:c + n]

        def flat(t):
            return t.rearrange("p a b -> p (a b)")

        def v16(t):
            return t.rearrange("p (a c) -> p a c", c=CHUNK)

        cursor[0] = mix0
        ROWS = at("rows", [P, 2, D])
        MIX2 = at("mix2", [P, KT, TOK])
        KVL = at("kvl", [P, 1024])
        QM = at("qm", [P, 2, TOK])
        PM2 = at("pm2", [P, 2, 2, TOK])
        PT2 = at("pt2", [P, 2, 2, TOK])
        both = cursor[0]
        GO2 = at("go2", [P, TT, 768], off=both)
        GQ = at("gq", [P, 4, TOK])
        GK = at("gk", [P, 4, TOK])
        GV = at("gv", [P, TT, 768])
        GR = at("gr", [P, TT, 768])
        LG = at("lg", [P, 4, TOK])
        KTD = at("ktd", [P, 4, TOK], off=cursor[0] - 4096)
        GO = at("go", [P, TT, 768], off=cursor[0] - 4096)
        RG = at("rg", [P, TT, 768], off=cursor[0] + 2048)
        B = at("b", [P, 4, TOK])
        KE = at("ke", [P, 4, TOK])
        SM = at("sm", [P, 4, TOK], off=cursor[0] - 4096)
        QTD = at("qtd", [P, 4, TOK])
        KER = at("ker", [P, TT, 4 * GLA_K])
        ATT = at("att", [P, 8, GLA_C])
        STA = at("sta", [P, 4, GLA_V])
        WG2 = at("wg2", [P, 4 * GLA_K])
        P2 = at("p2", [P, 16])
        BL = at("bl", [P, 16])
        assert cursor[0] <= end
        EXA = at("exa", [P, 4, TOK], off=both - 8192)
        EXB = at("exb", [P, 4, TOK], off=both - 4096)
        cursor[0] = both
        QD = at("qd", [P, GROUPS * SLOT_H, TOK])
        KD = at("kd", [P, SLOT_H, TOK])
        VD = at("vd", [P, TT, 768])
        DM = at("dm", [P, TT, GROUPS * TOK])
        S3 = at("s3", [P, 2, GROUPS * TOK])
        PD = at("pd", [P, 2, 2, TOK])
        PTD = at("ptd", [P, 2, TOK])
        assert cursor[0] <= end
        cursor[0] = mix0
        EQ = at("eq", [P, PH, TOPK, TOPK], off=mix0)
        QP = at("qp", [P, 2 * PH, TOK])
        CD2 = at("cd2", [P, PH, TOPK * TOPK], off=cursor[0])
        SC = at("sc", [P, TT, 2 * PH, KEYS])
        S2 = at("s2", [P, TT, 2 * PH, KEYS], off=cursor[0])
        CD = at("cd", [P, TT, PH, TOPK * TOPK])
        TS = at("ts", [P, TT, 2 * PH, TOPK])
        TI = at("ti", [P, TT, 2 * PH, TOPK], U32)
        TF = at("tf", [P, TT, 2 * PH, TOPK])
        BS = at("bs", [P, TT * PH, TOPK])
        GX = at("gx", [P, TT * PH, TOPK])
        BJ = at("bj", [P, TT, PH, TOPK], U32)
        BK = at("bk", [P, 2, TT * PH * TOPK], U32)
        JF = at("jf", [P, 2, TT, PH, TOPK])
        GSUM = at("gsum", [P, TT * PH])
        SEL = at("sel", [P, 3, TT, PH * TOPK])
        SK = at("sk", [P, 2, KEYS])
        HA = at("ha", [P, AHEAD, 512])
        assert cursor[0] <= end
        x0 = mix0 - 8192
        PF = at("pf", [P, TOK], off=x0)
        PB = at("pb", [P, 2, TOK], BF16, off=x0 + 1024)
        EQB = at("eqb", [P, BC, TPS], BF16, off=x0 + 2048)
        OB = at("ob", [P, 3, BC, TPS], BF16, off=x0 + 3072)
        GS = at("gs", [P, 3, TOK], BF16, off=x0 + 6144)
        IOT = at("iot", [P, KEYS, TPS], BF16, off=cst0 + 4 * CONST["blk"][0])
        cursor[0] = mix0
        G = [at(f"g{i}", [P, BC, TOK]) for i in range(2)]
        g1 = mix0 + 4 * BC * TOK
        GA = at("ga", [P, AHEAD, 512], off=g1)
        OA2 = at("oa2", [P, KEYS, TPS], BF16, off=g1 + 16384)
        OB2 = at("ob2", [P, 3, BC, TPS], BF16, off=g1 + 16384 + 4096)
        GE = at("ge", [P, 2, 512])
        AH = [at(f"ah{i}", [P, 512], F32R) for i in range(2)]
        AL = [at(f"al{i}", [P, 512], F32R) for i in range(2)]
        OA = at("oa", [P, KEYS, TPS], BF16)
        assert cursor[0] <= end
        x_scr = nc.dram_tensor("x_scratch", [P, TT, D], F32).ap()
        PS = [ctx.enter_context(nc.psum_tensor(f"lin{i}", [P, 512], F32)) for i in range(4)]
        M = [ctx.enter_context(nc.psum_tensor(f"m{i}", [P, 512], F32)) for i in range(4)]
        UB = [PS[0:4], [M[1], M[2], M[3], PS[0]]]
        mem_scr = nc.dram_tensor("mem_kv_scratch", [DEPTH, P, 1024], F32).ap()

        raw_loaded = [sem(f"raw_loaded{i}") for i in range(SLOTS)]
        bank_free = [sem(f"bank_free{i}") for i in range(4)]
        hi_ready, lo_ready, hp_used = sem("hi_ready"), sem("lo_ready"), sem("hp_used")

        read_out = [True] * N_HP
        for l in range(DEPTH):
            for i in range(N_DOWN - 4):
                read_out[HP_FIRST[l] + N_IN + N_OUT + N_UP + i] = False
            for i in range(N_DENSE):
                read_out[HP_DENSE[l] + i] = False

        def reads_before(i):
            return sum(read_out[j] for j in range(i % 4, i, 4))

        def evicted(eng, i, it=0):
            eng.wait_ge(bank_free[i % 4], reads_before(i) + 1 + it)

        block = ctx.enter_context(nc.Block())

        @block.sync
        def _(sp):
            sp.dma_start(X[:], mem_in.rearrange("(t p) d -> p t d", p=P)).then_inc(sem("mem_loaded"), 16)
            for i in range(SLOTS):
                sp.dma_start(RAW[:, i, :], stream[i]).then_inc(raw_loaded[i], 16)
            rounds = N_HP // SLOTS
            with sp.Fori(1, rounds) as g:
                for i in range(SLOTS):
                    sp.wait_ge(lo_ready, g * SLOTS + (i + 1 - SLOTS))
                    sp.dma_start(RAW[:, i, :], stream[g * SLOTS + i]).then_inc(raw_loaded[i], 16)
            for i in range(SLOTS * rounds, N_HP):
                sp.wait_ge(lo_ready, i + 1 - SLOTS)
                sp.dma_start(RAW[:, i % SLOTS, :], stream[i]).then_inc(raw_loaded[i % SLOTS], 16)
            sp.wait_ge(sem("x_final"), 1)
            sp.dma_start(out.rearrange("(t p) d -> p t d", p=P), X[:]).then_inc(sem("out_stored"), 16)
            sp.wait_ge(sem("out_stored"), 16)

        def attention_act(act, a, g0, heads, scale, dst, part, PM=PM, PT=PT, between=lambda n: None):
            def tail(n):
                g = g0 + n
                act.wait_ge(sem("pt_done"), g + 1)
                a.mark(act.activation(flat(PT[:, g % 2, :, :]), M[2][:], ACT.Copy), sem("pt_ready"))
                act.wait_ge(sem("pv_done"), g + 1)
                o = part(n)
                a.mark(act.activation(dst(n), M[3][o:o + 64, 0:256], ACT.Copy), sem("o_ready"))

            for n in range(heads):
                g = g0 + n
                act.wait_ge(sem("nb_ready"), g + 1)
                if n >= 2:
                    act.wait_ge(sem("pt_done"), g - 1)
                c = 16 + 8 * (g % 2)
                for qt in range(2):
                    ins = act.activation(PM[:, g % 2, qt, :], M[g % 2][:, 256 * qt:256 * qt + 256], ACT.Exp,
                                         scale=scale, bias=SMALL[:, c + 2 + qt:c + 3 + qt], accum_out=SMALL[:, c + 4 + qt:c + 5 + qt])
                a.mark(ins, sem("exp_ready"))
                if n >= 1:
                    tail(n - 1)
                between(n)
            tail(heads - 1)
            act.wait_ge(sem("o_ready"), g0 + heads)

        @block.scalar
        def _(act):
            a = Steps(act, sem("act_step"))
            nxt = [0]

            def hi(i, it=0):
                act.wait_ge(raw_loaded[i % SLOTS], 16 * (i // SLOTS + 1) + it * 16)
                if i >= SLOTS:
                    act.wait_ge(hp_used, i + 1 - SLOTS + it * SLOTS)
                act.activation(HI[i % SLOTS][:], RAW[:, i % SLOTS, :], ACT.Copy).then_inc(hi_ready, 1)

            def hi_to(n):
                while nxt[0] < min(n, N_HP):
                    hi(nxt[0])
                    nxt[0] += 1

            def xh_evict(inst, gain=None):
                for kp in range(4):
                    act.wait_ge(sem("t_done"), 4 * inst + kp + 1)
                    if gain is None:
                        ins = act.activation(flat(XH[:, 2 * kp:2 * kp + 2, :]), M[kp][:], ACT.Copy)
                    else:
                        act.activation(XH[:, 2 * kp, :], M[kp][:, 0:256], ACT.Copy, scale=gain(2 * kp))
                        ins = act.activation(XH[:, 2 * kp + 1, :], M[kp][:, 256:512], ACT.Copy, scale=gain(2 * kp + 1))
                    a.mark(ins, sem("xh_ready"))

            def rstd(out_, in_, n, eps, signal=None):
                a.step(act.activation(out_, in_, ACT.Ln, scale=1.0 / n, bias=eps))
                a.step(act.activation(out_, out_, ACT.Exp, scale=-0.5), signal)

            def rms_rows(junk):
                for tt in range(TT):
                    a.step(act.activation(junk[:, tt, :], X[:, tt, :], ACT.Square, accum_out=SMALL[:, tt:tt + 1]))
                rstd(SMALL[:, 2:4], SMALL[:, 0:2], D, EPS, sem("row_rstd"))

            act.dma_start(CST[:], const_in).then_inc(sem("cst_loaded"), 16)
            act.dma_start(LBS[:], lb_in).then_inc(sem("cst_loaded"), 16)
            act.dma_start(PR[:], par_in.rearrange("l p n -> p l n")).then_inc(sem("cst_loaded"), 16)
            act.preload_act_table_set("natural_log_exp_and_others")
            act.wait_ge(sem("lb_shifted"), 1)
            a.step(act.activation(LBS[:, 0:8], LBS[:, 0:8], ACT.Exp), sem("lb_exp"))
            hi_to(2)
            xh_evict(0)
            for l in range(DEPTH):
                hi_to(2 * l + 4)
                if l > 0:
                    act.wait_ge(sem("kvm_stored"), 16 * l)
                for i in (2 * l, 2 * l + 1):
                    act.wait_ge(hp_used, i + 1)
                    act.activation(KVM[:, 512 * (i % 2):512 * (i % 2) + 512], PS[i % 4][:], ACT.Copy).then_inc(bank_free[i % 4], 1)
                evicted(act, 2 * l)
                evicted(act, 2 * l + 1)
                act.dma_start(mem_scr[l], KVM[:]).then_inc(sem("kvm_stored"), 16)
            act.wait_ge(sem("t_done"), 4)
            act.dma_start(X[:], x_in.rearrange("(t p) d -> p t d", p=P)).then_inc(sem("x_loaded"), 16)
            act.wait_ge(sem("x_loaded"), 16)
            act.wait_ge(sem("kvm_stored"), 16 * DEPTH)

            for l in range(DEPTH):
                h0 = HP_FIRST[l]
                if l > 0:
                    for u in range(4):
                        evicted(act, h0 - 4 + u)
                rms_rows(XS)
                act.wait_ge(hp_used, h0)
                xh_evict(1 + 2 * l, lambda k: par(l, "norm_mix", k))
                dst = [VR, Q, (E, 0), (E, 1), GT, AC, EG, None, (QK, 0), (QK, 2)]
                for u in range(N_IN):
                    hi_to(h0 + u + 4)
                    i = h0 + u
                    act.wait_ge(hp_used, i + 1)
                    b = PS[i % 4]
                    if u == 7:
                        act.activation(QK[:, 4, :], b[:, 0:256], ACT.Copy)
                        ins = act.activation(flat(VA[:]), b[:, 256:512], ACT.Copy)
                    elif u in (2, 3):
                        ins = act.activation(E[:, u - 2, :], b[:], ACT.Exp, scale=-1.0)
                    elif u == 6:
                        ins = act.activation(EG[:], b[:], ACT.Exp, scale=-1.0)
                    elif u >= 8:
                        ins = act.activation(flat(QK[:, 2 * u - 16:2 * u - 14, :]), b[:], ACT.Copy)
                    else:
                        ins = act.activation(flat(VR[:]) if u == 0 else dst[u][:], b[:], ACT.Copy)
                    ins.then_inc(bank_free[i % 4], 1)
                    if u == 3:
                        act.wait_ge(sem("vt_done"), l + 1)
                        a.mark(act.activation(VT[:], M[0][:], ACT.Copy), sem("vt_ready"))
                hi_to(h0 + N_IN + N_OUT)
                for n in range(2 * CONV_K):
                    m = 2 * CONV_K * l + n
                    if n >= 4:
                        act.wait_ge(sem("diag_used"), m - 3)
                    a.mark(act.activation(DG[:, n % 4, :], cst("ident"), ACT.Copy, scale=par(l, "cw", n)), sem("diag_ready"))
                for d in range(2):
                    act.wait_ge(sem("kt_done"), 2 * l + d + 1)
                    a.step(act.activation(XX[:, 1 - d, :], M[2 - d][:], ACT.Copy), sem("kr_ready"))
                for j in range(3):
                    n = 512 if j < 2 else 256
                    act.wait_ge(sem("qss_done"), 3 * l + j + 1)
                    rstd(flat(QK3[:])[:, 512 * j:512 * j + n], M[1 + j][:, 0:n], HEAD, EPS, sem("qrs_ready"))
                act.wait_ge(sem("cvar_done"), l + 1)
                rstd(XX[:, 1, 0:256], PS[1][:, 256:512], 256, EPS, sem("crs_ready"))
                act.wait_ge(sem("hss_done"), l + 1)
                rstd(TB[:], PS[2][:], HEAD, EPS)
                a.step(act.activation(SCN[:], GT[:], ACT.Exp, scale=-1.0), sem("hrs_ready"))

                def conv_silu(n):
                    if n == 3:
                        act.wait_ge(sem("cy_ready"), l + 1)
                        a.step(act.activation(EG[:], AC[:], ACT.Exp, scale=-1.0), sem("ceg_ready"))

                attention_act(act, a, 8 * l, 8, HEAD ** -0.5, lambda n: MIXF[64 * (n // 4):64 * (n // 4) + 64, n % 4, :],
                              lambda n: 64 * (n // 4), between=conv_silu)
                act.wait_ge(sem("mix_ready"), l + 1)
                a.step(act.activation(flat(XH[:]), flat(MIXF[:]), ACT.Copy), sem("mixh_ready"))
                h1 = h0 + N_IN + N_OUT
                for u in range(4):
                    evicted(act, h1 - 4 + u)
                rms_rows(XS2)
                hi_to(h1 + 3)
                xh_evict(2 + 2 * l, lambda k: par(l, "norm_mlp", k))
                with act.Fori(0, N_UP // 4) as it:
                    for u in range(4):
                        hi(h1 + u + 3, it)
                        act.wait_ge(hp_used, h1 + u + 1 + it * 4)
                        act.wait_ge(sem("hid_ready"), 16 * l + u + 1 + it * 4)
                        act.activation(RB[:, u % 2, :], PS[(h1 + u) % 4][:], ACT.Relu).then_inc(bank_free[(h1 + u) % 4], 1)
                        evicted(act, h1 + u, it)
                        act.activation(flat(HH[:, bass.ds(it * 8 + 2 * u, 2), :]), RB[:, u % 2, :],
                                       ACT.Square).then_inc(sem("sq_ready"), 1)
                nxt[0] = h1 + N_UP + 3
                hi_to(h1 + N_UP + N_DOWN + 2)
            for l in range(DEPTH):
                s0 = HP_SECOND[l]
                act.wait_ge(sem("x_ready"), 2 * l + 1)
                act.wait_ge(hp_used, HP_SHARED if l > 0 else s0)
                for dst_, src_ in [(ROWS[:], rows_in[2 * l].partition_broadcast(P)), (KVL[:], mem_scr[l])] + \
                        ([(WG2[96:112, :], wg2_in), (P2[:], par2_in)] if l == 0 else [(DM[:], mask_in)]):
                    act.dma_start(dst_, src_).then_inc(sem(f"mix_loaded{l}"), 16)
                hi_to(HP_SHARED + 2 if l > 0 else s0 + 3)
                xh_evict(5 + 2 * l)
                if l > 0:
                    for u in range(N_SHARED):
                        hi_to(HP_SHARED + u + 4)
                        i = HP_SHARED + u
                        act.wait_ge(hp_used, i + 1)
                        b = PS[i % 4]
                        if u < 3:
                            ins = act.activation(flat(KD[:, 2 * u:2 * u + 2, :]), b[:], ACT.Copy)
                        else:
                            ins = act.activation(VD[:, :, 256 * (u - 3):256 * (u - 2)], b[:].rearrange("p (t n) -> p t n", t=2), ACT.Copy)
                        ins.then_inc(bank_free[i % 4], 1)
                for u in range(N_MIX2[l]):
                    hi_to(s0 + u + 4)
                    i = s0 + u
                    act.wait_ge(hp_used, i + 1)
                    b = PS[i % 4]
                    if l == 0 and u >= 5:
                        t, j = (GV, u - 5) if u < 8 else (GR, u - 8)
                        ins = act.activation(t[:, :, 256 * j:256 * j + 256], b[:].rearrange("p (t n) -> p t n", t=2), ACT.Copy)
                    else:
                        t = (QM if u == (4 if l == 0 else 9) else GQ[:, 2 * u:2 * u + 2, :] if u < 2 else GK[:, 2 * u - 4:2 * u - 2, :]) if l == 0 \
                            else QM if u == 9 else QD[:, 2 * u:2 * u + 2, :]
                        ins = act.activation(flat(t[:] if t is QM else t), b[:], ACT.Copy)
                    ins.then_inc(bank_free[i % 4], 1)
                hi_to(s0 + N_MIX2[l] + 3)
                k96 = slice(0, GLA_K)
                if l == 0:
                    act.wait_ge(sem("gpre_read"), 1)
                    act.wait_ge(sem("mix_loaded0"), 64)
                    for h in range(4):
                        ins = act.activation(EXA[k96, h, :], M[h // 2][k96, 256 * (h % 2):256 * (h % 2) + 256], ACT.Abs, bias=P2[k96, h:h + 1])
                    a.step(ins)
                    a.step(act.activation(flat(EXB[k96]), flat(EXA[k96]), ACT.Exp, scale=-1.0))
                    a.step(act.activation(flat(EXA[k96]), flat(EXB[k96]), ACT.Ln, bias=1.0), sem("lsig_ready"))
                    act.wait_ge(sem("cum_ready"), 1)
                    a.mark(act.activation(flat(EXA[k96]), flat(B[k96]), ACT.Exp, scale=1.0 / 16))
                    a.mark(act.activation(flat(EXB[k96]), flat(B[k96]), ACT.Exp, scale=-1.0 / 16))
                    a.mark(act.activation(flat(KE[k96]), flat(KE[k96]), ACT.Exp, scale=1.0 / 16))
                    a.step(act.activation(BL[k96], B[k96].rearrange("p h (n c) -> p (h n) c", c=GLA_C)[:, :, GLA_C - 1], ACT.Exp, scale=1.0 / 16), sem("gexp_ready"))
                    act.wait_ge(sem("ket_done"), 1)
                    for tt in range(TT):
                        ins = act.activation(KER[:, tt, :], M[2 + tt][:, 0:384], ACT.Copy)
                    a.step(ins, sem("ker_ready"))
                    a.step(act.activation(flat(RG[:]), flat(GR[:]), ACT.Exp, scale=-1.0), sem("rexp_ready"))
                    for ch in range(4):
                        rows = slice(64 * (ch % 2), 64 * (ch % 2) + 64)
                        act.wait_ge(sem("oc_done"), ch + 1)
                        for j in range(2):
                            ins = act.activation(GO[rows, ch // 2, 384 * j:384 * j + 384], M[2 + j][rows, 0:384], ACT.Copy)
                        a.step(ins, sem("go_ready"))
                    act.wait_ge(sem("gss_ready"), 1)
                    rstd(SMALL[:, 48:56], SMALL[:, 48:56], GLA_V, EPS, sem("grs_ready"))
                    act.wait_ge(sem("got_done"), 1)
                    for kt in range(6):
                        ins = act.activation(MIX2[:, kt, :], M[kt // 2][:, 256 * (kt % 2):256 * (kt % 2) + 256], ACT.Copy, scale=P2[:, 4 + kt:5 + kt])
                    a.step(ins, sem("glamix_ready"))
                else:
                    def slot_out(sl):
                        act.wait_ge(sem("dpt_done"), sl + 1)
                        a.mark(act.activation(flat(PTD[:]), M[2][:], ACT.Copy), sem("dpt_ready"))
                        act.wait_ge(sem("dpv_done"), sl + 1)
                        a.mark(act.activation(MIX2[:, sl, :], M[3][:, 0:256], ACT.Copy), sem("do_ready"))

                    for n in range(2 * SLOT_H):
                        act.wait_ge(sem("dnb_ready"), n + 1)
                        c = 48 + 2 * (n % 2)
                        a.mark(act.activation(S3[:, n % 2, :], S3[:, n % 2, :], ACT.Exp, scale=KEYS ** -0.5, bias=SMALL[:, c:c + 1],
                                              accum_out=SMALL[:, c + 1:c + 2]), sem("dexp_ready"))
                        if n >= 3 and n % 2 == 1:
                            slot_out(n // 2 - 1)
                    slot_out(SLOT_H - 1)
                    act.wait_ge(sem("do_ready"), SLOT_H)
                attention_act(act, a, 16 + 4 * l, 4, HEAD ** -0.5, lambda n: MIX2[64 * (n % 2):64 * (n % 2) + 64, 6 + n // 2, :],
                              lambda n: 64 * (n % 2), PM2, PT2)
                a.step(act.activation(flat(XH[:]), flat(MIX2[:]), ACT.Copy), sem("mix2h_ready"))
                w0 = s0 + N_MIX2[l] + N_OUT
                hi_to(w0)
                act.wait_ge(sem("ln_var"), 2 * l + 1)
                rstd(SMALL[:, 60:62], SMALL[:, 56:60].rearrange("p (t k) -> p t k", k=2)[:, :, 1], 1, LN_EPS, sem("ln_rstd"))
                def head_scores(h):
                    act.wait_ge(sem("keysc_done"), PH * l + h + 1)
                    a.mark(act.activation(SC[:, :, 2 * h:2 * h + 2, :], M[h % 4][:].rearrange("p (t s k) -> p t s k", t=TT, s=2), ACT.Copy), sem("keysc_ready"))

                act.wait_ge(sem("x_ready"), 2 * l + 2)
                act.dma_start(x_scr, X[:]).then_inc(sem("x_spilled"), 16)
                act.dma_start(SK[:], sk_in[l]).then_inc(sem("keys_loaded"), 16)
                hi_to(w0 + 3)
                xh_evict(6 + 2 * l)
                for u in range(N_WQ):
                    hi_to(w0 + u + 4)
                    i = w0 + u
                    act.wait_ge(hp_used, i + 1)
                    act.activation(flat(QP[:, 2 * u:2 * u + 2, :]), PS[i % 4][:], ACT.Copy).then_inc(bank_free[i % 4], 1)
                    if u >= 1:
                        head_scores(u - 1)
                head_scores(PH - 1)
                d0 = w0 + N_WQ
                for s in range(AHEAD):
                    hi_to(d0 + s + 4)
                    act.wait_ge(hp_used, d0 + s + 1)
                    act.activation(HA[:, s, :], PS[s % 2][:], ACT.Copy).then_inc(sem("ahead_copied"), 1)
                act.wait_ge(sem("gx_shifted"), l + 1)
                a.step(act.activation(flat(GX[:]), flat(GX[:]), ACT.Exp), sem("gx_ready"))
                act.wait_ge(sem("selt_done"), l + 1)
                act.wait_ge(sem("x_spilled"), 16 * (l + 1))
                a.mark(act.activation(flat(PB[:]), M[0][:], ACT.Copy))
                a.step(act.activation(PF[:], M[1][:, 0:256], ACT.Copy), sem("pf_ready"))

                t0, s00 = (CHUNKS * STEPS) * l, PAIRS * l

                def table_copy(q, k, it=0, per=2):
                    n = t0 + STEPS * q + k
                    act.wait_ge(sem("table_done"), n + 1 + it * per)
                    act.activation(G[q % 2][:, :, bass.ds(it * (per * TPS) + TPS * k, TPS)].rearrange("p b t -> p t b"),
                                   PS[2 + k % 2][:].rearrange("p (t b) -> p t b", b=BC), ACT.Copy).then_inc(sem("table_ready"), 1)

                def gelu(s, it=0):
                    act.wait_ge(hp_used, d0 + u_at(s) + 1 + it * 4)
                    act.wait_ge(sem("al_ready"), s00 + s - 1 + it * 2)
                    act.activation(GE[:, s % 2, :], PS[s % 2][:], ACT.Gelu).then_inc(sem("ge_ready"), 1)

                def act_high(s, it=0):
                    act.wait_ge(sem("a_ready"), s00 + s + 1 + it * 2)
                    if s >= 2:
                        act.wait_ge(hp_used, d0 + v_at(s - 2) + 1 + it * 4)
                    act.activation(AH[s % 2][:], GA[:, s, :] if s < AHEAD else GE[:, s % 2, :], ACT.Copy).then_inc(sem("ah_ready"), 1)

                def dense_step(q, j, it=0):
                    s = STEPS * q + j
                    if s < AHEAD - 2:
                        hi(d0 + AHEAD + 3 + s)
                    elif s >= AHEAD - 1:
                        for n in (3, 4):
                            if 2 * s + n < N_DENSE:
                                hi(d0 + 2 * s + n, it)
                    if AHEAD <= s + 1 < PAIRS:
                        gelu(s + 1, it)
                    two = q == 0 and AHEAD - 1 <= j < STEPS - 1
                    if two:
                        table_copy(1, 2 * (j - AHEAD + 1), it, 4)
                    elif 0 < q < CHUNKS - 1:
                        table_copy(q + 1, j, it)
                    if s + 1 < PAIRS:
                        act_high(s + 1, it)
                    if two:
                        table_copy(1, 2 * (j - AHEAD + 1) + 1, it, 4)

                for s in range(AHEAD):
                    a.mark(act.activation(GA[:, s, :], HA[:, s, :], ACT.Gelu), sem("ge_ready"))
                for k in range(STEPS):
                    table_copy(0, k)
                act_high(0)
                for j in range(AHEAD - 1):
                    dense_step(0, j)
                act.wait_ge(sem("al_ready"), s00 + AHEAD)
                for q in range(CHUNKS):
                    j0 = AHEAD - 1 if q == 0 else 0
                    with act.Fori(0, (STEPS - 1 - j0) // 2 - (q == 0)) as it:
                        for j in (j0, j0 + 1):
                            dense_step(q, j, it)
                    for j in range(STEPS - 3 if q == 0 else STEPS - 2, STEPS):
                        dense_step(q, j)
                nxt[0] = d0 + N_DENSE
                act.wait_ge(sem("f_done"), l + 1)
                act.wait_ge(sem("picks_used"), l + 1)
                act.dma_start(X[:], x_scr).then_inc(sem("x_back"), 16)
                act.dma_start(ROWS[:], rows_in[2 * l + 1].partition_broadcast(P)).then_inc(sem("x_back"), 16)
                act.wait_ge(sem("ln_var"), 2 * l + 2)
                rstd(SMALL[:, 60:62], SMALL[:, 56:60].rearrange("p (t k) -> p t k", k=2)[:, :, 1], 1, LN_EPS, sem("ln_rstd"))

        def attention_dve(dve, v, g0, heads, scale, PM=PM, between=lambda n: None):
            def head_max(n):
                g = g0 + n
                c = 16 + 8 * (g % 2)
                dve.wait_ge(sem("sc_done"), g + 1)
                v.step(dve.tensor_reduce(SMALL[:, c:c + 2], M[g % 2][:].rearrange("p (q k) -> p q k", q=2), AX.X, ALU.max))
                v.step(dve.tensor_scalar(SMALL[:, c + 2:c + 4], SMALL[:, c:c + 2], -scale, None, ALU.mult), sem("nb_ready"))

            def head_scale(n):
                g = g0 + n
                c = 16 + 8 * (g % 2)
                dve.wait_ge(sem("exp_ready"), g + 1)
                v.step(dve.reciprocal(SMALL[:, c + 6:c + 8], SMALL[:, c + 4:c + 6]))
                for qt in range(2):
                    ins = dve.tensor_scalar(PM[:, g % 2, qt, :], PM[:, g % 2, qt, :], SMALL[:, c + 6 + qt:c + 7 + qt], None, ALU.mult)
                v.step(ins, sem("sm_ready"))

            head_max(0)
            for n in range(heads):
                if n + 1 < heads:
                    head_max(n + 1)
                head_scale(n)
                between(n)

        @block.vector
        def _(dve):
            v = Steps(dve, sem("dve_step"))
            nxt = [0]

            def lo(i, it=0):
                dve.wait_ge(hi_ready, i + 1 + it * 4)
                dve.tensor_tensor(LO[i % SLOTS][:], RAW[:, i % SLOTS, :], HI[i % SLOTS][:].bitcast(F32), ALU.subtract).then_inc(lo_ready, 1)

            def lo_to(n):
                while nxt[0] < min(n, N_HP):
                    lo(nxt[0])
                    nxt[0] += 1

            def xl_evict(inst, gain=None):
                for kp in range(4):
                    dve.wait_ge(sem("xh_ready"), 4 * inst + kp + 1)
                    hi_ = XH[:, 2 * kp:2 * kp + 2, :].bitcast(F32)
                    if gain is None:
                        ins = dve.tensor_tensor(flat(XL[:, 2 * kp:2 * kp + 2, :]), M[kp][:], flat(hi_), ALU.subtract)
                    else:
                        for j in range(2):
                            ins = dve.scalar_tensor_tensor(out=XL[:, 2 * kp + j, :], in0=M[kp][:, 256 * j:256 * j + 256],
                                                           scalar=gain(2 * kp + j), in1=hi_[:, j, :], op0=ALU.mult, op1=ALU.subtract)
                    v.mark(ins, sem("xl_ready"))

            def norm_rows(dst, inst):
                dve.wait_ge(sem("row_rstd"), inst)
                for tt in range(TT):
                    ins = dve.tensor_scalar(dst[:, tt, :], X[:, tt, :], SMALL[:, 2 + tt:3 + tt], None, ALU.mult)
                v.mark(ins, sem("rows_ready"))

            def residual(h):
                for u in range(4):
                    i = h + u
                    dve.wait_ge(hp_used, i + 1)
                    xv = X[:, :, 256 * u:256 * u + 256]
                    dve.tensor_tensor(xv, xv, PS[i % 4][:].rearrange("p (t n) -> p t n", t=2), ALU.add).then_inc(bank_free[i % 4], 1)
                for u in range(4):
                    evicted(dve, h + u)

            dve.wait_ge(sem("cst_loaded"), 48)
            v.step(dve.tensor_tensor(LBS[:, 8:12], LBS[:, 0:4], LBS[:, 4:8], ALU.max))
            v.step(dve.tensor_tensor(LBS[:, 0:4], LBS[:, 0:4], LBS[:, 8:12], ALU.subtract))
            v.step(dve.tensor_tensor(LBS[:, 4:8], LBS[:, 4:8], LBS[:, 8:12], ALU.subtract), sem("lb_shifted"))
            dve.wait_ge(sem("lb_exp"), 1)
            v.step(dve.tensor_tensor(LBS[:, 8:12], LBS[:, 0:4], LBS[:, 4:8], ALU.add))
            v.step(dve.reciprocal(LBS[:, 8:12], LBS[:, 8:12]))
            v.step(dve.tensor_tensor(LBS[:, 0:4], LBS[:, 0:4], LBS[:, 8:12], ALU.mult))
            v.step(dve.tensor_tensor(LBS[:, 4:8], LBS[:, 4:8], LBS[:, 8:12], ALU.mult))
            v.step(dve.tensor_tensor(LBS[:, 4:8], LBS[:, 4:8], LBS[:, 0:4], ALU.add))
            lb4 = [LB[:, l, :, :, 0].rearrange("p a b -> p a b") for l in range(DEPTH)]
            p4 = [LBS[:, 4 * l:4 * l + 4].rearrange("p (a b) -> p a b", b=2) for l in range(DEPTH)]
            for l in range(DEPTH):
                v.step(dve.tensor_tensor(lb4[l], p4[l], p4[0], ALU.subtract))
                v.step(dve.tensor_scalar(LB[:, l, :, :, 1], lb4[l], -1.0, 1.0, ALU.mult, ALU.add))
            dve.memset(UP[:], 0.0).then_inc(sem("hid_ready"), 2)

            lo_to(2)
            xl_evict(0)
            lo_to(4)
            for l in range(DEPTH):
                h0 = HP_FIRST[l]
                norm_rows(XS, 2 * l + 1)
                xl_evict(1 + 2 * l, lambda k: par(l, "norm_mix", k))
                lo_to(h0 + 7)
                evicted(dve, h0 + 2)
                evicted(dve, h0 + 3)
                v.step(dve.tensor_scalar(flat(E[:]), flat(E[:]), 1.0, None, ALU.add))
                v.step(dve.reciprocal(flat(E[:]), flat(E[:])))
                for d in range(2):
                    for ht in range(2):
                        c = slice(256 * ht, 256 * ht + 256)
                        lb, om = LB[:, l, d, ht, 0:1], LB[:, l, d, ht, 1:2]
                        v.mark(dve.tensor_scalar(F[:, d, c], E[:, d, c], om, lb, ALU.mult, ALU.add))
                        v.step(dve.tensor_scalar(KG[:, d, c], E[:, d, c], -1.0, 1.0, ALU.mult, ALU.add))
                        v.step(dve.tensor_scalar(KG[:, d, c], KG[:, d, c], om, None, ALU.mult))
                lo_to(h0 + 9)
                evicted(dve, h0 + 1)
                dve.wait_ge(sem("vt_ready"), l + 1)
                v.step(dve.memset(ACC[:], 0.0))

                def conv_gate():
                    evicted(dve, h0 + 5)
                    evicted(dve, h0 + 6)
                    v.step(dve.tensor_scalar(EG[:], EG[:], 1.0, None, ALU.add))
                    v.step(dve.reciprocal(EG[:], EG[:]))
                    if l > 0:
                        v.step(dve.memset(UP[:], 0.0))
                    v.step(dve.tensor_tensor(UP[:, :, CONV_PAD:CONV_PAD + TOK], AC[:].rearrange("p (a t) -> p a t", a=2),
                                             EG[:].rearrange("p (a t) -> p a t", a=2), ALU.mult), sem("up_ready"))

                def lag_value(n):
                    d, g = divmod(n, CHUNK)
                    dve.wait_ge(sem("lag_done"), 2 * CHUNK * l + n + 1)
                    here, there = (slice(g, 16), slice(0, 16 - g)) if d == 0 else (slice(0, 16 - g), slice(g, 16))
                    return v.mark(dve.tensor_tensor(v16(TB[:])[:, :, here], v16(M[n % 2][:])[:, :, here], v16(VT[:])[:, :, there], ALU.mult)), here

                def lag_sum(value):
                    count, here = value
                    dve.wait_ge(sem("dve_step"), count)
                    return v.mark(dve.tensor_tensor(v16(ACC[:])[:, :, here], v16(ACC[:])[:, :, here], v16(TB[:])[:, :, here], ALU.add))

                for n in range(2 * CHUNK):
                    d, g = divmod(n, CHUNK)
                    f, k, w = v16(F[:, d, :]), v16(KG[:, d, :]), v16(W[:])
                    if n == 3:
                        conv_gate()
                    lo_to(h0 + (9 if n < 2 else 10 if n < 9 else N_IN + N_OUT))
                    here, there = (slice(g, 16), slice(0, 16 - g)) if d == 0 else (slice(0, 16 - g), slice(g, 16))
                    if n >= 1:
                        dve.wait_ge(sem("lagx_ready"), 2 * CHUNK * l + n)
                    if g == 0:
                        decayed = v.mark(dve.tensor_copy(W[:], Q[:]))
                    else:
                        fs = slice(1, 17 - g) if d == 0 else slice(g - 1, 15)
                        decayed = v.mark(dve.tensor_tensor(w[:, :, here], w[:, :, here], f[:, :, fs], ALU.mult))
                    if n >= 2:
                        dve.wait_ge(sem("dve_step"), summed)
                    if n >= 1:
                        value = lag_value(n - 1)
                    dve.wait_ge(sem("dve_step"), decayed)
                    v.mark(dve.tensor_tensor(v16(XX[:, n % 2, :])[:, :, here], w[:, :, here], k[:, :, there], ALU.mult), sem("lagx_ready"))
                    if n >= 1:
                        summed = lag_sum(value)
                    if g == CHUNK - 1:
                        e = f[:, :, 0:1] if d == 0 else f[:, :, 15:16]
                        v.step(dve.tensor_tensor(v16(QB[:, d, :]), w, e.to_broadcast([P, 32, 16]), ALU.mult))
                value = lag_value(2 * CHUNK - 1)
                dve.wait_ge(sem("dve_step"), summed)
                lag_sum(value)
                dve.wait_ge(sem("diag_used"), 2 * CONV_K * (l + 1))
                for ct in range(2):
                    c = slice(256 * ct, 256 * ct + 256)
                    v.step(dve.tensor_scalar(AC[:, c], M[2][:, c], par(l, "cb", ct), None, ALU.add), sem("cy0_ready"))
                keys_end, decays = [XX[:, 0, :], TB[:]], [SCN, W]
                for d in range(2):
                    f, k, ke, dc = v16(F[:, d, :]), v16(KG[:, d, :]), v16(keys_end[d]), decays[d]
                    keep, edge = ("notlast", "last") if d == 0 else ("notfirst", "first")
                    bc = [P, 32, 16]
                    v.mark(dve.tensor_tensor(v16(E[:, 0, :]), f, cst(keep).unsqueeze(1).to_broadcast(bc), ALU.mult))
                    v.step(dve.tensor_tensor(v16(E[:, 1, :]), f, cst(edge).unsqueeze(1).to_broadcast(bc), ALU.mult))
                    if d == 0:
                        pp = E[:].ap[0]
                        back = [bass.AP(E, 2 * TOK * j + 2 * TOK - 1, [list(pp), [-1, 2 * TOK]]) for j in range(2)]
                        o = bass.AP(dc, 2 * TOK - 1, [list(dc[:].ap[0]), [-1, 2 * TOK]])
                    else:
                        back, o = [E[:, 0, :], E[:, 1, :]], dc[:]
                    v.step(dve.tensor_tensor_scan(o, back[0], back[1], 0.0, ALU.mult, ALU.add))
                    s = v16(dc[:])
                    if d == 0:
                        v.mark(dve.tensor_tensor(ke[:, :, 0:15], k[:, :, 0:15], s[:, :, 1:16], ALU.mult))
                        v.step(dve.tensor_copy(ke[:, :, 15:16], k[:, :, 15:16]), sem("ke_ready"))
                    else:
                        v.mark(dve.tensor_tensor(ke[:, :, 1:16], k[:, :, 1:16], s[:, :, 0:15], ALU.mult))
                        v.step(dve.tensor_copy(ke[:, :, 0:1], k[:, :, 0:1]), sem("ke_ready"))
                for d in range(2):
                    first = 0 if d == 0 else NCH - 1
                    last = [v.mark(dve.memset(ST[d][:, :, first, :], 0.0))] * 2
                    dec = decays[d][:].rearrange("p (h n c) -> p h n c", h=2, c=CHUNK)[:, :, :, 0 if d == 0 else 15]
                    for n, tt in enumerate((0, 1) if d == 0 else (1, 0)):
                        dve.wait_ge(sem("u_done"), 8 * l + 4 * d + 2 * n + 2)
                        for c in range(8) if d == 0 else range(7, -1, -1):
                            ch = 8 * tt + c
                            to = ch + 1 if d == 0 else ch - 1
                            if 0 <= to < NCH:
                                for ht in range(2):
                                    dve.wait_ge(sem("dve_step"), last[ht])
                                    last[ht] = v.mark(dve.scalar_tensor_tensor(
                                        out=ST[d][:, ht, to, :], in0=ST[d][:, ht, ch, :], scalar=dec[:, ht, ch:ch + 1],
                                        in1=UB[d][2 * n + ht][:, 64 * c:64 * c + 64], op0=ALU.mult, op1=ALU.add))
                    dve.wait_ge(sem("dve_step"), last[1])
                    v.step(dve.memset(SMALL[:, 41:42], 0.0), sem("state_ready"))
                for i in (7, 8, 9):
                    evicted(dve, h0 + i)
                v.step(dve.tensor_tensor(flat(QK2[:]), flat(QK[:]), flat(QK[:]), ALU.mult), sem("qsq_ready"))
                dve.wait_ge(sem("csum_done"), l + 1)
                for ct in range(2):
                    c = slice(256 * ct, 256 * ct + 256)
                    v.step(dve.scalar_tensor_tensor(out=W[:, c], in0=PS[1][:, 0:256], scalar=-1.0 / 256, in1=AC[:, c], op0=ALU.mult, op1=ALU.add))
                    v.step(dve.tensor_tensor(EG[:, c], W[:, c], W[:, c], ALU.mult), sem("csq_ready"))
                dve.wait_ge(sem("qrs_ready"), 3 * l + 3)
                v.mark(dve.scalar_tensor_tensor(out=flat(QK2[:, 0:4, :]), in0=flat(QK[:, 0:4, :]), scalar=par(l, "qg"), in1=flat(QK3[:, 0:4, :]),
                                                op0=ALU.mult, op1=ALU.mult))
                v.step(dve.scalar_tensor_tensor(out=QK2[:, 4, :], in0=QK[:, 4, :], scalar=par(l, "kg"), in1=QK3[:, 4, :],
                                                op0=ALU.mult, op1=ALU.mult), sem("qn_ready"))
                v.step(dve.tensor_tensor(QK3[:], QK2[:], cst("cos").unsqueeze(1).to_broadcast([P, 5, TOK]), ALU.mult))
                dve.wait_ge(sem("inter_done"), 2 * l + 2)
                v.step(dve.tensor_tensor(ACC[:], ACC[:], M[0][:], ALU.add))
                v.step(dve.tensor_tensor(XX[:, 0, :], ACC[:], ACC[:], ALU.mult), sem("hsq_ready"))
                for j in range(3):
                    n = 2 if j < 2 else 1
                    dve.wait_ge(sem("rot_done"), 3 * l + j + 1)
                    v.step(dve.tensor_tensor(QK[:, 2 * j:2 * j + n, :], M[1 + j][:, 0:256 * n].rearrange("p (a t) -> p a t", t=TOK),
                                             cst("sin").unsqueeze(1).to_broadcast([P, n, TOK]), ALU.mult))
                v.step(dve.tensor_tensor(flat(QK[:]), flat(QK[:]), flat(QK3[:]), ALU.add), sem("qk_ready"))

                def other_outputs(n):
                    if n == 0:
                        dve.wait_ge(sem("hrs_ready"), l + 1)
                        v.step(dve.tensor_scalar(SCN[:], SCN[:], 1.0, None, ALU.add))
                        v.step(dve.reciprocal(SCN[:], SCN[:]))
                    elif n == 1:
                        v.step(dve.tensor_tensor(SCN[:], SCN[:], GT[:], ALU.mult))
                        for ht in range(2):
                            c = slice(256 * ht, 256 * ht + 256)
                            v.step(dve.scalar_tensor_tensor(out=ACC[:, c], in0=ACC[:, c], scalar=par(l, "ng", ht), in1=TB[:, c],
                                                            op0=ALU.mult, op1=ALU.mult))
                        v.step(dve.tensor_tensor(flat(MIXF[:, 4:6, :]), ACC[:], SCN[:], ALU.mult))
                    elif n == 2:
                        dve.wait_ge(sem("crs_ready"), l + 1)
                        for ct in range(2):
                            c = slice(256 * ct, 256 * ct + 256)
                            v.step(dve.scalar_tensor_tensor(out=W[:, c], in0=W[:, c], scalar=par(l, "lng", ct), in1=XX[:, 1, 0:256],
                                                            op0=ALU.mult, op1=ALU.mult))
                            ins = dve.tensor_scalar(AC[:, c], W[:, c], par(l, "lnb", ct), None, ALU.add)
                            if ct == 0:
                                v.step(ins)
                            else:
                                v.step(ins, sem("cy_ready"))
                    elif n == 4:
                        dve.wait_ge(sem("ceg_ready"), l + 1)
                        v.step(dve.tensor_scalar(EG[:], EG[:], 1.0, None, ALU.add))
                        v.step(dve.reciprocal(EG[:], EG[:]))
                    elif n == 5:
                        v.step(dve.tensor_tensor(flat(MIXF[:, 6:8, :]), AC[:], EG[:], ALU.mult), sem("mix_ready"))

                lo_to(h0 + N_IN + N_OUT)
                attention_dve(dve, v, 8 * l, 8, HEAD ** -0.5, between=other_outputs)
                dve.wait_ge(sem("mixh_ready"), l + 1)
                v.step(dve.tensor_tensor(flat(XL[:]), flat(MIXF[:]), flat(XH[:].bitcast(F32)), ALU.subtract), sem("mixl_ready"))
                residual(h0 + N_IN)
                h1 = h0 + N_IN + N_OUT
                norm_rows(XS2, 2 * l + 2)
                lo_to(h1 + 3)
                xl_evict(2 + 2 * l, lambda k: par(l, "norm_mlp", k))
                with dve.Fori(0, N_UP // 4) as it:
                    for u in range(4):
                        lo(h1 + u + 3, it)
                        dve.wait_ge(bank_free[(h1 + u) % 4], reads_before(h1 + u) + 1 + it)
                        dve.tensor_tensor(SQ[:], RB[:, u % 2, :], RB[:, u % 2, :], ALU.mult).then_inc(sem("hsq2"), 1)
                        dve.wait_ge(sem("hsq2"), 16 * l + u + 1 + it * 4)
                        dve.wait_ge(sem("sq_ready"), 16 * l + u + 1 + it * 4)
                        at_ = bass.ds(it * 8 + 2 * u, 2)
                        dve.tensor_tensor(flat(HL[:, at_, :]), SQ[:], flat(HH[:, at_, :].bitcast(F32)), ALU.subtract)\
                           .then_inc(sem("hid_ready"), 1)
                        dve.wait_ge(sem("hid_ready"), 16 * l + u + 3 + it * 4)
                nxt[0] = h1 + N_UP + 3
                lo_to(h1 + N_UP + N_DOWN + 2)
                residual(h1 + N_UP + N_DOWN - 4)
            def layer_norm(n):
                for tt in range(TT):
                    st = SMALL[:, 4:16].rearrange("p (a b) -> p a b", b=6)
                    for j in range(2):
                        ins = dve.bn_stats(st[:, j, :], X[:, tt, 512 * j:512 * j + 512])
                    v.step(ins)
                    ins = dve.bn_aggr(SMALL[:, 56 + 2 * tt:58 + 2 * tt], st)
                    v.step(ins) if tt == 0 else v.step(ins, sem("ln_var"))
                dve.wait_ge(sem("ln_rstd"), n)
                for tt in range(TT):
                    ins = dve.tensor_scalar(X[:, tt, :], X[:, tt, :], SMALL[:, 56 + 2 * tt:57 + 2 * tt], SMALL[:, 60 + tt:61 + tt],
                                            ALU.subtract, ALU.mult)
                v.step(ins)
                v.step(dve.tensor_tensor(X[:], X[:], ROWS[:, 0, :].unsqueeze(1).to_broadcast([P, TT, D]), ALU.mult))
                v.step(dve.tensor_tensor(X[:], X[:], ROWS[:, 1, :].unsqueeze(1).to_broadcast([P, TT, D]), ALU.add), sem("x_ready"))

            def best16(values, spare, top_, idx, groups):
                for g in range(groups):
                    ins = dve.max(top_(g)[:, 0:8], values(g))
                v.step(ins)
                for g in range(groups):
                    dve.max_index(idx(g)[:, 0:8], top_(g)[:, 0:8], values(g))
                    ins = dve.match_replace(spare(g), top_(g)[:, 0:8], values(g), -3.0e38)
                v.step(ins)
                for g in range(groups):
                    ins = dve.max(top_(g)[:, 8:16], spare(g))
                v.step(ins)
                for g in range(groups):
                    ins = dve.max_index(idx(g)[:, 8:16], top_(g)[:, 8:16], spare(g))
                v.step(ins)

            k96 = slice(0, GLA_K)
            v.mark(dve.memset(SMALL[:, 43:44], 0.0), sem("x_ready"))
            for l in range(DEPTH):
                s0 = HP_SECOND[l]
                lo_to(HP_SHARED + 2 if l > 0 else s0 + 3)
                xl_evict(5 + 2 * l)
                if l == 0:
                    lo_to(s0 + N_MIX2[l])
                    dve.wait_ge(sem("mix_loaded0"), 64)
                    dve.wait_ge(sem("gpre_done"), 1)
                    for h in range(4):
                        ins = dve.tensor_scalar(LG[k96, h, :], M[h // 2][k96, 256 * (h % 2):256 * (h % 2) + 256], P2[k96, h:h + 1], 0.0, ALU.add, ALU.min)
                    v.step(ins, sem("gpre_read"))
                    v.step(dve.tensor_copy(flat(SM[:]).rearrange("p (n c) -> p n c", c=GLA_C), cst("gscan").unsqueeze(1).to_broadcast([P, 16, GLA_C])))
                    dve.wait_ge(sem("lsig_ready"), 1)
                    v.step(dve.tensor_tensor(flat(LG[k96]), flat(LG[k96]), flat(EXA[k96]), ALU.subtract))
                    v.step(dve.tensor_tensor_scan(flat(B[k96]), flat(SM[k96]), flat(LG[k96]), 0.0, ALU.mult, ALU.add))
                    bc = B[k96].rearrange("p h (n c) -> p (h n) c", c=GLA_C)
                    v.step(dve.tensor_tensor(KE[k96].rearrange("p h (n c) -> p (h n) c", c=GLA_C),
                                             bc[:, :, GLA_C - 1].unsqueeze(2).to_broadcast([GLA_K, 16, GLA_C]), bc, ALU.subtract), sem("cum_ready"))
                    dve.wait_ge(sem("gexp_ready"), 1)
                    v.mark(dve.tensor_tensor(flat(KE[k96]), flat(KE[k96]), flat(GK[k96]), ALU.mult))
                    v.mark(dve.tensor_tensor(flat(KTD[k96]), flat(EXB[k96]), flat(GK[k96]), ALU.mult))
                    v.step(dve.scalar_tensor_tensor(out=flat(QTD[k96]), in0=flat(GQ[k96]), scalar=GLA_K ** -0.5, in1=flat(EXA[k96]),
                                                    op0=ALU.mult, op1=ALU.mult), sem("gqk_ready"))
                    dve.wait_ge(sem("gatt_done"), 1)
                    cm = cst("causal").unsqueeze(1).to_broadcast([P, 8, GLA_C])
                    v.step(dve.scalar_tensor_tensor(out=ATT[:], in0=cm, scalar=3.0e38, in1=M[0][:].rearrange("p (a c) -> p a c", c=GLA_C),
                                                    op0=ALU.mult, op1=ALU.min))
                    v.step(dve.scalar_tensor_tensor(out=ATT[:], in0=cm, scalar=-3.0e38, in1=ATT[:], op0=ALU.mult, op1=ALU.max), sem("gattm_ready"))
                    for ch in range(3):
                        dve.wait_ge(sem("uc_done"), ch + 1)
                        for h in range(4):
                            u_ = M[h // 2][k96, GLA_V * (h % 2):GLA_V * (h % 2) + GLA_V]
                            if ch == 0:
                                ins = dve.tensor_copy(STA[k96, h, :], u_)
                            else:
                                ins = dve.scalar_tensor_tensor(out=STA[k96, h, :], in0=STA[k96, h, :], scalar=BL[k96, 4 * h + ch:4 * h + ch + 1],
                                                               in1=u_, op0=ALU.mult, op1=ALU.add)
                        v.step(ins, sem("sta_ready"))
                    dve.wait_ge(sem("rexp_ready"), 1)
                    v.step(dve.tensor_scalar(flat(RG[:]), flat(RG[:]), 1.0, None, ALU.add))
                    v.step(dve.reciprocal(flat(RG[:]), flat(RG[:])))
                    v.step(dve.tensor_tensor(flat(RG[:]), flat(RG[:]), flat(GR[:]), ALU.mult))
                    dve.wait_ge(sem("go_ready"), 4)
                    v.step(dve.tensor_tensor(flat(GO2[:]), flat(GO[:]), flat(GO[:]), ALU.mult))
                    v.step(dve.tensor_reduce(SMALL[:, 48:56], GO2[:].rearrange("p t (h c) -> p (t h) c", h=4), AX.X, ALU.add), sem("gss_ready"))
                    dve.wait_ge(sem("grs_ready"), 1)
                    v.step(dve.tensor_tensor(flat(GO[:]), flat(GO[:]), flat(RG[:]), ALU.mult))
                    go = GO[:].rearrange("p t (h c) -> p (t h) c", h=4)
                    v.step(dve.tensor_tensor(go, go, SMALL[:, 48:56].unsqueeze(2).to_broadcast([P, 8, GLA_V]), ALU.mult), sem("gon_ready"))
                else:
                    lo_to(s0 + N_MIX2[l])
                    dve.wait_ge(sem("mix_loaded1"), 48)

                    def slot_max(n):
                        dve.wait_ge(sem("dsc_done"), n + 1)
                        b2 = [M[0], M[1]] if n % 2 == 0 else [PS[0], PS[1]]
                        c = 48 + 2 * (n % 2)
                        for g in range(2):
                            w = slice(0, 512) if g == 0 else slice(512, 768)
                            ins = dve.tensor_tensor(S3[:, n % 2, w], b2[g][:, 0:w.stop - w.start], DM[:, n % 2, w], ALU.add)
                        v.step(ins, sem("dsc_read"))
                        v.step(dve.tensor_reduce(SMALL[:, 52:53], S3[:, n % 2, :], AX.X, ALU.max))
                        v.step(dve.tensor_scalar(SMALL[:, c:c + 1], SMALL[:, 52:53], -KEYS ** -0.5, None, ALU.mult), sem("dnb_ready"))

                    def slot_sum(n):
                        dve.wait_ge(sem("dexp_ready"), n + 1)
                        if n >= 4 and n % 2 == 0:
                            dve.wait_ge(sem("dpt_done"), n // 2 - 1)
                        c = 49 + 2 * (n % 2)
                        o = PD[:, (n // 2) % 2, n % 2, :]
                        v.mark(dve.reciprocal(SMALL[:, 53:54], SMALL[:, c:c + 1]))
                        v.step(dve.tensor_tensor(S3[:, n % 2, 0:256], S3[:, n % 2, 0:256], S3[:, n % 2, 256:512], ALU.add))
                        v.step(dve.tensor_tensor(S3[:, n % 2, 0:256], S3[:, n % 2, 0:256], S3[:, n % 2, 512:768], ALU.add))
                        v.step(dve.tensor_scalar(o, S3[:, n % 2, 0:256], SMALL[:, 53:54], None, ALU.mult), sem("dsm_ready"))

                    slot_max(0)
                    for n in range(2 * SLOT_H):
                        if n + 1 < 2 * SLOT_H:
                            slot_max(n + 1)
                        slot_sum(n)
                lo_to(s0 + N_MIX2[l] + 3)
                attention_dve(dve, v, 16 + 4 * l, 4, HEAD ** -0.5, PM2)
                dve.wait_ge(sem("mix2h_ready"), l + 1)
                v.step(dve.tensor_tensor(flat(XL[:]), flat(MIX2[:]), flat(XH[:].bitcast(F32)), ALU.subtract), sem("mix2l_ready"))
                w0 = s0 + N_MIX2[l] + N_OUT
                lo_to(w0)
                for u in range(4):
                    i = s0 + N_MIX2[l] + u
                    dve.wait_ge(hp_used, i + 1)
                    xv = X[:, :, 256 * u:256 * u + 256]
                    dve.scalar_tensor_tensor(out=xv, in0=xv, scalar=DN_ALPHA, in1=PS[i % 4][:].rearrange("p (t n) -> p t n", t=2),
                                             op0=ALU.mult, op1=ALU.add).then_inc(bank_free[i % 4], 1)
                for u in range(4):
                    evicted(dve, s0 + N_MIX2[l] + u)
                layer_norm(2 * l + 1)
                lo_to(w0 + 3)
                xl_evict(6 + 2 * l)
                d0 = w0 + N_WQ
                for h in range(PH):
                    lo_to(min(w0 + h + 6, d0))
                    dve.wait_ge(sem("keysc_ready"), PH * l + h + 1)
                    sc, ts, ti, s2 = (t[:, :, 2 * h:2 * h + 2, :] for t in (SC, TS, TI, S2))
                    best16(lambda g: sc[:, g // 2, g % 2, :], lambda g: s2[:, g // 2, g % 2, :],
                           lambda g: ts[:, g // 2, g % 2, :], lambda g: ti[:, g // 2, g % 2, :], 4)
                v.mark(dve.tensor_copy(TF[:].rearrange("p a b c -> p (a b c)"), TI[:].rearrange("p a b c -> p (a b c)")))
                bc4 = [P, PH, TOPK, TOPK]
                for tt in range(TT):
                    two = TS[:, tt].rearrange("p (h s) k -> p h s k", s=2)
                    ins = dve.tensor_tensor(CD[:, tt].rearrange("p h (i j) -> p h i j", j=TOPK), two[:, :, 0, :].unsqueeze(3).to_broadcast(bc4),
                                            two[:, :, 1, :].unsqueeze(2).to_broadcast(bc4), ALU.add)
                v.step(ins)
                for tt in range(TT):
                    best16(lambda g: CD[:, tt, g, :], lambda g: CD2[:, g, :], lambda g: BS[:, PH * tt + g, :], lambda g: BJ[:, tt, g, :], PH)
                v.step(dve.tensor_tensor(GX[:], BS[:], BS[:, :, 0:1].to_broadcast([P, TT * PH, TOPK]), ALU.subtract), sem("gx_shifted"))
                bj = BJ[:].rearrange("p a b c -> p (a b c)")
                v.mark(dve.tensor_scalar(BK[:, 0, :], bj, 4, None, ALU.logical_shift_right))
                v.step(dve.tensor_scalar(BK[:, 1, :], bj, TOPK - 1, None, ALU.bitwise_and))
                v.step(dve.tensor_copy(JF[:].rearrange("p s a b c -> p (s a b c)"), flat(BK[:])))
                for side in range(2):
                    for tt in range(TT):
                        v.step(dve.tensor_tensor(EQ[:], cst("iota")[:, 0:TOPK].unsqueeze(1).unsqueeze(1).to_broadcast(bc4),
                                                 JF[:, side, tt].unsqueeze(3).to_broadcast(bc4), ALU.is_equal))
                        v.step(dve.tensor_tensor(EQ[:], EQ[:], TF[:, tt].rearrange("p (h s) k -> p h s k", s=2)[:, :, side, :].unsqueeze(2).to_broadcast(bc4), ALU.mult))
                        v.step(dve.tensor_reduce(SEL[:, side, tt, :].rearrange("p (h k) -> p h k", k=TOPK), EQ[:], AX.X, ALU.add))
                dve.wait_ge(sem("gx_ready"), l + 1)
                v.step(dve.tensor_reduce(GSUM[:], GX[:], AX.X, ALU.add))
                v.step(dve.reciprocal(GSUM[:], GSUM[:]))
                v.step(dve.tensor_tensor(SEL[:, 2].rearrange("p t (h k) -> p (t h) k", k=TOPK), GX[:],
                                         GSUM[:].unsqueeze(2).to_broadcast([P, TT * PH, TOPK]), ALU.mult), sem("sel_ready"))
                if l == 0:
                    v.step(dve.tensor_copy(IOT[:], cst("iota").unsqueeze(2).to_broadcast([P, KEYS, TPS])))
                dve.wait_ge(sem("pf_ready"), l + 1)
                for c in range(3):
                    v.step(dve.tensor_copy(GS[:, c, :], PF[:]))
                    if c < 2:
                        v.step(dve.tensor_tensor(PF[:], PF[:], GS[:, c, :], ALU.subtract))

                dve.wait_ge(lo_ready, d0 + AHEAD)
                nxt[0] = d0 + AHEAD
                lo_to(d0 + AHEAD + 3)

                t0, s00 = (CHUNKS * STEPS) * l, PAIRS * l

                def one_hots(q, k, it=0, per=2):
                    n = t0 + STEPS * q + k
                    spare = q == 0 and k % 2 == 0
                    if n > t0 + 1:
                        dve.wait_ge(sem("table_done"), (n - 1 if q == 0 else n) + it * per)
                    oa, ob = (OA2, OB2) if spare else (OA, OB)
                    t = bass.ds(it * (per * TPS) + TPS * k, TPS)
                    dve.tensor_tensor(EQB[:], IOT[:, BC * q:BC * q + BC, :], PB[:, 1, t].unsqueeze(1).to_broadcast([P, BC, TPS]),
                                      ALU.is_equal).then_inc(sem("eqb_ready"), 1)
                    dve.tensor_tensor(oa[:], IOT[:], PB[:, 0, t].unsqueeze(1).to_broadcast([P, KEYS, TPS]),
                                      ALU.is_equal).then_inc(sem("oa_ready"), 1)
                    dve.wait_ge(sem("eqb_ready"), n + 1 + it * per)
                    dve.tensor_tensor(ob[:], EQB[:].unsqueeze(1).to_broadcast([P, 3, BC, TPS]),
                                      GS[:, :, t].unsqueeze(2).to_broadcast([P, 3, BC, TPS]), ALU.mult).then_inc(sem("ob_ready"), 1)
                    dve.wait_ge(sem("ob_ready"), n + 1 + it * per)

                def product(s, q, k, it=0):
                    dve.wait_ge(sem("ge_ready"), s00 + s + 1 + it * 2)
                    if isinstance(it, int):
                        dve.wait_ge(sem("table_ready"), t0 + STEPS * (q + 1))
                    ge = GA[:, s, :] if s < AHEAD else GE[:, s % 2, :]
                    dve.tensor_tensor(ge, ge, flat(G[q % 2][:, bass.ds(it * 4 + 2 * k, 2), :]), ALU.mult).then_inc(sem("a_ready"), 1)
                    dve.wait_ge(sem("ah_ready"), s00 + s + 1 + it * 2)
                    dve.wait_ge(sem("a_ready"), s00 + s + 1 + it * 2)
                    dve.tensor_tensor(AL[s % 2][:], ge, AH[s % 2][:].bitcast(F32), ALU.subtract).then_inc(sem("al_ready"), 1)

                def dense_step(q, j, it=0):
                    s = STEPS * q + j
                    if s < AHEAD - 2:
                        lo(d0 + AHEAD + 3 + s)
                    elif s >= AHEAD - 1:
                        for n in (3, 4):
                            if 2 * s + n < N_DENSE:
                                lo(d0 + 2 * s + n, it)
                    if s + 1 < PAIRS:
                        product(s + 1, q + (j + 1) // STEPS, (j + 1) % STEPS, it)
                    if q == 0:
                        if AHEAD - 1 <= j < STEPS - 1:
                            for k in (2 * (j - AHEAD + 1) + 1, 2 * (j - AHEAD + 1) + 2):
                                one_hots(1 + k // STEPS, k % STEPS, it, 4)
                    else:
                        nq = q + 1 + (j + 1) // STEPS
                        if nq < CHUNKS:
                            one_hots(nq, (j + 1) % STEPS, it)

                for k in range(STEPS + 1):
                    if k == 1:
                        dve.wait_ge(sem("ge_ready"), s00 + AHEAD)
                    one_hots(k // STEPS, k % STEPS)
                product(0, 0, 0)
                for j in range(AHEAD - 1):
                    dense_step(0, j)
                for q in range(CHUNKS):
                    j0 = AHEAD - 1 if q == 0 else 0
                    with dve.Fori(0, (STEPS - 1 - j0) // 2 - (q == 0)) as it:
                        for j in (j0, j0 + 1):
                            dense_step(q, j, it)
                    for j in range(STEPS - 3 if q == 0 else STEPS - 2, STEPS):
                        dense_step(q, j)
                nxt[0] = d0 + N_DENSE
                dve.wait_ge(sem("al_ready"), PAIRS * (l + 1))
                v.mark(dve.memset(SMALL[:, 44:45], 0.0), sem("picks_used"))
                dve.wait_ge(sem("f_done"), l + 1)
                dve.wait_ge(sem("x_back"), 32 * (l + 1))
                for tt in range(TT):
                    for n in range(2):
                        xv = X[:, tt, 512 * n:512 * n + 512]
                        ins = dve.scalar_tensor_tensor(out=xv, in0=xv, scalar=DN_ALPHA, in1=M[2 * tt + n][:], op0=ALU.mult, op1=ALU.add)
                v.step(ins)
                layer_norm(2 * l + 2)
            v.step(dve.memset(SMALL[:, 45:46], 0.0), sem("x_final"))

        @block.gpsimd
        def _(pool):
            p = Steps(pool, sem("pool_step"))
            pool.wait_ge(sem("cst_loaded"), 48)
            for l in range(DEPTH):
                h0 = HP_FIRST[l]
                evicted(pool, h0)
                pool.wait_ge(sem("t_done"), 4 * (2 * l + 2))
                for tt in range(TT):
                    for h in range(4):
                        ins = pool.tensor_tensor(VX[:, tt, h, :, :], VR[:, tt, 64 * h:64 * h + 64].unsqueeze(1).to_broadcast([P, 8, HEAD]),
                                                 cst("chunkmask").unsqueeze(2).to_broadcast([P, 8, HEAD]), ALU.mult)
                p.mark(ins, sem("vx_ready"))
            for l in range(DEPTH):
                d0 = HP_DENSE[l]
                pool.wait_ge(lo_ready, d0)
                for i in range(d0, d0 + AHEAD):
                    pool.wait_ge(hi_ready, i + 1)
                    pool.tensor_tensor(LO[i % SLOTS][:], RAW[:, i % SLOTS, :], HI[i % SLOTS][:].bitcast(F32), ALU.subtract).then_inc(lo_ready, 1)

        @block.tensor
        def _(pe):
            def transposes(inst, src, ready):
                ready()
                for kp in range(4):
                    for j in range(2):
                        for tt in range(TT):
                            k = 2 * kp + j
                            ins = pe.transpose(M[kp][:, 256 * j + P * tt:256 * j + P * tt + P], src[:, tt, P * k:P * k + P], cst("ident"))
                    ins.then_inc(sem("t_done"), 1)

            def three(out_, ah, al, bh, bl, first, last, **kw):
                pe.matmul(out_, ah, bh, start=first, stop=False, **kw)
                pe.matmul(out_, ah, bl, start=False, stop=False, **kw)
                return pe.matmul(out_, al, bh, start=False, stop=last, **kw)

            def hp_wait(i, it=0, bank=True):
                pe.wait_ge(lo_ready, i + 1 + it * 4)
                if bank and reads_before(i) > 0:
                    pe.wait_ge(bank_free[i % 4], reads_before(i) + it)

            def half(i, modes, it=0, hh=XH, hl=XL, k0=0, first=True, last=True, between=lambda c: None):
                hp_wait(i, it, first)
                s, b = i % SLOTS, PS[i % 4]
                wh, wl = (t[s][:].rearrange("p (k n) -> p k n", k=KT) for t in (HI, LO))
                if modes == "rr":
                    for tt in range(TT):
                        for k in range(KT):
                            ins = three(b[:, 256 * tt:256 * tt + 256], hh[:, k0 + k, P * tt:P * tt + P], hl[:, k0 + k, P * tt:P * tt + P],
                                        wh[:, k, :], wl[:, k, :], first and k == 0 and (last or tt == 0), last and k == KT - 1, skip_group_check=not (first and last))
                else:
                    for c, mode in enumerate(modes):
                        if c == 1:
                            between(0)
                        n = slice(P * c, P * c + P)
                        if mode == "c":
                            for k in range(KT):
                                ins = three(b[:, 256 * c:256 * c + 256], wh[:, k, n], wl[:, k, n], hh[:, k, :], hl[:, k, :], k == 0, k == KT - 1)
                        else:
                            for tt in range(TT):
                                for k in range(KT):
                                    ins = three(b[:, 256 * c + P * tt:256 * c + P * tt + P], hh[:, k, P * tt:P * tt + P], hl[:, k, P * tt:P * tt + P],
                                                wh[:, k, n], wl[:, k, n], k == 0, k == KT - 1)
                ins.then_inc(hp_used, 1)
                between(1)

            def attention_pe(g0, heads, q, k, val, part, PM=PM, PT=PT):
                def scores(n):
                    g = g0 + n
                    if n >= 2:
                        pe.wait_ge(sem("exp_ready"), g - 1)
                    for qt in range(2):
                        ins = pe.matmul(M[g % 2][:, 256 * qt:256 * qt + 256], q(n)[:, P * qt:P * qt + P], k(n), start=True, stop=True)
                    ins.then_inc(sem("sc_done"), 1)

                scores(0)
                scores(1)
                for n in range(heads):
                    g = g0 + n
                    pe.wait_ge(sem("sm_ready"), g + 1)
                    if n >= 1:
                        pe.wait_ge(sem("pt_ready"), g)
                    for kt in range(2):
                        for qt in range(2):
                            ins = pe.transpose(M[2][:, 256 * kt + P * qt:256 * kt + P * qt + P], PM[:, g % 2, qt, P * kt:P * kt + P], cst("ident"))
                    ins.then_inc(sem("pt_done"), 1)
                    if n + 2 < heads:
                        scores(n + 2)
                    pe.wait_ge(sem("pt_ready"), g + 1)
                    if n >= 1:
                        pe.wait_ge(sem("o_ready"), g)
                    o = part(n)
                    for kt in range(2):
                        ins = pe.matmul(M[3][o:o + 64, 0:256], val(n, kt), PT[:, g % 2, kt, :], start=(kt == 0), stop=(kt == 1))
                    ins.then_inc(sem("pv_done"), 1)

            pe.wait_ge(sem("cst_loaded"), 48)
            transposes(0, X, lambda: pe.wait_ge(sem("mem_loaded"), 16))
            pe.wait_ge(sem("xl_ready"), 4)
            for i in range(N_MEM):
                half(i, "cc" if i % 2 == 0 else "rr")
            for l in range(DEPTH):
                h0 = HP_FIRST[l]
                transposes(1 + 2 * l, XS, lambda: pe.wait_ge(sem("rows_ready"), 2 * l + 1))
                pe.wait_ge(sem("xl_ready"), 4 * (2 * l + 2))
                def lag(n):
                    d, g = divmod(n, CHUNK)
                    here = slice(g, 16) if d == 0 else slice(0, 16 - g)
                    pe.wait_ge(sem("lagx_ready"), 2 * CHUNK * l + n + 1)
                    pe.matmul(v16(M[n % 2][:])[:, :, here], cst("blk"), v16(XX[:, n % 2, :])[:, :, here], start=True, stop=True)\
                      .then_inc(sem("lag_done"), 1)

                def tap(n):
                    ct, k = divmod(n, CONV_K)
                    pe.wait_ge(sem("diag_ready"), 2 * CONV_K * l + n + 1)
                    pe.matmul(M[2][:, 256 * ct:256 * ct + 256], DG[:, n % 4, :], UP[:, ct, k:k + TOK], start=(k == 0), stop=(k == CONV_K - 1))\
                      .then_inc(sem("diag_used"), 1)

                for u in range(4):
                    half(h0 + u, "rr" if u == 0 else "cc")
                evicted(pe, h0)
                for ht in range(2):
                    for tt in range(TT):
                        ins = pe.transpose(M[0][:, 256 * ht + P * tt:256 * ht + P * tt + P], VR[:, tt, P * ht:P * ht + P], cst("ident"))
                ins.then_inc(sem("vt_done"), 1)
                half(h0 + 4, "cc")
                half(h0 + 5, "cc")
                pe.wait_ge(sem("vt_ready"), l + 1)
                for u in range(6, N_IN):
                    half(h0 + u, "cr" if u == 7 else "cc", between=lambda c: lag(2 * (u - 6) + c))
                pe.wait_ge(sem("up_ready"), l + 1)
                for n in range(2 * (N_IN - 6), 2 * CHUNK):
                    lag(n)
                    taps, lags = 2 * CONV_K, 2 * CHUNK - 2 * (N_IN - 6)
                    first = n - 2 * (N_IN - 6)
                    for m in range(taps * first // lags, taps * (first + 1) // lags):
                        tap(m)
                started = set()
                pe.wait_ge(sem("cy0_ready"), 2 * (l + 1))
                for d, ke in enumerate((XX[:, 0, :], TB[:])):
                    pe.wait_ge(sem("ke_ready"), 2 * l + d + 1)
                    for tt in range(TT):
                        for ht in range(2):
                            ins = pe.transpose(M[2 - d][:, 256 * tt + P * ht:256 * tt + P * ht + P], ke[:, 256 * ht + P * tt:256 * ht + P * tt + P], cst("ident"))
                    ins.then_inc(sem("kt_done"), 1)
                for u in range(N_IN - 4, N_IN):
                    evicted(pe, h0 + u)
                pe.wait_ge(sem("vx_ready"), l + 1)

                def keys_values(d, n):
                    tt, ht = (n // 2 if d == 0 else 1 - n // 2), n % 2
                    for j in range(2):
                        c = 256 * tt + P * ht + 64 * j
                        ins = pe.matmul(UB[d][n][64 * j:64 * j + 64, :], XX[:, 1 - d, c:c + 64],
                                        VX[:, tt, 2 * ht + j, :, :].rearrange("p a b -> p (a b)"), start=True, stop=True)
                    ins.then_inc(sem("u_done"), 1)

                def from_states(d):
                    pe.wait_ge(sem("state_ready"), 2 * l + d + 1)
                    for ht in range(2):
                        for ch in range(NCH):
                            for j in range(2):
                                o = slice(64 * j, 64 * j + 64)
                                c = 256 * ht + CHUNK * ch
                                ins = pe.matmul(M[0][o, c:c + CHUNK], ST[d][o, ht, ch, :], QB[o, d, c:c + CHUNK],
                                                start=j not in started, stop=(d == 1), skip_group_check=True)
                                started.add(j)
                    ins.then_inc(sem("inter_done"), 1)

                def over_channels(ready, src, c0, done):
                    pe.wait_ge(sem(ready), 2 * (l + 1))
                    for ct in range(2):
                        ins = pe.matmul(PS[1][:, c0:c0 + 256], cst("ones"), src[:, 256 * ct:256 * ct + 256], start=(ct == 0), stop=(ct == 1))
                    ins.then_inc(sem(done), 1)

                def over_heads(ready, lhs, done):
                    pe.wait_ge(sem(ready), l + 1)
                    for j in range(3):
                        n = 512 if j < 2 else 256
                        pe.matmul(M[1 + j][:, 0:n], cst(lhs), flat(QK2[:])[:, 512 * j:512 * j + n], start=True, stop=True).then_inc(sem(done), 1)

                pe.wait_ge(sem("kr_ready"), 2 * l + 1)
                for n in range(4):
                    keys_values(0, n)
                pe.wait_ge(sem("kr_ready"), 2 * l + 2)
                for n in range(3):
                    keys_values(1, n)
                pe.wait_ge(sem("state_ready"), 2 * l + 1)
                keys_values(1, 3)
                over_channels("cy0_ready", AC, 0, "csum_done")
                from_states(0)
                over_heads("qsq_ready", "blk", "qss_done")
                over_channels("csq_ready", EG, 256, "cvar_done")
                from_states(1)
                over_heads("qn_ready", "rot", "rot_done")
                pe.wait_ge(sem("hsq_ready"), l + 1)
                pe.matmul(PS[2][:], cst("blk"), XX[:, 0, :], start=True, stop=True).then_inc(sem("hss_done"), 1)
                pe.wait_ge(sem("qk_ready"), l + 1)
                attention_pe(8 * l, 8, lambda n: QK[64 * (n // 4):64 * (n // 4) + 64, n % 4, :],
                             lambda n: QK[64 * (n // 4):64 * (n // 4) + 64, 4, :],
                             lambda n, kt: VA[:, kt, 64 * (n // 4):64 * (n // 4) + 64], lambda n: 64 * (n // 4))
                pe.wait_ge(sem("mixl_ready"), l + 1)
                for u in range(N_OUT):
                    half(h0 + N_IN + u, "rr")
                h1 = h0 + N_IN + N_OUT
                transposes(2 + 2 * l, XS2, lambda: pe.wait_ge(sem("rows_ready"), 2 * l + 2))
                pe.wait_ge(sem("xl_ready"), 4 * (2 * l + 3))
                with pe.Fori(0, N_UP // 4) as it:
                    for u in range(4):
                        half(h1 + u, "cc", it)
                h2 = h1 + N_UP
                pe.wait_ge(sem("hid_ready"), 16 * (l + 1) + 2)
                for u in range(N_DOWN):
                    half(h2 + u, "rr", 0, HH, HL, 8 * (u // 4), u < 4, u >= N_DOWN - 4)
            k96 = slice(0, GLA_K)
            for l in range(DEPTH):
                s0 = HP_SECOND[l]
                transposes(5 + 2 * l, X, lambda: pe.wait_ge(sem("x_ready"), 2 * l + 1))
                pe.wait_ge(sem("xl_ready"), 4 * (6 + 2 * l))
                if l > 0:
                    for u in range(N_SHARED):
                        half(HP_SHARED + u, "cc" if u < 3 else "rr")
                for u in range(N_MIX2[l]):
                    half(s0 + u, "rr" if l == 0 and u >= 5 else "cc")
                for u in range(4):
                    evicted(pe, s0 + N_MIX2[l] - 4 + u)
                pe.wait_ge(sem(f"mix_loaded{l}"), 64 if l == 0 else 48)
                if l == 0:
                    for h in range(4):
                        ins = pe.matmul(M[h // 2][k96, 256 * (h % 2):256 * (h % 2) + 256], WG2[96:112, GLA_K * h:GLA_K * h + GLA_K],
                                        GQ[96:112, 0, :], start=True, stop=True, tile_position=(96, 0))
                    ins.then_inc(sem("gpre_done"), 1)
                    pe.wait_ge(sem("gqk_ready"), 1)
                    for tt in range(TT):
                        for h in range(4):
                            ins = pe.transpose(M[2 + tt][:, GLA_K * h:GLA_K * h + GLA_K], KE[k96, h, P * tt:P * tt + P], cst("ident")[k96, k96])
                    ins.then_inc(sem("ket_done"), 1)
                    for h in range(4):
                        for ch in range(4):
                            c = slice(GLA_C * ch, GLA_C * ch + GLA_C)
                            a_ = GLA_C * (2 * h + ch // 2)
                            ins = pe.matmul(M[0][64 * (ch % 2):64 * (ch % 2) + 64, a_:a_ + GLA_C], KTD[k96, h, c], QTD[k96, h, c], start=True, stop=True)
                    ins.then_inc(sem("gatt_done"), 1)
                    pe.wait_ge(sem("gattm_ready"), 1)
                    pe.wait_ge(sem("ker_ready"), 1)
                    for ch in range(4):
                        r, tt = slice(64 * (ch % 2), 64 * (ch % 2) + 64), ch // 2
                        if ch >= 1:
                            pe.wait_ge(sem("sta_ready"), ch)
                            pe.wait_ge(sem("go_ready"), ch)
                        for h in range(4):
                            o = M[2 + h // 2][r, GLA_V * (h % 2):GLA_V * (h % 2) + GLA_V]
                            ins = pe.matmul(o, ATT[r, 2 * h + tt, :], GV[r, tt, GLA_V * h:GLA_V * h + GLA_V], start=True, stop=(ch == 0))
                            if ch > 0:
                                ins = pe.matmul(o, QTD[k96, h, GLA_C * ch:GLA_C * ch + GLA_C], STA[k96, h, :], start=False, stop=True)
                        ins.then_inc(sem("oc_done"), 1)
                        if ch < 3:
                            for h in range(4):
                                ins = pe.matmul(M[h // 2][k96, GLA_V * (h % 2):GLA_V * (h % 2) + GLA_V], KER[r, tt, GLA_K * h:GLA_K * h + GLA_K],
                                                GV[r, tt, GLA_V * h:GLA_V * h + GLA_V], start=True, stop=True)
                            ins.then_inc(sem("uc_done"), 1)
                    pe.wait_ge(sem("gon_ready"), 1)
                    for kt in range(6):
                        for tt in range(TT):
                            c = 256 * (kt % 2) + P * tt
                            ins = pe.transpose(M[kt // 2][:, c:c + P], GO[:, tt, P * kt:P * kt + P], cst("ident"))
                    ins.then_inc(sem("got_done"), 1)
                    pe.wait_ge(sem("glamix_ready"), 1)
                else:
                    def slot_scores(n):
                        if n >= 2:
                            pe.wait_ge(sem("dsc_read"), n - 1)
                        sl, qt = divmod(n, 2)
                        b2 = [M[0], M[1]] if n % 2 == 0 else [PS[0], PS[1]]
                        for g in range(GROUPS):
                            ins = pe.matmul(b2[g // 2][:, 256 * (g % 2):256 * (g % 2) + 256], QD[:, SLOT_H * g + sl, P * qt:P * qt + P],
                                            KD[:, sl, :], start=True, stop=True)
                        ins.then_inc(sem("dsc_done"), 1)

                    slot_scores(0)
                    slot_scores(1)
                    for sl in range(SLOT_H):
                        if sl + 1 < SLOT_H:
                            slot_scores(2 * sl + 2)
                            slot_scores(2 * sl + 3)
                        pe.wait_ge(sem("dsm_ready"), 2 * sl + 2)
                        if sl >= 1:
                            pe.wait_ge(sem("dpt_ready"), sl)
                        for kt in range(2):
                            for qt in range(2):
                                ins = pe.transpose(M[2][:, 256 * kt + P * qt:256 * kt + P * qt + P], PD[:, sl % 2, qt, P * kt:P * kt + P], cst("ident"))
                        ins.then_inc(sem("dpt_done"), 1)
                        pe.wait_ge(sem("dpt_ready"), sl + 1)
                        if sl >= 1:
                            pe.wait_ge(sem("do_ready"), sl)
                        for kt in range(2):
                            ins = pe.matmul(M[3][:, 0:256], VD[:, kt, P * sl:P * sl + P], PTD[:, kt, :], start=(kt == 0), stop=(kt == 1))
                        ins.then_inc(sem("dpv_done"), 1)
                    pe.wait_ge(sem("do_ready"), SLOT_H)
                    pe.wait_ge(sem("dsc_read"), 2 * SLOT_H)
                attention_pe(16 + 4 * l, 4, lambda n: QM[64 * (n % 2):64 * (n % 2) + 64, n // 2, :],
                             lambda n: KVL[64 * (n % 2):64 * (n % 2) + 64, 256 * (n // 2):256 * (n // 2) + 256],
                             lambda n, kt: KVL[:, 512 + 256 * kt + 64 * n:512 + 256 * kt + 64 * n + 64], lambda n: 64 * (n % 2), PM2, PT2)
                pe.wait_ge(sem("mix2l_ready"), l + 1)
                for u in range(N_OUT):
                    half(s0 + N_MIX2[l] + u, "rr")
                w0 = s0 + N_MIX2[l] + N_OUT
                transposes(6 + 2 * l, X, lambda: pe.wait_ge(sem("x_ready"), 2 * l + 2))
                pe.wait_ge(sem("xl_ready"), 4 * (7 + 2 * l))
                def head_scores(h):
                    evicted(pe, w0 + h)
                    if h >= 4:
                        pe.wait_ge(sem("keysc_ready"), PH * l + h - 3)
                    for tt in range(TT):
                        for side in range(2):
                            c = 256 * tt + P * side
                            ins = pe.matmul(M[h % 4][:, c:c + P], QP[:, 2 * h + side, P * tt:P * tt + P], SK[:, side, :], start=True, stop=True)
                    ins.then_inc(sem("keysc_done"), 1)

                pe.wait_ge(sem("keys_loaded"), 16 * (l + 1))
                for u in range(N_WQ):
                    half(w0 + u, "cc")
                    if u >= 1:
                        head_scores(u - 1)
                head_scores(PH - 1)
                d0 = w0 + N_WQ
                t0, s00 = (CHUNKS * STEPS) * l, PAIRS * l

                def expert_in(s, it=0):
                    i = d0 + u_at(s)
                    pe.wait_ge(lo_ready, i + 1 + it * 4)
                    if 2 <= s < AHEAD:
                        pe.wait_ge(sem("ahead_copied"), AHEAD * l + s - 1)
                    elif s >= AHEAD:
                        pe.wait_ge(sem("ge_ready"), s00 + s - 1 + it * 2)
                    wh, wl = (t[i % SLOTS][:].rearrange("p (k n) -> p k n", k=KT) for t in (HI, LO))
                    for c in range(2):
                        n = slice(P * c, P * c + P)
                        for k in range(KT):
                            ins = three(PS[s % 2][:, 256 * c:256 * c + 256], wh[:, k, n], wl[:, k, n], XH[:, k, :], XL[:, k, :], k == 0, k == KT - 1)
                    ins.then_inc(hp_used, 1)

                for s in range(AHEAD):
                    expert_in(s)
                pe.wait_ge(sem("keysc_ready"), 8 * l + 8)
                pe.wait_ge(sem("sel_ready"), l + 1)
                for c in range(3):
                    for tt in range(TT):
                        ins = pe.transpose(M[c // 2][:, 256 * (c % 2) + P * tt:256 * (c % 2) + P * tt + P], SEL[:, c, tt, :], cst("ident"))
                ins.then_inc(sem("selt_done"), 1)
                pe.wait_ge(sem("pf_ready"), l + 1)
                for n in range(4):
                    for j in range(4):
                        pe.matmul(M[n][:, P * j:P * j + P], cst("zero"), cst("zero"), start=(j == 0), stop=False, skip_group_check=True)
                def table(q, k, it=0, per=2):
                    n = t0 + STEPS * q + k
                    pe.wait_ge(sem("oa_ready"), n + 1 + it * per)
                    pe.wait_ge(sem("ob_ready"), n + 1 + it * per)
                    if n >= 2:
                        pe.wait_ge(sem("table_ready"), n - 1 + it * per)
                    oa, ob = (OA2, OB2) if q == 0 and k % 2 == 0 else (OA, OB)
                    for t in range(TPS):
                        for c in range(3):
                            ins = pe.matmul(PS[2 + k % 2][:, BC * t:BC * t + BC], oa[:, :, t], ob[:, c, :, t], start=(c == 0), stop=(c == 2))
                    ins.then_inc(sem("table_done"), 1)

                def expert_out(s, it=0):
                    i = d0 + v_at(s)
                    pe.wait_ge(lo_ready, i + 1 + it * 4)
                    pe.wait_ge(sem("al_ready"), s00 + s + 1 + it * 2)
                    vh, vl = (t[i % SLOTS][:].rearrange("p (b n) -> p b n", b=2) for t in (HI, LO))
                    for bi in range(2):
                        for tt in range(TT):
                            for n in range(2):
                                c = slice(512 * n, 512 * n + 512)
                                m = slice(256 * bi + P * tt, 256 * bi + P * tt + P)
                                ins = three(M[2 * tt + n][:], AH[s % 2][:, m], AL[s % 2][:, m], vh[:, bi, c], vl[:, bi, c], False, False, skip_group_check=True)
                    ins.then_inc(hp_used, 1)

                def dense_step(q, j, it=0):
                    s = STEPS * q + j
                    if AHEAD <= s + 1 < PAIRS:
                        expert_in(s + 1, it)
                    two = q == 0 and AHEAD - 1 <= j < STEPS - 1
                    if two:
                        table(1, 2 * (j - AHEAD + 1), it, 4)
                    elif 0 < q < CHUNKS - 1:
                        table(q + 1, j, it)
                    expert_out(s, it)
                    if two:
                        table(1, 2 * (j - AHEAD + 1) + 1, it, 4)

                for k in range(STEPS):
                    table(0, k)
                for j in range(AHEAD - 1):
                    dense_step(0, j)
                for q in range(CHUNKS):
                    j0 = AHEAD - 1 if q == 0 else 0
                    with pe.Fori(0, (STEPS - 1 - j0) // 2 - (q == 0)) as it:
                        for j in (j0, j0 + 1):
                            dense_step(q, j, it)
                    for j in range(STEPS - 3 if q == 0 else STEPS - 2, STEPS):
                        dense_step(q, j)
                for n in range(4):
                    ins = pe.matmul(M[n][:, 0:P], cst("zero"), cst("zero"), start=False, stop=True, skip_group_check=True)
                ins.then_inc(sem("f_done"), 1)



def _half_panels(w):
    n = w.shape[1]
    return w.reshape(KT, P, n // 256, 256).transpose(2, 1, 0, 3).reshape(n // 256, P, HP)


def _constants():
    c = np.zeros((P, N_CONST), np.float32)
    i = np.arange(P)

    def put(name, v):
        a, b = CONST[name]
        c[:, a:b] = v

    put("ident", np.eye(P))
    put("iota", i[None, :])
    put("blk", (i[:, None] // HEAD) == (i[None, :] // HEAD))
    put("ones", 1.0)
    rot = np.zeros((P, P))
    for m in range(P):
        if m % 32 < 16:
            rot[m + 16, m] = -1.0
        else:
            rot[m - 16, m] = 1.0
    put("rot", rot)
    tok = np.arange(TOK)
    inv = (np.float32(10000.0) ** (-np.arange(0, 32, 2, dtype=np.float32) / np.float32(32)))
    pos = np.where(((i % 64) // 32 == 0)[:, None], (tok // 64)[None, :], (tok % 64)[None, :]).astype(np.float32)
    ang = pos * inv[i % 16][:, None]
    put("cos", np.cos(ang))
    put("sin", np.sin(ang))
    put("chunkmask", (i[:, None] // CHUNK) == np.arange(8)[None, :])
    j = np.arange(16)
    for name, v in (("first", j == 0), ("notfirst", j > 0), ("last", j == 15), ("notlast", j < 15)):
        put(name, v)
    put("gscan", (np.arange(64) > 0))
    put("causal", (i % 64)[:, None] <= np.arange(64)[None, :])
    return c


def _order_in():
    sizes = [512, 128, 128, 256, 256, 256, 256, 256, 256, 256]
    at = np.concatenate([[0], np.cumsum(sizes)])
    qa, ka, va, qh, ih, ff, fb, gh, ac, gc = [np.arange(at[n], at[n + 1]) for n in range(10)]
    heads = qa.reshape(8, HEAD)
    q = np.concatenate([heads[[c, c + 4]].reshape(-1) for c in range(4)])
    return np.concatenate([ih, qh, ff, fb, gh, ac, gc, ka, va, q])


def _order_out():
    heads = np.arange(512).reshape(8, HEAD)
    return np.concatenate([heads[[c, c + 4]].reshape(-1) for c in range(4)] + [np.arange(512, 1024)])


def _columns(v):
    return v.reshape(v.shape[0], -1, P).transpose(0, 2, 1)


def layout_first(inp):
    f = lambda n: np.asarray(inp[n])
    parts = []
    wm = f("w_mem_kv_2")
    for l in range(DEPTH):
        parts.append(_half_panels(wm[l]))
    oi, oo = _order_in(), _order_out()
    for l in range(DEPTH):
        parts.append(_half_panels(f("w_in")[l][:, oi]))
        parts.append(_half_panels(f("w_out")[l][oo]))
        parts.append(_half_panels(f("w_mlp_in")[l]))
        for kc in range(4):
            parts.append(_half_panels(f("w_mlp_out")[l][1024 * kc:1024 * kc + 1024]))
    par = np.concatenate([
        _columns(f("norm_mix")), _columns(f("norm_mlp")),
        np.tile(f("q_norm"), (1, 2))[:, :, None], np.tile(f("k_norm"), (1, 2))[:, :, None],
        _columns(f("hgrn_norm")),
        f("conv_w").reshape(DEPTH, CONV_K, 2, P).transpose(0, 3, 2, 1).reshape(DEPTH, P, 62),
        _columns(f("conv_b")), _columns(f("conv_ln_g")), _columns(f("conv_ln_b"))], axis=2)
    lb = np.stack([f("hgrn_lb_fwd"), f("hgrn_lb_bwd")], 1).reshape(DEPTH, 2, 2, P).transpose(3, 0, 1, 2).reshape(P, 8)
    lb = np.concatenate([lb, np.zeros((P, 8), np.float32)], 1)
    return parts, par, lb


def layout_second(inp):
    f = lambda n: np.asarray(inp[n])
    parts = []
    qk = np.arange(GLA_H * GLA_K).reshape(GLA_H, GLA_K)
    wa = f("a_w_in_2")[0]
    n_qk, n_v = GLA_H * GLA_K, GLA_H * GLA_V
    gate0 = 2 * n_qk + 2 * n_v
    pad = np.zeros((D, 2 * GLA_H, P), np.float32)
    pad[:, :, :GLA_K] = wa[:, :2 * n_qk].reshape(D, 2 * GLA_H, GLA_K)
    pad[:, 0, GLA_K:GLA_K + 16] = wa[:, gate0:gate0 + 16]
    a_in = np.concatenate([pad.reshape(D, -1), wa[:, gate0 + 16:], wa[:, 2 * n_qk:gate0]], axis=1)
    for l, w_in in enumerate([a_in, f("b_w_in_2")[0]]):
        if l > 0:
            parts.append(_half_panels(f("shared_w_kv_2")))
        parts.append(_half_panels(w_in))
        parts.append(_half_panels(f("w_out_2")[l]))
        parts.append(_half_panels(f("peer_w_q_2")[l]))
        u = f("peer_u_2")[l].reshape(KEYS, PAIRS, 2, KT, P).transpose(1, 4, 3, 2, 0).reshape(PAIRS, P, HP)
        v = f("peer_v_2")[l].reshape(KEYS, PAIRS, 2, D).transpose(1, 0, 2, 3).reshape(PAIRS, P, HP)
        dense = np.empty((2 * PAIRS, P, HP), np.float32)
        for s in range(PAIRS):
            dense[u_at(s)], dense[v_at(s)] = u[s], v[s]
        parts.append(dense)
    par2 = np.zeros((P, 16), np.float32)
    par2[:GLA_K, 0:GLA_H] = f("a_b_gate_2")[0].reshape(GLA_H, GLA_K).T
    par2[:, 4:10] = f("a_norm_g_2")[0].reshape(6, P).T
    rows = np.stack([np.stack([f(f"ln_{n}_g_2")[l], f(f"ln_{n}_b_2")[l]]) for l in range(DEPTH) for n in ("mix", "ffn")])
    keys = np.ascontiguousarray(f("peer_sub_keys_2").transpose(0, 3, 1, 2))
    return parts, par2, np.ascontiguousarray(f("a_w_gate2_2")[0]), rows, keys


def _dilated_mask():
    i, j = np.arange(TOK)[:, None], np.arange(TOK)[None, :]
    groups = [(i >= j) & (i - j <= w) & ((i - j) % d == 0) for w, d in ((128, 1), (512, 4), (2048, 16))]
    m = np.where(np.stack(groups, 1), 0.0, NEG).astype(np.float32)
    return np.ascontiguousarray(m.reshape(TT, P, GROUPS * TOK).transpose(1, 0, 2))


def kernel(**inputs):
    import concourse.bacc as _bacc
    from concourse.bass_utils import run_bass_kernel_spmd

    parts, par, lb = layout_first(inputs)
    more, par2, wg2, rows, keys = layout_second(inputs)
    f = lambda n: np.asarray(inputs[n])
    arrays = {"stream": np.concatenate(parts + more, 0), "x": f("x")[0], "mem": f("mem_2")[0], "consts": _constants(),
              "par": np.ascontiguousarray(par), "lb": np.ascontiguousarray(lb), "par2": par2, "wg2": wg2,
              "mask": _dilated_mask(), "rows": rows, "keys": keys}
    nc = _bacc.Bacc("TRN2", target_bir_lowering=False, num_devices=1)
    aps = {k: nc.dram_tensor(k, v.shape, F32, kind="ExternalInput").ap() for k, v in arrays.items()}
    out = nc.dram_tensor("out", (TOK, D), F32, kind="ExternalOutput").ap()
    build(nc, aps["stream"], aps["x"], aps["mem"], aps["consts"], aps["par"], aps["lb"], aps["par2"], aps["wg2"], aps["mask"],
          aps["rows"], aps["keys"], out)
    r = run_bass_kernel_spmd(nc, [arrays], core_ids=[0])
    return np.asarray(r.results[0]["out"]).reshape(1, TOK, D)
```

```python
from contextlib import ExitStack

import numpy as np
import concourse.bass as bass
from concourse import mybir

F32 = mybir.dt.float32
BF16 = mybir.dt.bfloat16
F32R = mybir.dt.float32r
I32 = mybir.dt.int32
U32 = mybir.dt.uint32
ALU = mybir.AluOpType
ACT = mybir.ActivationFunctionType
AX = mybir.AxisListType

P = 128
TOK = 256
TT = TOK // P
D = 1024
KT = D // P
DEPTH = 2
HP = 2048
SLOTS = 4
HEAD = 64
EPS = 1e-6
LN_EPS = 1e-5
CHUNK = 16
NCH = TOK // CHUNK
CONV_K = 31
CONV_PAD = 15
D_FF = 4096
GLA_H, GLA_K, GLA_V, GLA_C = 4, 96, 192, 64
MEM_H = 4
SLOT_H = 6
GROUPS = 3
DN_ALPHA = (2.0 * DEPTH) ** 0.25
NEG = -1.0e30
KEYS = 128
PH = 8
TOPK = 16
FULL, NARROW = 4, 4
CANDS = FULL * TOPK + (TOPK - FULL) * NARROW
PAIRS = KEYS // 2
CHUNKS = 4
BC = KEYS // CHUNKS
STEPS = PAIRS // CHUNKS
AHEAD = 8
TPS = TOK // STEPS

N_MEM = 2 * DEPTH
N_IN, N_OUT, N_UP, N_DOWN = 10, 4, 16, 16
N_FIRST = N_IN + N_OUT + N_UP + N_DOWN
N_MIX2, N_WQ, N_DENSE, N_SHARED = [11, 10], 8, 2 * PAIRS, 6
N_SECOND = [m + N_OUT + N_WQ + N_DENSE for m in N_MIX2]
HP_FIRST = [N_MEM + l * N_FIRST for l in range(DEPTH)]
HP_SHARED = N_MEM + DEPTH * N_FIRST + N_SECOND[0]
HP_SECOND = [N_MEM + DEPTH * N_FIRST, HP_SHARED + N_SHARED]
HP_DENSE = [HP_SECOND[l] + N_MIX2[l] + N_OUT + N_WQ for l in range(DEPTH)]
N_HP = HP_SECOND[1] + N_SECOND[1]



def u_at(s):
    return s if s < AHEAD else 2 * s - 1


def v_at(s):
    return AHEAD + s if s < AHEAD - 1 else min(2 * s + 2, N_DENSE - 1)


CONST = {}
_c = 0
for _n, _w in (("ident", 128), ("iota", 128), ("zero", 128), ("blk", 128), ("ones", 128), ("rot", 128),
               ("cos", 256), ("sin", 256), ("chunkmask", 8), ("notfirst", 16), ("first", 16),
               ("notlast", 16), ("last", 16), ("gscan", 64), ("causal", 64)):
    CONST[_n] = (_c, _c + _w)
    _c += _w
N_CONST = _c
PAR = {}
_c = 0
for _n, _w in (("norm_mix", 8), ("norm_mlp", 8), ("qg", 1), ("kg", 1), ("ng", 2), ("cw", 62), ("cb", 2),
               ("lng", 2), ("lnb", 2)):
    PAR[_n] = (_c, _c + _w)
    _c += _w
N_PAR = _c


class Steps:

    def __init__(self, eng, own):
        self.eng, self.own, self.count = eng, own, {}

    def mark(self, ins, s=None, n=1):
        s = self.own if s is None else s
        self.count[s.name] = self.count.get(s.name, 0) + n
        ins.then_inc(s, n)
        return self.count[s.name]

    def step(self, ins, s=None):
        s = self.own if s is None else s
        self.eng.wait_ge(s, self.mark(ins, s))


def build(nc, stream, x_in, mem_in, const_in, par_in, lb_in, par2_in, wg2_in, mask_in, rows_in, sk_in, out):
    ctx = ExitStack()
    with ctx:
        sems = {}

        def sem(name):
            if name not in sems:
                sems[name] = ctx.enter_context(nc.semaphore(name))
            return sems[name]

        cursor = [(nc.sbuf_base + 63) // 64 * 64]
        end = nc.sbuf_usable_end // 64 * 64

        def at(name, shape, dt=F32, off=None):
            size = int(np.prod(shape[1:])) * (2 if dt == BF16 else 4)
            o = cursor[0] if off is None else off
            if off is None:
                cursor[0] += (size + 63) // 64 * 64
            assert o + size <= end, (name, o + size, end)
            return nc.alloc_sbuf_tensor_at(name, list(shape), dt, offset=o)

        RAW = at("raw", [P, SLOTS, HP])
        HI = [at(f"hi{i}", [P, HP], F32R) for i in range(SLOTS)]
        LO = [at(f"lo{i}", [P, HP], F32R) for i in range(SLOTS)]
        XH = at("xh", [P, KT, TOK], F32R)
        XL = at("xl", [P, KT, TOK], F32R)
        cst0 = cursor[0]
        CST = at("cst", [P, N_CONST])
        SMALL = at("small", [P, 112])
        X = at("x", [P, TT, D])
        mix0 = cursor[0]
        LBS = at("lbs", [P, 16], off=end - 64)
        PR = at("pr", [P, DEPTH, N_PAR], off=end - 64 - 704)
        LB = at("lb", [P, DEPTH, 2, 2, 2], off=end - 64 - 704 - 64)
        top = end - 64 - 704 - 64

        E = at("e", [P, 2, 2 * TOK])
        F = at("f", [P, 2, 2 * TOK])
        KG = at("kg", [P, 2, 2 * TOK])
        MIXF = at("mixf", [P, KT, TOK], off=cursor[0] - 8192)
        Q = at("q", [P, 2 * TOK])
        VR = at("vr", [P, TT, 256])
        VT = at("vt", [P, 2 * TOK])
        GT = at("gt", [P, 2 * TOK])
        AC = at("ac", [P, 2 * TOK])
        EG = at("eg", [P, 2 * TOK])
        UP = at("up", [P, 2, TOK + 2 * CONV_PAD])
        W = at("w", [P, 2 * TOK])
        XX = at("xx", [P, 2, 2 * TOK])
        TB = at("tb", [P, 2 * TOK])
        ACC = at("acc", [P, 2 * TOK])
        SCN = at("scn", [P, 2 * TOK])
        QB = at("qb", [P, 2, 2 * TOK])
        ST = [at("st0", [P, 2, NCH, HEAD]), at("st1", [P, 2, NCH, HEAD], off=mix0)]
        DG = at("dg", [P, 4, P])
        QK = at("qk", [P, 5, TOK])
        VA = at("va", [P, TT, P])
        r1 = cursor[0]
        VX = at("vx", [P, TT, 4, 8, HEAD])
        assert cursor[0] <= top, (cursor[0], top)
        XS = at("xs", [P, TT, D], off=r1)
        QK2 = at("qk2", [P, 5, TOK], off=r1)
        QK3 = at("qk3", [P, 5, TOK], off=r1 + 5 * TOK * 4)
        PM = at("pm", [P, 2, 2, TOK], off=r1)
        PT = at("pt", [P, 2, 2, TOK], off=r1 + 4096)
        KVM = at("kvm", [P, 1024], off=mix0)
        HH = at("hh", [P, 32, TOK], F32R, off=mix0)
        HL = at("hl", [P, 32, TOK], F32R, off=mix0 + 32768)
        RB = at("rb", [P, 2, 2 * TOK], off=mix0 + 65536)
        SQ = at("sq", [P, 2 * TOK], off=mix0 + 65536 + 4096)
        XS2 = at("xs2", [P, TT, D], off=mix0 + 65536 + 6144)
        assert mix0 + 65536 + 6144 + 8192 <= top

        def cst(name):
            a, b = CONST[name]
            return CST[:, a:b]

        def par(l, name, i=0, n=1):
            c = PAR[name][0] + i
            return PR[:, l, c:c + n]

        def flat(t):
            return t.rearrange("p a b -> p (a b)")

        def v16(t):
            return t.rearrange("p (a c) -> p a c", c=CHUNK)

        cursor[0] = mix0
        ROWS = at("rows", [P, 2, D])
        MIX2 = at("mix2", [P, KT, TOK])
        KVL = at("kvl", [P, 1024])
        QM = at("qm", [P, 2, TOK])
        PM2 = at("pm2", [P, 2, 2, TOK])
        PT2 = at("pt2", [P, 2, 2, TOK])
        both = cursor[0]
        GO2 = at("go2", [P, TT, 768], off=both)
        GSQ = at("gsq", [P, GLA_V], off=both + 6144)
        GQ = at("gq", [P, 4, TOK])
        GK = at("gk", [P, 4, TOK])
        GV = at("gv", [P, TT, 768])
        GR = at("gr", [P, TT, 768])
        LG = at("lg", [P, 4, TOK])
        KTD = at("ktd", [P, 4, TOK], off=cursor[0] - 4096)
        GO = at("go", [P, TT, 768], off=cursor[0] - 4096)
        RG = at("rg", [P, TT, 768], off=cursor[0] + 2048)
        B = at("b", [P, 4, TOK])
        KE = at("ke", [P, 4, TOK])
        SM = at("sm", [P, 4, TOK], off=cursor[0] - 4096)
        QTD = at("qtd", [P, 4, TOK])
        KER = at("ker", [P, TT, 4 * GLA_K])
        ATT = at("att", [P, 8, GLA_C])
        STA = at("sta", [P, 4, GLA_V])
        WG2 = at("wg2", [P, 4 * GLA_K])
        P2 = at("p2", [P, 16])
        BL = at("bl", [P, 16])
        assert cursor[0] <= end
        EXA = at("exa", [P, 4, TOK], off=both - 8192)
        EXB = at("exb", [P, 4, TOK], off=both - 4096)
        cursor[0] = both
        QD = at("qd", [P, GROUPS * SLOT_H, TOK])
        KD = at("kd", [P, SLOT_H, TOK])
        VD = at("vd", [P, TT, 768])
        DM = at("dm", [P, TT, GROUPS * TOK])
        S3 = at("s3", [P, 2, GROUPS * TOK])
        PD = at("pd", [P, 2, 2, TOK])
        PTD = at("ptd", [P, 2, TOK])
        assert cursor[0] <= end
        cursor[0] = mix0
        TFX = at("tfx", [P, 2, TT * PH, TOPK, TOPK], BF16, off=mix0)
        QP = at("qp", [P, 2 * PH, TOK])
        CD2 = at("cd2", [P, PH, CANDS], off=cursor[0])
        EQ = at("eq", [P, TT * PH, TOPK, TOPK], BF16, off=cursor[0] + 8192)
        SC = at("sc", [P, TT, 2 * PH, KEYS])
        S2 = at("s2", [P, TT, 2 * PH, KEYS], off=cursor[0])
        cd0 = cursor[0]
        CD = at("cd", [P, TT, PH, CANDS])
        BK = at("bk", [P, 4, TT * PH * TOPK], U32)
        BF = at("bf", [P, 4, TT * PH * TOPK])
        WIDE = at("wide", [P, TT * PH * TOPK])
        assert cursor[0] <= cd0 + 16384
        cursor[0] = cd0 + 16384
        TS = at("ts", [P, TT, 2 * PH, TOPK])
        TI = at("ti", [P, TT, 2 * PH, TOPK], U32)
        TF = at("tf", [P, TT, 2 * PH, TOPK])
        BS = at("bs", [P, TT * PH, TOPK])
        GX = at("gx", [P, TT * PH, TOPK])
        BJ = at("bj", [P, TT, PH, TOPK], U32)
        JF = at("jf", [P, 2, TT * PH, TOPK], BF16)
        GSUM = at("gsum", [P, TT * PH])
        SEL = at("sel", [P, 3, TT, PH * TOPK])
        SK = at("sk", [P, 2, KEYS])
        HA = at("ha", [P, AHEAD, 512])
        assert cursor[0] <= end
        x0 = mix0 - 8192
        PF = at("pf", [P, TOK], off=x0)
        PB = at("pb", [P, 2, TOK], BF16, off=x0 + 1024)
        EQB = at("eqb", [P, BC, TPS], BF16, off=x0 + 2048)
        OB = at("ob", [P, 3, BC, TPS], BF16, off=x0 + 3072)
        GS = at("gs", [P, 3, TOK], BF16, off=x0 + 6144)
        IOT = at("iot", [P, KEYS, TPS], BF16, off=cst0 + 4 * CONST["blk"][0])
        cursor[0] = mix0
        G = [at(f"g{i}", [P, BC, TOK]) for i in range(2)]
        g1 = mix0 + 4 * BC * TOK
        GA = at("ga", [P, AHEAD, 512], off=g1)
        OA2 = at("oa2", [P, KEYS, TPS], BF16, off=g1 + 16384)
        OB2 = at("ob2", [P, 3, BC, TPS], BF16, off=g1 + 16384 + 4096)
        GE = at("ge", [P, 2, 512])
        AH = [at(f"ah{i}", [P, 512], F32R) for i in range(2)]
        AL = [at(f"al{i}", [P, 512], F32R) for i in range(2)]
        OA = at("oa", [P, KEYS, TPS], BF16)
        assert cursor[0] <= end
        x_scr = nc.dram_tensor("x_scratch", [P, TT, D], F32).ap()
        PS = [ctx.enter_context(nc.psum_tensor(f"lin{i}", [P, 512], F32)) for i in range(4)]
        M = [ctx.enter_context(nc.psum_tensor(f"m{i}", [P, 512], F32)) for i in range(4)]
        UB = [PS[0:4], [M[1], M[2], M[3], PS[0]]]
        UC = [[M[0], M[1]], [PS[0], PS[1]]]
        mem_scr = nc.dram_tensor("mem_kv_scratch", [DEPTH, P, 1024], F32).ap()

        raw_loaded = [sem(f"raw_loaded{i}") for i in range(SLOTS)]
        bank_free = [sem(f"bank_free{i}") for i in range(4)]
        hi_ready, lo_ready, hp_used = sem("hi_ready"), sem("lo_ready"), sem("hp_used")

        read_out = [True] * N_HP
        for l in range(DEPTH):
            for i in range(N_DOWN - 4):
                read_out[HP_FIRST[l] + N_IN + N_OUT + N_UP + i] = False
            for i in range(N_DENSE):
                read_out[HP_DENSE[l] + i] = False

        def reads_before(i):
            return sum(read_out[j] for j in range(i % 4, i, 4))

        def evicted(eng, i, it=0):
            eng.wait_ge(bank_free[i % 4], reads_before(i) + 1 + it)

        block = ctx.enter_context(nc.Block())

        @block.sync
        def _(sp):
            sp.dma_start(X[:], mem_in.rearrange("(t p) d -> p t d", p=P)).then_inc(sem("mem_loaded"), 16)
            for i in range(SLOTS):
                if i == 1:
                    sp.wait_ge(sem("mem_loaded"), 16)
                sp.dma_start(RAW[:, i, :], stream[i]).then_inc(raw_loaded[i], 16)
            rounds = N_HP // SLOTS
            with sp.Fori(1, rounds) as g:
                for i in range(SLOTS):
                    sp.wait_ge(lo_ready, g * SLOTS + (i + 1 - SLOTS))
                    sp.dma_start(RAW[:, i, :], stream[g * SLOTS + i]).then_inc(raw_loaded[i], 16)
            for i in range(SLOTS * rounds, N_HP):
                sp.wait_ge(lo_ready, i + 1 - SLOTS)
                sp.dma_start(RAW[:, i % SLOTS, :], stream[i]).then_inc(raw_loaded[i % SLOTS], 16)
            sp.wait_ge(sem("x_final"), 1)
            sp.dma_start(out.rearrange("(t p) d -> p t d", p=P), X[:]).then_inc(sem("out_stored"), 16)
            sp.wait_ge(sem("out_stored"), 16)

        def attention_act(act, a, g0, heads, scale, dst, part, PM=PM, PT=PT, between=lambda n: None, panel=lambda n: None):
            def tail(n):
                g = g0 + n
                act.wait_ge(sem("pt_done"), g + 1)
                a.mark(act.activation(flat(PT[:, g % 2, :, :]), M[2][:], ACT.Copy), sem("pt_ready"))
                panel(n + 1)
                act.wait_ge(sem("pv_done"), g + 1)
                o = part(n)
                a.mark(act.activation(dst(n), M[3][o:o + 64, 0:256], ACT.Copy), sem("o_ready"))

            for n in range(heads):
                g = g0 + n
                act.wait_ge(sem("nb_ready"), g + 1)
                if n >= 2:
                    act.wait_ge(sem("pt_done"), g - 1)
                c = 16 + 8 * (g % 2)
                for qt in range(2):
                    ins = act.activation(PM[:, g % 2, qt, :], M[g % 2][:, 256 * qt:256 * qt + 256], ACT.Exp,
                                         scale=scale, bias=SMALL[:, c + 2 + qt:c + 3 + qt], accum_out=SMALL[:, c + 4 + qt:c + 5 + qt])
                a.mark(ins, sem("exp_ready"))
                if n == 0:
                    panel(0)
                if n >= 1:
                    tail(n - 1)
                between(n)
            tail(heads - 1)
            act.wait_ge(sem("o_ready"), g0 + heads)

        @block.scalar
        def _(act):
            a = Steps(act, sem("act_step"))
            nxt = [0]

            def hi(i, it=0):
                act.wait_ge(raw_loaded[i % SLOTS], 16 * (i // SLOTS + 1) + it * 16)
                if i >= SLOTS:
                    act.wait_ge(hp_used, i + 1 - SLOTS + it * SLOTS)
                act.activation(HI[i % SLOTS][:], RAW[:, i % SLOTS, :], ACT.Copy).then_inc(hi_ready, 1)

            def hi_to(n):
                while nxt[0] < min(n, N_HP):
                    hi(nxt[0])
                    nxt[0] += 1

            def xh_evict(inst, gain=None):
                for kp in range(4):
                    act.wait_ge(sem("t_done"), 4 * inst + kp + 1)
                    if gain is None:
                        ins = act.activation(flat(XH[:, 2 * kp:2 * kp + 2, :]), M[kp][:], ACT.Copy)
                    else:
                        act.activation(XH[:, 2 * kp, :], M[kp][:, 0:256], ACT.Copy, scale=gain(2 * kp))
                        ins = act.activation(XH[:, 2 * kp + 1, :], M[kp][:, 256:512], ACT.Copy, scale=gain(2 * kp + 1))
                    a.mark(ins, sem("xh_ready"))

            def rstd(out_, in_, n, eps, signal=None):
                a.step(act.activation(out_, in_, ACT.Ln, scale=1.0 / n, bias=eps))
                a.step(act.activation(out_, out_, ACT.Exp, scale=-0.5), signal)

            def sigmoid(t, signal):
                a.step(act.activation(t, t, ACT.Ln, bias=1.0))
                a.mark(act.activation(t, t, ACT.Exp, scale=-1.0), signal)

            def rms_rows(junk):
                for tt in range(TT):
                    a.step(act.activation(junk[:, tt, :], X[:, tt, :], ACT.Square, accum_out=SMALL[:, tt:tt + 1]))
                rstd(SMALL[:, 2:4], SMALL[:, 0:2], D, EPS, sem("row_rstd"))

            act.dma_start(CST[:], const_in).then_inc(sem("cst_loaded"), 16)
            act.dma_start(LBS[:], lb_in).then_inc(sem("cst_loaded"), 16)
            act.dma_start(PR[:], par_in.rearrange("l p n -> p l n")).then_inc(sem("cst_loaded"), 16)
            act.preload_act_table_set("natural_log_exp_and_others")
            act.wait_ge(sem("lb_shifted"), 1)
            a.step(act.activation(LBS[:, 0:8], LBS[:, 0:8], ACT.Exp), sem("lb_exp"))
            hi_to(2)
            xh_evict(0)
            act.wait_ge(sem("t_done"), 4)
            act.dma_start(X[:], x_in.rearrange("(t p) d -> p t d", p=P)).then_inc(sem("x_loaded"), 16)
            for l in range(DEPTH):
                hi_to(2 * l + 4)
                if l > 0:
                    act.wait_ge(sem("kvm_stored"), 16 * l)
                for i in (2 * l, 2 * l + 1):
                    act.wait_ge(hp_used, i + 1)
                    act.activation(KVM[:, 512 * (i % 2):512 * (i % 2) + 512], PS[i % 4][:], ACT.Copy).then_inc(bank_free[i % 4], 1)
                evicted(act, 2 * l)
                evicted(act, 2 * l + 1)
                act.dma_start(mem_scr[l], KVM[:]).then_inc(sem("kvm_stored"), 16)
            act.wait_ge(sem("x_loaded"), 16)

            for l in range(DEPTH):
                h0 = HP_FIRST[l]
                if l > 0:
                    for u in range(4):
                        evicted(act, h0 - 4 + u)
                rms_rows(XS)
                hi_to(h0 + 3)
                act.wait_ge(hp_used, h0)
                xh_evict(1 + 2 * l, lambda k: par(l, "norm_mix", k))
                dst = [VR, Q, (E, 0), (E, 1), GT, AC, EG, None, (QK, 0), (QK, 2)]
                if l == 0:
                    act.wait_ge(sem("kvm_stored"), 16 * DEPTH)
                for u in range(N_IN):
                    hi_to(h0 + u + 4)
                    i = h0 + u
                    act.wait_ge(hp_used, i + 1)
                    b = PS[i % 4]
                    if u == 7:
                        act.activation(QK[:, 4, :], b[:, 0:256], ACT.Copy)
                        ins = act.activation(flat(VA[:]), b[:, 256:512], ACT.Copy)
                    elif u in (2, 3):
                        ins = act.activation(E[:, u - 2, :], b[:], ACT.Exp, scale=-1.0)
                    elif u == 6:
                        ins = act.activation(EG[:], b[:], ACT.Exp, scale=-1.0)
                    elif u >= 8:
                        ins = act.activation(flat(QK[:, 2 * u - 16:2 * u - 14, :]), b[:], ACT.Copy)
                    else:
                        ins = act.activation(flat(VR[:]) if u == 0 else dst[u][:], b[:], ACT.Copy)
                    ins.then_inc(bank_free[i % 4], 1)
                    if u in (2, 3, 6):
                        evicted(act, i)
                        sigmoid(EG[:] if u == 6 else E[:, u - 2, :], sem("gates_ready"))
                    if u == 3:
                        act.wait_ge(sem("vt_done"), l + 1)
                        a.mark(act.activation(VT[:], M[0][:], ACT.Copy), sem("vt_ready"))
                hi_to(h0 + N_IN + N_OUT)
                for n in range(2 * CONV_K):
                    m = 2 * CONV_K * l + n
                    if n >= 4:
                        act.wait_ge(sem("diag_used"), m - 3)
                    a.mark(act.activation(DG[:, n % 4, :], cst("ident"), ACT.Copy, scale=par(l, "cw", n)), sem("diag_ready"))
                for d in range(2):
                    act.wait_ge(sem("kt_done"), 2 * l + d + 1)
                    a.step(act.activation(XX[:, 1 - d, :], M[2 - d][:], ACT.Copy), sem("kr_ready"))
                for j in range(3):
                    n = 512 if j < 2 else 256
                    act.wait_ge(sem("qss_done"), 3 * l + j + 1)
                    rstd(flat(QK3[:])[:, 512 * j:512 * j + n], M[1 + j][:, 0:n], HEAD, EPS, sem("qrs_ready"))
                act.wait_ge(sem("cvar_done"), l + 1)
                rstd(XX[:, 1, 0:256], PS[1][:, 256:512], 256, EPS, sem("crs_ready"))
                act.wait_ge(sem("hss_done"), l + 1)
                rstd(TB[:], PS[2][:], HEAD, EPS)
                a.step(act.activation(SCN[:], GT[:], ACT.Exp, scale=-1.0))
                sigmoid(SCN[:], sem("hrs_ready"))

                def conv_silu(n):
                    if n == 3:
                        act.wait_ge(sem("cy_ready"), l + 1)
                        a.step(act.activation(EG[:], AC[:], ACT.Exp, scale=-1.0))
                        sigmoid(EG[:], sem("ceg_ready"))
                    elif n == 6:
                        act.wait_ge(sem("mix_ready"), l + 1)
                        a.mark(act.activation(flat(XH[:, 4:8, :]), flat(MIXF[:, 4:8, :]), ACT.Copy), sem("mixh_ready"))

                attention_act(act, a, 8 * l, 8, HEAD ** -0.5, lambda n: MIXF[64 * (n // 4):64 * (n // 4) + 64, n % 4, :],
                              lambda n: 64 * (n // 4), between=conv_silu)
                a.step(act.activation(flat(XH[:, 0:4, :]), flat(MIXF[:, 0:4, :]), ACT.Copy), sem("mixh_ready"))
                h1 = h0 + N_IN + N_OUT
                hi_to(h1 + 2)
                for u in range(4):
                    evicted(act, h1 - 4 + u)
                rms_rows(XS2)
                hi_to(h1 + 3)
                xh_evict(2 + 2 * l, lambda k: par(l, "norm_mlp", k))
                with act.Fori(0, N_UP // 4) as it:
                    for u in range(4):
                        hi(h1 + u + 3, it)
                        act.wait_ge(hp_used, h1 + u + 1 + it * 4)
                        act.wait_ge(sem("hid_ready"), 16 * l + u + 1 + it * 4)
                        act.activation(RB[:, u % 2, :], PS[(h1 + u) % 4][:], ACT.Relu).then_inc(bank_free[(h1 + u) % 4], 1)
                        evicted(act, h1 + u, it)
                        act.activation(flat(HH[:, bass.ds(it * 8 + 2 * u, 2), :]), RB[:, u % 2, :],
                                       ACT.Square).then_inc(sem("sq_ready"), 1)
                nxt[0] = h1 + N_UP + 3
                hi_to(h1 + N_UP + N_DOWN + 2)
            for l in range(DEPTH):
                s0 = HP_SECOND[l]
                act.wait_ge(sem("x_ready"), 2 * l + 1)
                act.wait_ge(hp_used, HP_SHARED if l > 0 else s0)
                for dst_, src_ in [(ROWS[:], rows_in[2 * l].partition_broadcast(P)), (KVL[:], mem_scr[l])] + \
                        ([(WG2[96:112, :], wg2_in), (P2[:], par2_in)] if l == 0 else [(DM[:], mask_in)]):
                    act.dma_start(dst_, src_).then_inc(sem(f"mix_loaded{l}"), 16)
                hi_to(HP_SHARED + 2 if l > 0 else s0 + 3)
                xh_evict(5 + 2 * l)
                if l > 0:
                    for u in range(N_SHARED):
                        hi_to(HP_SHARED + u + 4)
                        i = HP_SHARED + u
                        act.wait_ge(hp_used, i + 1)
                        b = PS[i % 4]
                        if u < 3:
                            ins = act.activation(flat(KD[:, 2 * u:2 * u + 2, :]), b[:], ACT.Copy)
                        else:
                            ins = act.activation(VD[:, :, 256 * (u - 3):256 * (u - 2)], b[:].rearrange("p (t n) -> p t n", t=2), ACT.Copy)
                        ins.then_inc(bank_free[i % 4], 1)
                def mixing_panel(u):
                    hi_to(s0 + u + 4)
                    i = s0 + u
                    act.wait_ge(hp_used, i + 1)
                    b = PS[i % 4]
                    if l == 0 and u >= 5:
                        t, j = (GV, u - 5) if u < 8 else (GR, u - 8)
                        ins = act.activation(t[:, :, 256 * j:256 * j + 256], b[:].rearrange("p (t n) -> p t n", t=2), ACT.Copy)
                    else:
                        t = (QM if u == 4 else GQ[:, 2 * u:2 * u + 2, :] if u < 2 else GK[:, 2 * u - 4:2 * u - 2, :]) if l == 0 \
                            else QM if u == 0 else QD[:, 2 * u - 2:2 * u, :]
                        ins = act.activation(flat(t[:] if t is QM else t), b[:], ACT.Copy)
                    ins.then_inc(bank_free[i % 4], 1)

                k96 = slice(0, GLA_K)
                if l == 0:
                    for u in range(4):
                        mixing_panel(u)
                    act.wait_ge(sem("gpre_read"), 1)
                    act.wait_ge(sem("mix_loaded0"), 64)
                    for h in range(4):
                        ins = act.activation(EXA[k96, h, :], M[h // 2][k96, 256 * (h % 2):256 * (h % 2) + 256], ACT.Abs, bias=P2[k96, h:h + 1])
                    a.step(ins)
                    a.step(act.activation(flat(EXB[k96]), flat(EXA[k96]), ACT.Exp, scale=-1.0))
                    a.step(act.activation(flat(EXA[k96]), flat(EXB[k96]), ACT.Ln, bias=1.0), sem("lsig_ready"))
                    mixing_panel(4)
                    act.wait_ge(sem("cum_ready"), 1)
                    a.mark(act.activation(flat(EXA[k96]), flat(B[k96]), ACT.Exp, scale=1.0 / 16))
                    a.mark(act.activation(flat(EXB[k96]), flat(B[k96]), ACT.Exp, scale=-1.0 / 16))
                    a.mark(act.activation(flat(KE[k96]), flat(KE[k96]), ACT.Exp, scale=1.0 / 16))
                    a.step(act.activation(BL[k96], B[k96].rearrange("p h (n c) -> p (h n) c", c=GLA_C)[:, :, GLA_C - 1], ACT.Exp, scale=1.0 / 16), sem("gexp_ready"))
                    mixing_panel(5)
                else:
                    mixing_panel(0)
                p0 = 6 if l == 0 else 1
                attention_act(act, a, 16 + 4 * l, MEM_H, HEAD ** -0.5, lambda n: MIX2[64 * (n % 2):64 * (n % 2) + 64, 6 + n // 2, :],
                              lambda n: 64 * (n % 2), PM2, PT2,
                              panel=lambda n: mixing_panel(p0 + n))
                p1 = p0 + MEM_H + 1

                def mix_high(a0, a1):
                    a.mark(act.activation(flat(XH[:, a0:a1, :]), flat(MIX2[:, a0:a1, :]), ACT.Copy), sem(f"mix_high{l}"))

                if l == 0:
                    mix_high(6, 8)
                    hi_to(s0 + N_MIX2[l] + 3)
                    act.wait_ge(sem("ket_done"), 1)
                    for tt in range(TT):
                        ins = act.activation(KER[:, tt, :], M[2 + tt][:, 0:384], ACT.Copy)
                    a.step(ins, sem("ker_ready"))
                    a.step(act.activation(flat(RG[:]), flat(GR[:]), ACT.Exp, scale=-1.0))
                    sigmoid(flat(RG[:]), sem("rsig_ready"))
                    for ch in range(4):
                        rows = slice(64 * (ch % 2), 64 * (ch % 2) + 64)
                        act.wait_ge(sem("oc_done"), ch + 1)
                        for j in range(2):
                            ins = act.activation(GO[rows, ch // 2, 384 * j:384 * j + 384], M[2 + j][rows, 0:384], ACT.Copy)
                        a.step(ins, sem("go_ready"))
                        for h in range(4):
                            c = 48 + 4 * (ch // 2) + h
                            ins = act.activation(GSQ[rows, :], GO[rows, ch // 2, GLA_V * h:GLA_V * h + GLA_V], ACT.Square, accum_out=SMALL[rows, c:c + 1])
                            a.step(ins)
                    rstd(SMALL[:, 48:56], SMALL[:, 48:56], GLA_V, EPS, sem("grs_ready"))
                    act.wait_ge(sem("got_done"), 1)
                    for kt in range(6):
                        ins = act.activation(XH[:, kt, :], M[kt // 2][:, 256 * (kt % 2):256 * (kt % 2) + 256], ACT.Copy, scale=P2[:, 4 + kt:5 + kt])
                        if kt % 2 == 1:
                            a.mark(ins, sem("mix_high0"))
                else:
                    def slot_out(sl):
                        act.wait_ge(sem("dpt_done"), sl + 1)
                        a.mark(act.activation(flat(PTD[:]), M[2][:], ACT.Copy), sem("dpt_ready"))
                        if p1 + sl < N_MIX2[l]:
                            mixing_panel(p1 + sl)
                        act.wait_ge(sem("dpv_done"), sl + 1)
                        a.mark(act.activation(MIX2[:, sl, :], M[3][:, 0:256], ACT.Copy), sem("do_ready"))

                    for n in range(2 * SLOT_H):
                        act.wait_ge(sem("dnb_ready"), n + 1)
                        c = 48 + 2 * (n % 2)
                        a.mark(act.activation(S3[:, n % 2, :], S3[:, n % 2, :], ACT.Exp, scale=KEYS ** -0.5, bias=SMALL[:, c:c + 1],
                                              accum_out=SMALL[:, c + 1:c + 2]), sem("dexp_ready"))
                        if n >= 3 and n % 2 == 1:
                            slot_out(n // 2 - 1)
                    act.wait_ge(sem("do_ready"), SLOT_H - 1)
                    mix_high(0, SLOT_H - 1)
                    mix_high(6, 8)
                    slot_out(SLOT_H - 1)
                    act.wait_ge(sem("do_ready"), SLOT_H)
                    mix_high(SLOT_H - 1, SLOT_H)
                    hi_to(s0 + N_MIX2[l] + 3)
                w0 = s0 + N_MIX2[l] + N_OUT
                hi_to(w0 + 3)
                act.wait_ge(sem("ln_var"), 2 * l + 1)
                rstd(SMALL[:, 60:62], SMALL[:, 56:60].rearrange("p (t k) -> p t k", k=2)[:, :, 1], 1, LN_EPS, sem("ln_rstd"))
                def head_scores(h):
                    act.wait_ge(sem("keysc_done"), PH * l + h + 1)
                    a.mark(act.activation(SC[:, :, 2 * h:2 * h + 2, :], M[h % 4][:].rearrange("p (t s k) -> p t s k", t=TT, s=2), ACT.Copy), sem("keysc_ready"))

                act.wait_ge(sem("x_ready"), 2 * l + 2)
                act.dma_start(x_scr, X[:]).then_inc(sem("x_spilled"), 16)
                act.dma_start(SK[:], sk_in[l]).then_inc(sem("keys_loaded"), 16)
                hi_to(w0 + 3)
                xh_evict(6 + 2 * l)
                for u in range(N_WQ):
                    hi_to(w0 + u + 4)
                    i = w0 + u
                    act.wait_ge(hp_used, i + 1)
                    act.activation(flat(QP[:, 2 * u:2 * u + 2, :]), PS[i % 4][:], ACT.Copy).then_inc(bank_free[i % 4], 1)
                    if u >= 1:
                        head_scores(u - 1)
                head_scores(PH - 1)
                d0 = w0 + N_WQ
                for s in range(AHEAD):
                    hi_to(d0 + s + 4)
                    act.wait_ge(hp_used, d0 + s + 1)
                    act.activation(HA[:, s, :], PS[s % 2][:], ACT.Copy).then_inc(sem("ahead_copied"), 1)
                    if s >= AHEAD - 4:
                        side, tt = divmod(s - AHEAD + 4, 2)
                        act.wait_ge(sem("tf_ready"), l + 1)
                        a.mark(act.activation(TFX[:, side, PH * tt:PH * tt + PH, :, :],
                                              TF[:, tt].rearrange("p (h s) k -> p h s k", s=2)[:, :, side, :].unsqueeze(3).to_broadcast([P, PH, TOPK, TOPK]),
                                              ACT.Copy), sem("tfx_ready"))
                act.wait_ge(sem("gx_shifted"), l + 1)
                a.step(act.activation(flat(GX[:]), flat(GX[:]), ACT.Exp), sem("gx_ready"))
                act.wait_ge(sem("selt_done"), l + 1)
                act.wait_ge(sem("x_spilled"), 16 * (l + 1))
                a.mark(act.activation(flat(PB[:]), M[0][:], ACT.Copy))
                a.step(act.activation(PF[:], M[1][:, 0:256], ACT.Copy), sem("pf_ready"))

                t0, s00 = (CHUNKS * STEPS) * l, PAIRS * l

                def table_copy(q, k, it=0, per=2):
                    n = t0 + STEPS * q + k
                    act.wait_ge(sem("table_done"), n + 1 + it * per)
                    act.activation(G[q % 2][:, :, bass.ds(it * (per * TPS) + TPS * k, TPS)].rearrange("p b t -> p t b"),
                                   PS[2 + k % 2][:].rearrange("p (t b) -> p t b", b=BC), ACT.Copy).then_inc(sem("table_ready"), 1)

                def gelu(s, it=0):
                    act.wait_ge(hp_used, d0 + u_at(s) + 1 + it * 4)
                    act.wait_ge(sem("al_ready"), s00 + s - 1 + it * 2)
                    act.activation(GE[:, s % 2, :], PS[s % 2][:], ACT.Gelu).then_inc(sem("ge_ready"), 1)

                def act_high(s, it=0):
                    act.wait_ge(sem("a_ready"), s00 + s + 1 + it * 2)
                    if s >= 2:
                        act.wait_ge(hp_used, d0 + v_at(s - 2) + 1 + it * 4)
                    act.activation(AH[s % 2][:], GA[:, s, :] if s < AHEAD else GE[:, s % 2, :], ACT.Copy).then_inc(sem("ah_ready"), 1)

                def dense_step(q, j, it=0):
                    s = STEPS * q + j
                    if s < AHEAD - 2:
                        hi(d0 + AHEAD + 3 + s)
                    elif s >= AHEAD - 1:
                        for n in (3, 4):
                            if 2 * s + n < N_DENSE:
                                hi(d0 + 2 * s + n, it)
                    if AHEAD <= s + 1 < PAIRS:
                        gelu(s + 1, it)
                    two = q == 0 and AHEAD - 1 <= j < STEPS - 1
                    if two:
                        table_copy(1, 2 * (j - AHEAD + 1), it, 4)
                    elif 0 < q < CHUNKS - 1:
                        table_copy(q + 1, j, it)
                    if s + 1 < PAIRS:
                        act_high(s + 1, it)
                    if two:
                        table_copy(1, 2 * (j - AHEAD + 1) + 1, it, 4)

                for s in range(AHEAD):
                    a.mark(act.activation(GA[:, s, :], HA[:, s, :], ACT.Gelu), sem("ge_ready"))
                for k in range(STEPS):
                    table_copy(0, k)
                act_high(0)
                for j in range(AHEAD - 1):
                    dense_step(0, j)
                act.wait_ge(sem("al_ready"), s00 + AHEAD)
                for q in range(CHUNKS):
                    j0 = AHEAD - 1 if q == 0 else 0
                    if q == CHUNKS - 1:
                        act.wait_ge(sem("table_done"), t0 + CHUNKS * STEPS)
                        act.wait_ge(sem("al_ready"), s00 + STEPS * q)
                        act.dma_start(X[:], x_scr).then_inc(sem("x_back"), 16)
                        act.dma_start(ROWS[:], rows_in[2 * l + 1].partition_broadcast(P)).then_inc(sem("x_back"), 16)
                    with act.Fori(0, (STEPS - 1 - j0) // 2 - (q == 0)) as it:
                        for j in (j0, j0 + 1):
                            dense_step(q, j, it)
                    for j in range(STEPS - 3 if q == 0 else STEPS - 2, STEPS):
                        dense_step(q, j)
                nxt[0] = d0 + N_DENSE
                hi_to(d0 + N_DENSE + 2)
                act.wait_ge(sem("ln_var"), 2 * l + 2)
                rstd(SMALL[:, 60:62], SMALL[:, 56:60].rearrange("p (t k) -> p t k", k=2)[:, :, 1], 1, LN_EPS, sem("ln_rstd"))

        def attention_dve(dve, v, g0, heads, scale, PM=PM, between=lambda n: None):
            def head_max(n):
                g = g0 + n
                c = 16 + 8 * (g % 2)
                dve.wait_ge(sem("sc_done"), g + 1)
                v.step(dve.tensor_reduce(SMALL[:, c:c + 2], M[g % 2][:].rearrange("p (q k) -> p q k", q=2), AX.X, ALU.max))
                v.step(dve.tensor_scalar(SMALL[:, c + 2:c + 4], SMALL[:, c:c + 2], -scale, None, ALU.mult), sem("nb_ready"))

            def head_scale(n):
                g = g0 + n
                c = 16 + 8 * (g % 2)
                dve.wait_ge(sem("exp_ready"), g + 1)
                v.step(dve.reciprocal(SMALL[:, c + 6:c + 8], SMALL[:, c + 4:c + 6]))
                for qt in range(2):
                    ins = dve.tensor_scalar(PM[:, g % 2, qt, :], PM[:, g % 2, qt, :], SMALL[:, c + 6 + qt:c + 7 + qt], None, ALU.mult)
                v.step(ins, sem("sm_ready"))

            head_max(0)
            for n in range(heads):
                if n + 1 < heads:
                    head_max(n + 1)
                head_scale(n)
                between(n)

        @block.vector
        def _(dve):
            v = Steps(dve, sem("dve_step"))
            nxt = [0]

            def lo(i, it=0):
                dve.wait_ge(hi_ready, i + 1 + it * 4)
                dve.tensor_tensor(LO[i % SLOTS][:], RAW[:, i % SLOTS, :], HI[i % SLOTS][:].bitcast(F32), ALU.subtract).then_inc(lo_ready, 1)

            def lo_to(n):
                while nxt[0] < min(n, N_HP):
                    lo(nxt[0])
                    nxt[0] += 1

            def xl_evict(inst, gain=None):
                for kp in range(4):
                    dve.wait_ge(sem("xh_ready"), 4 * inst + kp + 1)
                    hi_ = XH[:, 2 * kp:2 * kp + 2, :].bitcast(F32)
                    if gain is None:
                        ins = dve.tensor_tensor(flat(XL[:, 2 * kp:2 * kp + 2, :]), M[kp][:], flat(hi_), ALU.subtract)
                    else:
                        for j in range(2):
                            ins = dve.scalar_tensor_tensor(out=XL[:, 2 * kp + j, :], in0=M[kp][:, 256 * j:256 * j + 256],
                                                           scalar=gain(2 * kp + j), in1=hi_[:, j, :], op0=ALU.mult, op1=ALU.subtract)
                    v.mark(ins, sem("xl_ready"))

            def norm_rows(dst, inst):
                dve.wait_ge(sem("row_rstd"), inst)
                for tt in range(TT):
                    ins = dve.tensor_scalar(dst[:, tt, :], X[:, tt, :], SMALL[:, 2 + tt:3 + tt], None, ALU.mult)
                v.mark(ins, sem("rows_ready"))

            def residual(h):
                for u in range(4):
                    i = h + u
                    if u >= 2:
                        lo_to(h + 4 + u - 1)
                    dve.wait_ge(hp_used, i + 1)
                    xv = X[:, :, 256 * u:256 * u + 256]
                    dve.tensor_tensor(xv, xv, PS[i % 4][:].rearrange("p (t n) -> p t n", t=2), ALU.add).then_inc(bank_free[i % 4], 1)
                for u in range(4):
                    evicted(dve, h + u)

            dve.wait_ge(sem("cst_loaded"), 48)
            v.step(dve.tensor_tensor(LBS[:, 8:12], LBS[:, 0:4], LBS[:, 4:8], ALU.max))
            v.step(dve.tensor_tensor(LBS[:, 0:4], LBS[:, 0:4], LBS[:, 8:12], ALU.subtract))
            v.step(dve.tensor_tensor(LBS[:, 4:8], LBS[:, 4:8], LBS[:, 8:12], ALU.subtract), sem("lb_shifted"))
            dve.wait_ge(sem("lb_exp"), 1)
            v.step(dve.tensor_tensor(LBS[:, 8:12], LBS[:, 0:4], LBS[:, 4:8], ALU.add))
            v.step(dve.reciprocal(LBS[:, 8:12], LBS[:, 8:12]))
            v.step(dve.tensor_tensor(LBS[:, 0:4], LBS[:, 0:4], LBS[:, 8:12], ALU.mult))
            v.step(dve.tensor_tensor(LBS[:, 4:8], LBS[:, 4:8], LBS[:, 8:12], ALU.mult))
            v.step(dve.tensor_tensor(LBS[:, 4:8], LBS[:, 4:8], LBS[:, 0:4], ALU.add))
            lb4 = [LB[:, l, :, :, 0].rearrange("p a b -> p a b") for l in range(DEPTH)]
            p4 = [LBS[:, 4 * l:4 * l + 4].rearrange("p (a b) -> p a b", b=2) for l in range(DEPTH)]
            for l in range(DEPTH):
                v.step(dve.tensor_tensor(lb4[l], p4[l], p4[0], ALU.subtract))
                v.step(dve.tensor_scalar(LB[:, l, :, :, 1], lb4[l], -1.0, 1.0, ALU.mult, ALU.add))
            dve.memset(UP[:], 0.0).then_inc(sem("hid_ready"), 2)

            lo_to(2)
            xl_evict(0)
            lo_to(4)
            for l in range(DEPTH):
                h0 = HP_FIRST[l]
                if l == 0:
                    lo_to(h0 + 2)
                norm_rows(XS, 2 * l + 1)
                xl_evict(1 + 2 * l, lambda k: par(l, "norm_mix", k))
                lo_to(h0 + 7)
                dve.wait_ge(sem("gates_ready"), 3 * l + 2)
                for d in range(2):
                    for ht in range(2):
                        c = slice(256 * ht, 256 * ht + 256)
                        lb, om = LB[:, l, d, ht, 0:1], LB[:, l, d, ht, 1:2]
                        v.mark(dve.tensor_scalar(F[:, d, c], E[:, d, c], om, lb, ALU.mult, ALU.add))
                        v.step(dve.tensor_scalar(KG[:, d, c], E[:, d, c], -1.0, 1.0, ALU.mult, ALU.add))
                        v.step(dve.tensor_scalar(KG[:, d, c], KG[:, d, c], om, None, ALU.mult))
                lo_to(h0 + 9)
                evicted(dve, h0 + 1)
                dve.wait_ge(sem("vt_ready"), l + 1)
                v.step(dve.memset(ACC[:], 0.0))

                def conv_gate():
                    evicted(dve, h0 + 5)
                    dve.wait_ge(sem("gates_ready"), 3 * l + 3)
                    if l > 0:
                        v.step(dve.memset(UP[:], 0.0))
                    v.step(dve.tensor_tensor(UP[:, :, CONV_PAD:CONV_PAD + TOK], AC[:].rearrange("p (a t) -> p a t", a=2),
                                             EG[:].rearrange("p (a t) -> p a t", a=2), ALU.mult), sem("up_ready"))

                def lag_value(n):
                    d, g = divmod(n, CHUNK)
                    dve.wait_ge(sem("lag_done"), 2 * CHUNK * l + n + 1)
                    here, there = (slice(g, 16), slice(0, 16 - g)) if d == 0 else (slice(0, 16 - g), slice(g, 16))
                    return v.mark(dve.tensor_tensor(v16(TB[:])[:, :, here], v16(M[n % 2][:])[:, :, here], v16(VT[:])[:, :, there], ALU.mult)), here

                def lag_sum(value):
                    count, here = value
                    dve.wait_ge(sem("dve_step"), count)
                    return v.mark(dve.tensor_tensor(v16(ACC[:])[:, :, here], v16(ACC[:])[:, :, here], v16(TB[:])[:, :, here], ALU.add))

                for n in range(2 * CHUNK):
                    d, g = divmod(n, CHUNK)
                    f, k, w = v16(F[:, d, :]), v16(KG[:, d, :]), v16(W[:])
                    if n == 3:
                        conv_gate()
                    lo_to(h0 + (9 if n < 2 else 10 if n < 9 else N_IN + N_OUT))
                    here, there = (slice(g, 16), slice(0, 16 - g)) if d == 0 else (slice(0, 16 - g), slice(g, 16))
                    if n >= 1:
                        dve.wait_ge(sem("lagx_ready"), 2 * CHUNK * l + n)
                    if g == 0:
                        decayed = v.mark(dve.tensor_copy(W[:], Q[:]))
                    else:
                        fs = slice(1, 17 - g) if d == 0 else slice(g - 1, 15)
                        decayed = v.mark(dve.tensor_tensor(w[:, :, here], w[:, :, here], f[:, :, fs], ALU.mult))
                    if n >= 2:
                        dve.wait_ge(sem("dve_step"), summed)
                    if n >= 1:
                        value = lag_value(n - 1)
                    dve.wait_ge(sem("dve_step"), decayed)
                    v.mark(dve.tensor_tensor(v16(XX[:, n % 2, :])[:, :, here], w[:, :, here], k[:, :, there], ALU.mult), sem("lagx_ready"))
                    if n >= 1:
                        summed = lag_sum(value)
                    if g == CHUNK - 1:
                        e = f[:, :, 0:1] if d == 0 else f[:, :, 15:16]
                        v.step(dve.tensor_tensor(v16(QB[:, d, :]), w, e.to_broadcast([P, 32, 16]), ALU.mult))
                value = lag_value(2 * CHUNK - 1)
                dve.wait_ge(sem("dve_step"), summed)
                lag_sum(value)
                dve.wait_ge(sem("diag_used"), 2 * CONV_K * (l + 1))
                for ct in range(2):
                    c = slice(256 * ct, 256 * ct + 256)
                    v.step(dve.tensor_scalar(AC[:, c], M[2][:, c], par(l, "cb", ct), None, ALU.add), sem("cy0_ready"))
                keys_end, decays = [XX[:, 0, :], TB[:]], [SCN, W]
                for d in range(2):
                    f, k, ke, dc = v16(F[:, d, :]), v16(KG[:, d, :]), v16(keys_end[d]), decays[d]
                    keep, edge = ("notlast", "last") if d == 0 else ("notfirst", "first")
                    bc = [P, 32, 16]
                    v.mark(dve.tensor_tensor(v16(E[:, 0, :]), f, cst(keep).unsqueeze(1).to_broadcast(bc), ALU.mult))
                    v.step(dve.tensor_tensor(v16(E[:, 1, :]), f, cst(edge).unsqueeze(1).to_broadcast(bc), ALU.mult))
                    if d == 0:
                        pp = E[:].ap[0]
                        back = [bass.AP(E, 2 * TOK * j + 2 * TOK - 1, [list(pp), [-1, 2 * TOK]]) for j in range(2)]
                        o = bass.AP(dc, 2 * TOK - 1, [list(dc[:].ap[0]), [-1, 2 * TOK]])
                    else:
                        back, o = [E[:, 0, :], E[:, 1, :]], dc[:]
                    v.step(dve.tensor_tensor_scan(o, back[0], back[1], 0.0, ALU.mult, ALU.add))
                    s = v16(dc[:])
                    if d == 0:
                        v.mark(dve.tensor_tensor(ke[:, :, 0:15], k[:, :, 0:15], s[:, :, 1:16], ALU.mult))
                        v.step(dve.tensor_copy(ke[:, :, 15:16], k[:, :, 15:16]), sem("ke_ready"))
                    else:
                        v.mark(dve.tensor_tensor(ke[:, :, 1:16], k[:, :, 1:16], s[:, :, 0:15], ALU.mult))
                        v.step(dve.tensor_copy(ke[:, :, 0:1], k[:, :, 0:1]), sem("ke_ready"))
                for d in range(2):
                    first = 0 if d == 0 else NCH - 1
                    last = [v.mark(dve.memset(ST[d][:, :, first, :], 0.0))] * 2
                    dec = decays[d][:].rearrange("p (h n c) -> p h n c", h=2, c=CHUNK)[:, :, :, 0 if d == 0 else 15]
                    for n, tt in enumerate((0, 1) if d == 0 else (1, 0)):
                        dve.wait_ge(sem("u_done"), 8 * l + 4 * d + 2 * n + 2)
                        for c in range(8) if d == 0 else range(7, -1, -1):
                            ch = 8 * tt + c
                            to = ch + 1 if d == 0 else ch - 1
                            if 0 <= to < NCH:
                                for ht in range(2):
                                    dve.wait_ge(sem("dve_step"), last[ht])
                                    last[ht] = v.mark(dve.scalar_tensor_tensor(
                                        out=ST[d][:, ht, to, :], in0=ST[d][:, ht, ch, :], scalar=dec[:, ht, ch:ch + 1],
                                        in1=UB[d][2 * n + ht][:, 64 * c:64 * c + 64], op0=ALU.mult, op1=ALU.add))
                    dve.wait_ge(sem("dve_step"), last[1])
                    v.step(dve.memset(SMALL[:, 41:42], 0.0), sem("state_ready"))
                for i in (7, 8, 9):
                    evicted(dve, h0 + i)
                v.step(dve.tensor_tensor(flat(QK2[:]), flat(QK[:]), flat(QK[:]), ALU.mult), sem("qsq_ready"))
                dve.wait_ge(sem("csum_done"), l + 1)
                for ct in range(2):
                    c = slice(256 * ct, 256 * ct + 256)
                    v.step(dve.scalar_tensor_tensor(out=W[:, c], in0=PS[1][:, 0:256], scalar=-1.0 / 256, in1=AC[:, c], op0=ALU.mult, op1=ALU.add))
                    v.step(dve.tensor_tensor(EG[:, c], W[:, c], W[:, c], ALU.mult), sem("csq_ready"))
                dve.wait_ge(sem("qrs_ready"), 3 * l + 3)
                v.mark(dve.scalar_tensor_tensor(out=flat(QK2[:, 0:4, :]), in0=flat(QK[:, 0:4, :]), scalar=par(l, "qg"), in1=flat(QK3[:, 0:4, :]),
                                                op0=ALU.mult, op1=ALU.mult))
                v.step(dve.scalar_tensor_tensor(out=QK2[:, 4, :], in0=QK[:, 4, :], scalar=par(l, "kg"), in1=QK3[:, 4, :],
                                                op0=ALU.mult, op1=ALU.mult), sem("qn_ready"))
                v.step(dve.tensor_tensor(QK3[:], QK2[:], cst("cos").unsqueeze(1).to_broadcast([P, 5, TOK]), ALU.mult))
                dve.wait_ge(sem("inter_done"), 2 * l + 2)
                v.step(dve.tensor_tensor(ACC[:], ACC[:], M[0][:], ALU.add))
                v.step(dve.tensor_tensor(XX[:, 0, :], ACC[:], ACC[:], ALU.mult), sem("hsq_ready"))
                for j in range(3):
                    n = 2 if j < 2 else 1
                    dve.wait_ge(sem("rot_done"), 3 * l + j + 1)
                    v.step(dve.tensor_tensor(QK[:, 2 * j:2 * j + n, :], M[1 + j][:, 0:256 * n].rearrange("p (a t) -> p a t", t=TOK),
                                             cst("sin").unsqueeze(1).to_broadcast([P, n, TOK]), ALU.mult))
                v.step(dve.tensor_tensor(flat(QK[:]), flat(QK[:]), flat(QK3[:]), ALU.add), sem("qk_ready"))

                def mix_low(a, b, n):
                    dve.wait_ge(sem("mixh_ready"), n)
                    v.step(dve.tensor_tensor(flat(XL[:, a:b, :]), flat(MIXF[:, a:b, :]), flat(XH[:, a:b, :].bitcast(F32)), ALU.subtract), sem("mixl_ready"))

                def other_outputs(n):
                    if n == 1:
                        dve.wait_ge(sem("hrs_ready"), l + 1)
                        v.step(dve.tensor_tensor(SCN[:], SCN[:], GT[:], ALU.mult))
                        for ht in range(2):
                            c = slice(256 * ht, 256 * ht + 256)
                            v.step(dve.scalar_tensor_tensor(out=ACC[:, c], in0=ACC[:, c], scalar=par(l, "ng", ht), in1=TB[:, c],
                                                            op0=ALU.mult, op1=ALU.mult))
                        v.step(dve.tensor_tensor(flat(MIXF[:, 4:6, :]), ACC[:], SCN[:], ALU.mult))
                    elif n == 2:
                        dve.wait_ge(sem("crs_ready"), l + 1)
                        for ct in range(2):
                            c = slice(256 * ct, 256 * ct + 256)
                            v.step(dve.scalar_tensor_tensor(out=W[:, c], in0=W[:, c], scalar=par(l, "lng", ct), in1=XX[:, 1, 0:256],
                                                            op0=ALU.mult, op1=ALU.mult))
                            ins = dve.tensor_scalar(AC[:, c], W[:, c], par(l, "lnb", ct), None, ALU.add)
                            if ct == 0:
                                v.step(ins)
                            else:
                                v.step(ins, sem("cy_ready"))
                    elif n == 5:
                        dve.wait_ge(sem("ceg_ready"), l + 1)
                        v.step(dve.tensor_tensor(flat(MIXF[:, 6:8, :]), AC[:], EG[:], ALU.mult), sem("mix_ready"))
                    elif n == 7:
                        mix_low(4, 8, 2 * l + 1)

                lo_to(h0 + N_IN + N_OUT)
                attention_dve(dve, v, 8 * l, 8, HEAD ** -0.5, between=other_outputs)
                mix_low(0, 4, 2 * l + 2)
                residual(h0 + N_IN)
                h1 = h0 + N_IN + N_OUT
                norm_rows(XS2, 2 * l + 2)
                xl_evict(2 + 2 * l, lambda k: par(l, "norm_mlp", k))
                lo_to(h1 + 3)
                with dve.Fori(0, N_UP // 4) as it:
                    for u in range(4):
                        lo(h1 + u + 3, it)
                        dve.wait_ge(bank_free[(h1 + u) % 4], reads_before(h1 + u) + 1 + it)
                        dve.tensor_tensor(SQ[:], RB[:, u % 2, :], RB[:, u % 2, :], ALU.mult).then_inc(sem("hsq2"), 1)
                        dve.wait_ge(sem("hsq2"), 16 * l + u + 1 + it * 4)
                        dve.wait_ge(sem("sq_ready"), 16 * l + u + 1 + it * 4)
                        at_ = bass.ds(it * 8 + 2 * u, 2)
                        dve.tensor_tensor(flat(HL[:, at_, :]), SQ[:], flat(HH[:, at_, :].bitcast(F32)), ALU.subtract)\
                           .then_inc(sem("hid_ready"), 1)
                        dve.wait_ge(sem("hid_ready"), 16 * l + u + 3 + it * 4)
                nxt[0] = h1 + N_UP + 3
                lo_to(h1 + N_UP + N_DOWN + 2)
                residual(h1 + N_UP + N_DOWN - 4)
            STATS = SMALL[:, 64:112].rearrange("p (t c k) -> p t c k", t=TT, k=6)

            def layer_norm(n, chunks):
                for tt in range(TT):
                    ins = dve.bn_aggr(SMALL[:, 56 + 2 * tt:58 + 2 * tt], STATS[:, tt, 0:chunks, :])
                v.step(ins, sem("ln_var"))
                for tt in range(TT):
                    ins = dve.scalar_tensor_tensor(out=X[:, tt, :], in0=X[:, tt, :], scalar=SMALL[:, 56 + 2 * tt:57 + 2 * tt], in1=ROWS[:, 0, :],
                                                   op0=ALU.subtract, op1=ALU.mult)
                v.step(ins)
                dve.wait_ge(sem("ln_rstd"), n)
                for tt in range(TT):
                    ins = dve.scalar_tensor_tensor(out=X[:, tt, :], in0=X[:, tt, :], scalar=SMALL[:, 60 + tt:61 + tt], in1=ROWS[:, 1, :],
                                                   op0=ALU.mult, op1=ALU.add)
                v.step(ins, sem("x_ready"))

            def best16(values, spare, top_, idx, groups):
                for g in range(groups):
                    ins = dve.max(top_(g)[:, 0:8], values(g))
                v.step(ins)
                for g in range(groups):
                    dve.max_index(idx(g)[:, 0:8], top_(g)[:, 0:8], values(g))
                    ins = dve.match_replace(spare(g), top_(g)[:, 0:8], values(g), -3.0e38)
                v.step(ins)
                for g in range(groups):
                    ins = dve.max(top_(g)[:, 8:16], spare(g))
                v.step(ins)
                for g in range(groups):
                    ins = dve.max_index(idx(g)[:, 8:16], top_(g)[:, 8:16], spare(g))
                v.step(ins)

            k96 = slice(0, GLA_K)
            v.mark(dve.memset(SMALL[:, 43:44], 0.0), sem("x_ready"))
            for l in range(DEPTH):
                s0 = HP_SECOND[l]
                xl_evict(5 + 2 * l)
                lo_to(HP_SHARED + 2 if l > 0 else s0 + 3)
                if l == 0:
                    lo_to(s0 + 7)
                    dve.wait_ge(sem("mix_loaded0"), 64)
                    dve.wait_ge(sem("gpre_done"), 1)
                    for h in range(4):
                        ins = dve.tensor_scalar(LG[k96, h, :], M[h // 2][k96, 256 * (h % 2):256 * (h % 2) + 256], P2[k96, h:h + 1], 0.0, ALU.add, ALU.min)
                    v.step(ins, sem("gpre_read"))
                    v.step(dve.tensor_copy(flat(SM[:]).rearrange("p (n c) -> p n c", c=GLA_C), cst("gscan").unsqueeze(1).to_broadcast([P, 16, GLA_C])))
                    dve.wait_ge(sem("lsig_ready"), 1)
                    v.step(dve.tensor_tensor(flat(LG[k96]), flat(LG[k96]), flat(EXA[k96]), ALU.subtract))
                    v.step(dve.tensor_tensor_scan(flat(B[k96]), flat(SM[k96]), flat(LG[k96]), 0.0, ALU.mult, ALU.add))
                    bc = B[k96].rearrange("p h (n c) -> p (h n) c", c=GLA_C)
                    v.step(dve.tensor_tensor(KE[k96].rearrange("p h (n c) -> p (h n) c", c=GLA_C),
                                             bc[:, :, GLA_C - 1].unsqueeze(2).to_broadcast([GLA_K, 16, GLA_C]), bc, ALU.subtract), sem("cum_ready"))
                    lo_to(s0 + 8)
                    dve.wait_ge(sem("gexp_ready"), 1)
                    v.mark(dve.tensor_tensor(flat(KE[k96]), flat(KE[k96]), flat(GK[k96]), ALU.mult))
                    v.mark(dve.tensor_tensor(flat(KTD[k96]), flat(EXB[k96]), flat(GK[k96]), ALU.mult))
                    v.step(dve.scalar_tensor_tensor(out=flat(QTD[k96]), in0=flat(GQ[k96]), scalar=GLA_K ** -0.5, in1=flat(EXA[k96]),
                                                    op0=ALU.mult, op1=ALU.mult), sem("gqk_ready"))
                p0 = s0 + (6 if l == 0 else 1)
                lo_to(p0 + 3)
                attention_dve(dve, v, 16 + 4 * l, MEM_H, HEAD ** -0.5, PM2, between=lambda n: lo_to(p0 + 4 + n))

                def mix_low(a, b, n):
                    dve.wait_ge(sem(f"mix_high{l}"), n)
                    v.mark(dve.tensor_tensor(flat(XL[:, a:b, :]), flat(MIX2[:, a:b, :]), flat(XH[:, a:b, :].bitcast(F32)), ALU.subtract))

                if l == 0:
                    lo_to(s0 + N_MIX2[l])
                    mix_low(6, 8, 1)
                    dve.wait_ge(sem("gatt_done"), 1)
                    cm = cst("causal").unsqueeze(1).to_broadcast([P, 8, GLA_C])
                    v.step(dve.scalar_tensor_tensor(out=ATT[:], in0=cm, scalar=3.0e38, in1=M[0][:].rearrange("p (a c) -> p a c", c=GLA_C),
                                                    op0=ALU.mult, op1=ALU.min))
                    v.step(dve.scalar_tensor_tensor(out=ATT[:], in0=cm, scalar=-3.0e38, in1=ATT[:], op0=ALU.mult, op1=ALU.max), sem("gattm_ready"))
                    for ch in range(3):
                        dve.wait_ge(sem("uc_done"), ch + 1)
                        if ch > 0:
                            dve.wait_ge(sem("oc_done"), ch + 1)
                        for h in range(4):
                            u_ = UC[ch % 2][h // 2][k96, GLA_V * (h % 2):GLA_V * (h % 2) + GLA_V]
                            if ch == 0:
                                ins = dve.tensor_copy(STA[k96, h, :], u_)
                            else:
                                ins = dve.scalar_tensor_tensor(out=STA[k96, h, :], in0=STA[k96, h, :], scalar=BL[k96, 4 * h + ch:4 * h + ch + 1],
                                                               in1=u_, op0=ALU.mult, op1=ALU.add)
                        v.step(ins, sem("sta_ready"))
                    dve.wait_ge(sem("rsig_ready"), 1)
                    v.step(dve.tensor_tensor(flat(RG[:]), flat(RG[:]), flat(GR[:]), ALU.mult))
                    dve.wait_ge(sem("go_ready"), 4)
                    v.step(dve.tensor_tensor(flat(GO2[:]), flat(GO[:]), flat(RG[:]), ALU.mult))
                    dve.wait_ge(sem("grs_ready"), 1)
                    go = GO2[:].rearrange("p t (h c) -> p (t h) c", h=4)
                    v.step(dve.tensor_tensor(go, go, SMALL[:, 48:56].unsqueeze(2).to_broadcast([P, 8, GLA_V]), ALU.mult), sem("gon_ready"))
                else:
                    dve.wait_ge(sem("mix_loaded1"), 48)

                    def slot_max(n):
                        dve.wait_ge(sem("dsc_done"), n + 1)
                        c = 48 + 2 * (n % 2)
                        for g in range(2):
                            w = slice(0, 512) if g == 0 else slice(512, 768)
                            ins = dve.tensor_tensor(S3[:, n % 2, w], M[g][:, 0:w.stop - w.start], DM[:, n % 2, w], ALU.add)
                        v.step(ins, sem("dsc_read"))
                        v.step(dve.tensor_reduce(SMALL[:, 52:53], S3[:, n % 2, :], AX.X, ALU.max))
                        v.step(dve.tensor_scalar(SMALL[:, c:c + 1], SMALL[:, 52:53], -KEYS ** -0.5, None, ALU.mult), sem("dnb_ready"))

                    def slot_sum(n):
                        dve.wait_ge(sem("dexp_ready"), n + 1)
                        if n >= 4 and n % 2 == 0:
                            dve.wait_ge(sem("dpt_done"), n // 2 - 1)
                        c = 49 + 2 * (n % 2)
                        o = PD[:, (n // 2) % 2, n % 2, :]
                        v.mark(dve.reciprocal(SMALL[:, 53:54], SMALL[:, c:c + 1]))
                        v.step(dve.tensor_tensor(S3[:, n % 2, 0:256], S3[:, n % 2, 0:256], S3[:, n % 2, 256:512], ALU.add))
                        v.step(dve.tensor_tensor(S3[:, n % 2, 0:256], S3[:, n % 2, 0:256], S3[:, n % 2, 512:768], ALU.add))
                        v.step(dve.tensor_scalar(o, S3[:, n % 2, 0:256], SMALL[:, 53:54], None, ALU.mult), sem("dsm_ready"))

                    lo_to(s0 + 9)
                    slot_max(0)
                    for n in range(2 * SLOT_H):
                        if n == 4:
                            lo_to(s0 + N_MIX2[l])
                        if n + 1 < 2 * SLOT_H:
                            slot_max(n + 1)
                        slot_sum(n)
                lo_to(s0 + N_MIX2[l] + 3)
                if l == 0:
                    for kt in range(6):
                        if kt % 2 == 0:
                            dve.wait_ge(sem("mix_high0"), kt // 2 + 2)
                        v.mark(dve.scalar_tensor_tensor(out=XL[:, kt, :], in0=M[kt // 2][:, 256 * (kt % 2):256 * (kt % 2) + 256], scalar=P2[:, 4 + kt:5 + kt],
                                                        in1=XH[:, kt, :].bitcast(F32), op0=ALU.mult, op1=ALU.subtract))
                else:
                    mix_low(0, SLOT_H - 1, 1)
                    mix_low(6, 8, 2)
                    mix_low(SLOT_H - 1, SLOT_H, 3)
                dve.wait_ge(sem("dve_step"), v.count["dve_step"])
                v.step(dve.memset(SMALL[:, 46:47], 0.0), sem("mix2l_ready"))
                w0 = s0 + N_MIX2[l] + N_OUT
                lo_to(w0)
                for u in range(4):
                    i = s0 + N_MIX2[l] + u
                    if u >= 2:
                        lo_to(w0 + u - 1)
                    dve.wait_ge(hp_used, i + 1)
                    xv = X[:, :, 256 * u:256 * u + 256]
                    dve.scalar_tensor_tensor(out=xv, in0=xv, scalar=DN_ALPHA, in1=PS[i % 4][:].rearrange("p (t n) -> p t n", t=2),
                                             op0=ALU.mult, op1=ALU.add).then_inc(bank_free[i % 4], 1)
                    evicted(dve, i)
                    for tt in range(TT):
                        ins = dve.bn_stats(STATS[:, tt, u, :], X[:, tt, 256 * u:256 * u + 256])
                v.step(ins)
                layer_norm(2 * l + 1, 4)
                xl_evict(6 + 2 * l)
                lo_to(w0 + 3)
                d0 = w0 + N_WQ
                if l == 0:
                    v.step(dve.tensor_copy(IOT[:], cst("iota").unsqueeze(2).to_broadcast([P, KEYS, TPS])))
                for h in range(PH):
                    lo_to(min(w0 + h + 6, d0))
                    dve.wait_ge(sem("keysc_ready"), PH * l + h + 1)
                    sc, ts, ti, s2 = (t[:, :, 2 * h:2 * h + 2, :] for t in (SC, TS, TI, S2))
                    best16(lambda g: sc[:, g // 2, g % 2, :], lambda g: s2[:, g // 2, g % 2, :],
                           lambda g: ts[:, g // 2, g % 2, :], lambda g: ti[:, g // 2, g % 2, :], 4)
                v.mark(dve.tensor_copy(TF[:].rearrange("p a b c -> p (a b c)"), TI[:].rearrange("p a b c -> p (a b c)")), sem("tf_ready"))
                for tt in range(TT):
                    two = TS[:, tt].rearrange("p (h s) k -> p h s k", s=2)
                    for a0, a1, b1, c0 in ((0, FULL, TOPK, 0), (FULL, TOPK, NARROW, FULL * TOPK)):
                        shape = [P, PH, a1 - a0, b1]
                        ins = dve.tensor_tensor(CD[:, tt, :, c0:c0 + (a1 - a0) * b1].rearrange("p h (i j) -> p h i j", j=b1),
                                                two[:, :, 0, a0:a1].unsqueeze(3).to_broadcast(shape),
                                                two[:, :, 1, 0:b1].unsqueeze(2).to_broadcast(shape), ALU.add)
                v.step(ins)
                for tt in range(TT):
                    best16(lambda g: CD[:, tt, g, :], lambda g: CD2[:, g, :], lambda g: BS[:, PH * tt + g, :], lambda g: BJ[:, tt, g, :], PH)
                v.step(dve.tensor_tensor(GX[:], BS[:], BS[:, :, 0:1].to_broadcast([P, TT * PH, TOPK]), ALU.subtract), sem("gx_shifted"))
                bj = BJ[:].rearrange("p a b c -> p (a b c)")
                for j, (n, op) in enumerate(((4, ALU.logical_shift_right), (TOPK - 1, ALU.bitwise_and), (2, ALU.logical_shift_right), (NARROW - 1, ALU.bitwise_and))):
                    ins = dve.tensor_scalar(BK[:, j, :], bj, n, None, op)
                v.step(ins)
                v.step(dve.tensor_copy(flat(BF[:]), flat(BK[:])))
                v.mark(dve.tensor_scalar(WIDE[:], BF[:, 2, :], FULL * TOPK / NARROW, None, ALU.is_ge))
                v.mark(dve.tensor_tensor(BF[:, 3, :], BF[:, 3, :], BF[:, 1, :], ALU.subtract))
                v.step(dve.scalar_tensor_tensor(out=BF[:, 2, :], in0=BF[:, 2, :], scalar=FULL * TOPK / NARROW - FULL, in1=BF[:, 0, :],
                                                op0=ALU.subtract, op1=ALU.subtract))
                v.step(dve.tensor_tensor(BF[:, 2:4, :], BF[:, 2:4, :], WIDE[:].unsqueeze(1).to_broadcast([P, 2, TT * PH * TOPK]), ALU.mult))
                v.step(dve.tensor_tensor(JF[:].rearrange("p s g k -> p s (g k)"), BF[:, 0:2, :], BF[:, 2:4, :], ALU.add))
                for side in range(2):
                    bc = [P, TT * PH, TOPK, TOPK]
                    v.step(dve.tensor_tensor(EQ[:], IOT[:, 0:TOPK, :].unsqueeze(1).to_broadcast(bc), JF[:, side].unsqueeze(2).to_broadcast(bc), ALU.is_equal))
                    dve.wait_ge(sem("tfx_ready"), 4 * l + 2 * side + 2)
                    v.step(dve.tensor_tensor(EQ[:], EQ[:], TFX[:, side], ALU.mult))
                    for n in (8, 4, 2):
                        v.step(dve.tensor_tensor(EQ[:, :, 0:n, :], EQ[:, :, 0:n, :], EQ[:, :, n:2 * n, :], ALU.add))
                    v.step(dve.tensor_tensor(SEL[:, side].rearrange("p t (h k) -> p (t h) k", k=TOPK), EQ[:, :, 0, :], EQ[:, :, 1, :], ALU.add))
                dve.wait_ge(sem("gx_ready"), l + 1)
                v.step(dve.tensor_reduce(GSUM[:], GX[:], AX.X, ALU.add))
                v.step(dve.reciprocal(GSUM[:], GSUM[:]))
                v.step(dve.tensor_tensor(SEL[:, 2].rearrange("p t (h k) -> p (t h) k", k=TOPK), GX[:],
                                         GSUM[:].unsqueeze(2).to_broadcast([P, TT * PH, TOPK]), ALU.mult), sem("sel_ready"))
                dve.wait_ge(sem("pf_ready"), l + 1)
                for c in range(3):
                    v.step(dve.tensor_copy(GS[:, c, :], PF[:]))
                    if c < 2:
                        v.step(dve.tensor_tensor(PF[:], PF[:], GS[:, c, :], ALU.subtract))

                dve.wait_ge(lo_ready, d0 + AHEAD)
                nxt[0] = d0 + AHEAD
                lo_to(d0 + AHEAD + 3)

                t0, s00 = (CHUNKS * STEPS) * l, PAIRS * l

                def one_hots(q, k, it=0, per=2):
                    n = t0 + STEPS * q + k
                    spare = q == 0 and k % 2 == 0
                    if n > t0 + 1:
                        dve.wait_ge(sem("table_done"), (n - 1 if q == 0 else n) + it * per)
                    oa, ob = (OA2, OB2) if spare else (OA, OB)
                    t = bass.ds(it * (per * TPS) + TPS * k, TPS)
                    dve.tensor_tensor(EQB[:], IOT[:, BC * q:BC * q + BC, :], PB[:, 1, t].unsqueeze(1).to_broadcast([P, BC, TPS]),
                                      ALU.is_equal).then_inc(sem("eqb_ready"), 1)
                    dve.tensor_tensor(oa[:], IOT[:], PB[:, 0, t].unsqueeze(1).to_broadcast([P, KEYS, TPS]),
                                      ALU.is_equal).then_inc(sem("oa_ready"), 1)
                    dve.wait_ge(sem("eqb_ready"), n + 1 + it * per)
                    dve.tensor_tensor(ob[:], EQB[:].unsqueeze(1).to_broadcast([P, 3, BC, TPS]),
                                      GS[:, :, t].unsqueeze(2).to_broadcast([P, 3, BC, TPS]), ALU.mult).then_inc(sem("ob_ready"), 1)
                    dve.wait_ge(sem("ob_ready"), n + 1 + it * per)

                def product(s, q, k, it=0):
                    dve.wait_ge(sem("ge_ready"), s00 + s + 1 + it * 2)
                    if isinstance(it, int):
                        dve.wait_ge(sem("table_ready"), t0 + STEPS * (q + 1))
                    ge = GA[:, s, :] if s < AHEAD else GE[:, s % 2, :]
                    dve.tensor_tensor(ge, ge, flat(G[q % 2][:, bass.ds(it * 4 + 2 * k, 2), :]), ALU.mult).then_inc(sem("a_ready"), 1)
                    dve.wait_ge(sem("ah_ready"), s00 + s + 1 + it * 2)
                    dve.wait_ge(sem("a_ready"), s00 + s + 1 + it * 2)
                    dve.tensor_tensor(AL[s % 2][:], ge, AH[s % 2][:].bitcast(F32), ALU.subtract).then_inc(sem("al_ready"), 1)

                def dense_step(q, j, it=0):
                    s = STEPS * q + j
                    if s < AHEAD - 2:
                        lo(d0 + AHEAD + 3 + s)
                    elif s >= AHEAD - 1:
                        for n in (3, 4):
                            if 2 * s + n < N_DENSE:
                                lo(d0 + 2 * s + n, it)
                    if s + 1 < PAIRS:
                        product(s + 1, q + (j + 1) // STEPS, (j + 1) % STEPS, it)
                    if q == 0:
                        if AHEAD - 1 <= j < STEPS - 1:
                            for k in (2 * (j - AHEAD + 1) + 1, 2 * (j - AHEAD + 1) + 2):
                                one_hots(1 + k // STEPS, k % STEPS, it, 4)
                    else:
                        nq = q + 1 + (j + 1) // STEPS
                        if nq < CHUNKS:
                            one_hots(nq, (j + 1) % STEPS, it)

                for k in range(STEPS + 1):
                    if k == 1:
                        dve.wait_ge(sem("ge_ready"), s00 + AHEAD)
                    one_hots(k // STEPS, k % STEPS)
                product(0, 0, 0)
                for j in range(AHEAD - 1):
                    dense_step(0, j)
                for q in range(CHUNKS):
                    j0 = AHEAD - 1 if q == 0 else 0
                    with dve.Fori(0, (STEPS - 1 - j0) // 2 - (q == 0)) as it:
                        for j in (j0, j0 + 1):
                            dense_step(q, j, it)
                    for j in range(STEPS - 3 if q == 0 else STEPS - 2, STEPS):
                        dense_step(q, j)
                nxt[0] = d0 + N_DENSE
                lo_to(d0 + N_DENSE + 2)
                dve.wait_ge(sem("f_done"), l + 1)
                dve.wait_ge(sem("x_back"), 32 * (l + 1))
                for tt in range(TT):
                    for n in range(2):
                        xv = X[:, tt, 512 * n:512 * n + 512]
                        ins = dve.scalar_tensor_tensor(out=xv, in0=xv, scalar=DN_ALPHA, in1=M[2 * tt + n][:], op0=ALU.mult, op1=ALU.add)
                        count = v.mark(ins)
                for tt in range(TT):
                    for n in range(2):
                        dve.wait_ge(sem("dve_step"), count - 3 + 2 * tt + n)
                        ins = dve.bn_stats(STATS[:, tt, n, :], X[:, tt, 512 * n:512 * n + 512])
                v.step(ins)
                layer_norm(2 * l + 2, 2)
            v.step(dve.memset(SMALL[:, 45:46], 0.0), sem("x_final"))

        @block.gpsimd
        def _(pool):
            p = Steps(pool, sem("pool_step"))
            pool.wait_ge(sem("cst_loaded"), 48)
            for l in range(DEPTH):
                h0 = HP_FIRST[l]
                evicted(pool, h0)
                pool.wait_ge(sem("t_done"), 4 * (2 * l + 2))
                for tt in range(TT):
                    for h in range(4):
                        ins = pool.tensor_tensor(VX[:, tt, h, :, :], VR[:, tt, 64 * h:64 * h + 64].unsqueeze(1).to_broadcast([P, 8, HEAD]),
                                                 cst("chunkmask").unsqueeze(2).to_broadcast([P, 8, HEAD]), ALU.mult)
                p.mark(ins, sem("vx_ready"))
            for l in range(DEPTH):
                d0 = HP_DENSE[l]
                pool.wait_ge(lo_ready, d0)
                for i in range(d0, d0 + AHEAD):
                    pool.wait_ge(hi_ready, i + 1)
                    pool.tensor_tensor(LO[i % SLOTS][:], RAW[:, i % SLOTS, :], HI[i % SLOTS][:].bitcast(F32), ALU.subtract).then_inc(lo_ready, 1)

        @block.tensor
        def _(pe):
            def transposes(inst, src, ready):
                ready()
                for kp in range(4):
                    for j in range(2):
                        for tt in range(TT):
                            k = 2 * kp + j
                            ins = pe.transpose(M[kp][:, 256 * j + P * tt:256 * j + P * tt + P], src[:, tt, P * k:P * k + P], cst("ident"))
                    ins.then_inc(sem("t_done"), 1)

            def three(out_, ah, al, bh, bl, first, last, **kw):
                pe.matmul(out_, ah, bh, start=first, stop=False, **kw)
                pe.matmul(out_, ah, bl, start=False, stop=False, **kw)
                return pe.matmul(out_, al, bh, start=False, stop=last, **kw)

            def hp_wait(i, it=0, bank=True):
                pe.wait_ge(lo_ready, i + 1 + it * 4)
                if bank and reads_before(i) > 0:
                    pe.wait_ge(bank_free[i % 4], reads_before(i) + it)

            def half(i, modes, it=0, hh=XH, hl=XL, k0=0, first=True, last=True, between=lambda c: None, inst=None):
                hp_wait(i, it, first)

                def operand(start, k):
                    if inst is not None and start and k % 2 == 0:
                        pe.wait_ge(sem("xl_ready"), 4 * inst + k // 2 + 1)

                s, b = i % SLOTS, PS[i % 4]
                wh, wl = (t[s][:].rearrange("p (k n) -> p k n", k=KT) for t in (HI, LO))
                if modes == "rr":
                    for tt in range(TT):
                        for k in range(KT):
                            operand(tt == 0, k)
                            ins = three(b[:, 256 * tt:256 * tt + 256], hh[:, k0 + k, P * tt:P * tt + P], hl[:, k0 + k, P * tt:P * tt + P],
                                        wh[:, k, :], wl[:, k, :], first and k == 0 and (last or tt == 0), last and k == KT - 1, skip_group_check=not (first and last))
                else:
                    for c, mode in enumerate(modes):
                        if c == 1:
                            between(0)
                        n = slice(P * c, P * c + P)
                        if mode == "c":
                            for k in range(KT):
                                operand(c == 0, k)
                                ins = three(b[:, 256 * c:256 * c + 256], wh[:, k, n], wl[:, k, n], hh[:, k, :], hl[:, k, :], k == 0, k == KT - 1)
                        else:
                            for tt in range(TT):
                                for k in range(KT):
                                    ins = three(b[:, 256 * c + P * tt:256 * c + P * tt + P], hh[:, k, P * tt:P * tt + P], hl[:, k, P * tt:P * tt + P],
                                                wh[:, k, n], wl[:, k, n], k == 0, k == KT - 1)
                ins.then_inc(hp_used, 1)
                between(1)

            def attention_pe(g0, heads, q, k, val, part, PM=PM, PT=PT, panel=lambda n: None):
                def scores(n):
                    g = g0 + n
                    if n >= 2:
                        pe.wait_ge(sem("exp_ready"), g - 1)
                    for qt in range(2):
                        ins = pe.matmul(M[g % 2][:, 256 * qt:256 * qt + 256], q(n)[:, P * qt:P * qt + P], k(n), start=True, stop=True)
                    ins.then_inc(sem("sc_done"), 1)

                scores(0)
                scores(1)
                panel(0)
                for n in range(heads):
                    g = g0 + n
                    pe.wait_ge(sem("sm_ready"), g + 1)
                    if n >= 1:
                        pe.wait_ge(sem("pt_ready"), g)
                    for kt in range(2):
                        for qt in range(2):
                            ins = pe.transpose(M[2][:, 256 * kt + P * qt:256 * kt + P * qt + P], PM[:, g % 2, qt, P * kt:P * kt + P], cst("ident"))
                    ins.then_inc(sem("pt_done"), 1)
                    if n + 2 < heads:
                        scores(n + 2)
                    panel(n + 1)
                    pe.wait_ge(sem("pt_ready"), g + 1)
                    if n >= 1:
                        pe.wait_ge(sem("o_ready"), g)
                    o = part(n)
                    for kt in range(2):
                        ins = pe.matmul(M[3][o:o + 64, 0:256], val(n, kt), PT[:, g % 2, kt, :], start=(kt == 0), stop=(kt == 1))
                    ins.then_inc(sem("pv_done"), 1)

            pe.wait_ge(sem("cst_loaded"), 48)
            transposes(0, X, lambda: pe.wait_ge(sem("mem_loaded"), 16))
            for i in range(N_MEM):
                half(i, "cc" if i % 2 == 0 else "rr", inst=0 if i == 0 else None)
            for l in range(DEPTH):
                h0 = HP_FIRST[l]
                transposes(1 + 2 * l, XS, lambda: pe.wait_ge(sem("rows_ready"), 2 * l + 1))
                def lag(n):
                    d, g = divmod(n, CHUNK)
                    here = slice(g, 16) if d == 0 else slice(0, 16 - g)
                    pe.wait_ge(sem("lagx_ready"), 2 * CHUNK * l + n + 1)
                    pe.matmul(v16(M[n % 2][:])[:, :, here], cst("blk"), v16(XX[:, n % 2, :])[:, :, here], start=True, stop=True)\
                      .then_inc(sem("lag_done"), 1)

                def tap(n):
                    ct, k = divmod(n, CONV_K)
                    pe.wait_ge(sem("diag_ready"), 2 * CONV_K * l + n + 1)
                    pe.matmul(M[2][:, 256 * ct:256 * ct + 256], DG[:, n % 4, :], UP[:, ct, k:k + TOK], start=(k == 0), stop=(k == CONV_K - 1))\
                      .then_inc(sem("diag_used"), 1)

                for u in range(4):
                    half(h0 + u, "rr" if u == 0 else "cc", inst=2 * l + 1 if u == 0 else None)
                evicted(pe, h0)
                for ht in range(2):
                    for tt in range(TT):
                        ins = pe.transpose(M[0][:, 256 * ht + P * tt:256 * ht + P * tt + P], VR[:, tt, P * ht:P * ht + P], cst("ident"))
                ins.then_inc(sem("vt_done"), 1)
                half(h0 + 4, "cc")
                half(h0 + 5, "cc")
                pe.wait_ge(sem("vt_ready"), l + 1)
                for u in range(6, N_IN):
                    half(h0 + u, "cr" if u == 7 else "cc", between=lambda c: lag(2 * (u - 6) + c))
                pe.wait_ge(sem("up_ready"), l + 1)
                for n in range(2 * (N_IN - 6), 2 * CHUNK):
                    lag(n)
                    taps, lags = 2 * CONV_K, 2 * CHUNK - 2 * (N_IN - 6)
                    first = n - 2 * (N_IN - 6)
                    for m in range(taps * first // lags, taps * (first + 1) // lags):
                        tap(m)
                started = set()
                pe.wait_ge(sem("cy0_ready"), 2 * (l + 1))
                for d, ke in enumerate((XX[:, 0, :], TB[:])):
                    pe.wait_ge(sem("ke_ready"), 2 * l + d + 1)
                    for tt in range(TT):
                        for ht in range(2):
                            ins = pe.transpose(M[2 - d][:, 256 * tt + P * ht:256 * tt + P * ht + P], ke[:, 256 * ht + P * tt:256 * ht + P * tt + P], cst("ident"))
                    ins.then_inc(sem("kt_done"), 1)
                for u in range(N_IN - 4, N_IN):
                    evicted(pe, h0 + u)
                pe.wait_ge(sem("vx_ready"), l + 1)

                def keys_values(d, n):
                    tt, ht = (n // 2 if d == 0 else 1 - n // 2), n % 2
                    for j in range(2):
                        c = 256 * tt + P * ht + 64 * j
                        ins = pe.matmul(UB[d][n][64 * j:64 * j + 64, :], XX[:, 1 - d, c:c + 64],
                                        VX[:, tt, 2 * ht + j, :, :].rearrange("p a b -> p (a b)"), start=True, stop=True)
                    ins.then_inc(sem("u_done"), 1)

                def from_states(d):
                    pe.wait_ge(sem("state_ready"), 2 * l + d + 1)
                    for ht in range(2):
                        for ch in range(NCH):
                            for j in range(2):
                                o = slice(64 * j, 64 * j + 64)
                                c = 256 * ht + CHUNK * ch
                                ins = pe.matmul(M[0][o, c:c + CHUNK], ST[d][o, ht, ch, :], QB[o, d, c:c + CHUNK],
                                                start=j not in started, stop=(d == 1), skip_group_check=True)
                                started.add(j)
                    ins.then_inc(sem("inter_done"), 1)

                def over_channels(ready, src, c0, done):
                    pe.wait_ge(sem(ready), 2 * (l + 1))
                    for ct in range(2):
                        ins = pe.matmul(PS[1][:, c0:c0 + 256], cst("ones"), src[:, 256 * ct:256 * ct + 256], start=(ct == 0), stop=(ct == 1))
                    ins.then_inc(sem(done), 1)

                def over_heads(ready, lhs, done):
                    pe.wait_ge(sem(ready), l + 1)
                    for j in range(3):
                        n = 512 if j < 2 else 256
                        pe.matmul(M[1 + j][:, 0:n], cst(lhs), flat(QK2[:])[:, 512 * j:512 * j + n], start=True, stop=True).then_inc(sem(done), 1)

                pe.wait_ge(sem("kr_ready"), 2 * l + 1)
                for n in range(4):
                    keys_values(0, n)
                pe.wait_ge(sem("kr_ready"), 2 * l + 2)
                for n in range(3):
                    keys_values(1, n)
                pe.wait_ge(sem("state_ready"), 2 * l + 1)
                keys_values(1, 3)
                over_channels("cy0_ready", AC, 0, "csum_done")
                from_states(0)
                over_heads("qsq_ready", "blk", "qss_done")
                over_channels("csq_ready", EG, 256, "cvar_done")
                from_states(1)
                over_heads("qn_ready", "rot", "rot_done")
                pe.wait_ge(sem("hsq_ready"), l + 1)
                pe.matmul(PS[2][:], cst("blk"), XX[:, 0, :], start=True, stop=True).then_inc(sem("hss_done"), 1)
                pe.wait_ge(sem("qk_ready"), l + 1)
                attention_pe(8 * l, 8, lambda n: QK[64 * (n // 4):64 * (n // 4) + 64, n % 4, :],
                             lambda n: QK[64 * (n // 4):64 * (n // 4) + 64, 4, :],
                             lambda n, kt: VA[:, kt, 64 * (n // 4):64 * (n // 4) + 64], lambda n: 64 * (n // 4))
                pe.wait_ge(sem("mixl_ready"), 2 * l + 2)
                for u in range(N_OUT):
                    half(h0 + N_IN + u, "rr")
                h1 = h0 + N_IN + N_OUT
                transposes(2 + 2 * l, XS2, lambda: pe.wait_ge(sem("rows_ready"), 2 * l + 2))
                with pe.Fori(0, N_UP // 4) as it:
                    for u in range(4):
                        half(h1 + u, "cc", it, inst=2 * l + 2 if u == 0 else None)
                h2 = h1 + N_UP
                pe.wait_ge(sem("hid_ready"), 16 * (l + 1) + 2)
                for u in range(N_DOWN):
                    half(h2 + u, "rr", 0, HH, HL, 8 * (u // 4), u < 4, u >= N_DOWN - 4)
            k96 = slice(0, GLA_K)
            for l in range(DEPTH):
                s0 = HP_SECOND[l]
                transposes(5 + 2 * l, X, lambda: pe.wait_ge(sem("x_ready"), 2 * l + 1))
                if l > 0:
                    for u in range(N_SHARED):
                        half(HP_SHARED + u, "cc" if u < 3 else "rr", inst=7 if u == 0 else None)

                def mixing_panel(u):
                    half(s0 + u, "rr" if l == 0 and u >= 5 else "cc", inst=5 if l == 0 and u == 0 else None)

                if l == 0:
                    for u in range(4):
                        mixing_panel(u)
                    evicted(pe, s0)
                    pe.wait_ge(sem("mix_loaded0"), 64)
                    for h in range(4):
                        ins = pe.matmul(M[h // 2][k96, 256 * (h % 2):256 * (h % 2) + 256], WG2[96:112, GLA_K * h:GLA_K * h + GLA_K],
                                        GQ[96:112, 0, :], start=True, stop=True, tile_position=(96, 0))
                    ins.then_inc(sem("gpre_done"), 1)
                    mixing_panel(4)
                    mixing_panel(5)
                    pe.wait_ge(sem("lsig_ready"), 1)
                else:
                    mixing_panel(0)
                    pe.wait_ge(sem("mix_loaded1"), 48)
                evicted(pe, s0 + (4 if l == 0 else 0))
                p0 = 6 if l == 0 else 1
                attention_pe(16 + 4 * l, MEM_H, lambda n: QM[64 * (n % 2):64 * (n % 2) + 64, n // 2, :],
                             lambda n: KVL[64 * (n % 2):64 * (n % 2) + 64, 256 * (n // 2):256 * (n // 2) + 256],
                             lambda n, kt: KVL[:, 512 + 256 * kt + 64 * n:512 + 256 * kt + 64 * n + 64], lambda n: 64 * (n % 2), PM2, PT2,
                             panel=lambda n: mixing_panel(p0 + n))
                p1 = p0 + MEM_H + 1
                pe.wait_ge(sem("o_ready"), 16 + MEM_H * (l + 1))
                if l == 0:
                    for u in range(4):
                        evicted(pe, s0 + N_MIX2[l] - 4 + u)
                    pe.wait_ge(sem("gqk_ready"), 1)
                    for tt in range(TT):
                        for h in range(4):
                            ins = pe.transpose(M[2 + tt][:, GLA_K * h:GLA_K * h + GLA_K], KE[k96, h, P * tt:P * tt + P], cst("ident")[k96, k96])
                    ins.then_inc(sem("ket_done"), 1)
                    for h in range(4):
                        for ch in range(4):
                            c = slice(GLA_C * ch, GLA_C * ch + GLA_C)
                            a_ = GLA_C * (2 * h + ch // 2)
                            ins = pe.matmul(M[0][64 * (ch % 2):64 * (ch % 2) + 64, a_:a_ + GLA_C], KTD[k96, h, c], QTD[k96, h, c], start=True, stop=True)
                    ins.then_inc(sem("gatt_done"), 1)
                    pe.wait_ge(sem("gattm_ready"), 1)
                    pe.wait_ge(sem("ker_ready"), 1)
                    def chunk_keys_values(ch):
                        r, tt = slice(64 * (ch % 2), 64 * (ch % 2) + 64), ch // 2
                        for h in range(4):
                            ins = pe.matmul(UC[ch % 2][h // 2][k96, GLA_V * (h % 2):GLA_V * (h % 2) + GLA_V], KER[r, tt, GLA_K * h:GLA_K * h + GLA_K],
                                            GV[r, tt, GLA_V * h:GLA_V * h + GLA_V], start=True, stop=True)
                        ins.then_inc(sem("uc_done"), 1)

                    chunk_keys_values(0)
                    for ch in range(4):
                        r, tt = slice(64 * (ch % 2), 64 * (ch % 2) + 64), ch // 2
                        if ch == 0:
                            chunk_keys_values(1)
                        if ch >= 1:
                            pe.wait_ge(sem("sta_ready"), ch)
                            pe.wait_ge(sem("go_ready"), ch)
                        for h in range(4):
                            o = M[2 + h // 2][r, GLA_V * (h % 2):GLA_V * (h % 2) + GLA_V]
                            ins = pe.matmul(o, ATT[r, 2 * h + tt, :], GV[r, tt, GLA_V * h:GLA_V * h + GLA_V], start=True, stop=(ch == 0))
                            if ch > 0:
                                ins = pe.matmul(o, QTD[k96, h, GLA_C * ch:GLA_C * ch + GLA_C], STA[k96, h, :], start=False, stop=True)
                        ins.then_inc(sem("oc_done"), 1)
                        if ch == 1:
                            chunk_keys_values(2)
                    pe.wait_ge(sem("gon_ready"), 1)
                    for kt in range(6):
                        for tt in range(TT):
                            c = 256 * (kt % 2) + P * tt
                            ins = pe.transpose(M[kt // 2][:, c:c + P], GO2[:, tt, P * kt:P * kt + P], cst("ident"))
                    ins.then_inc(sem("got_done"), 1)
                else:
                    def slot_scores(n):
                        if n >= 1:
                            pe.wait_ge(sem("dsc_read"), n)
                        sl, qt = divmod(n, 2)
                        evicted(pe, s0 + 1 + (GROUPS * sl + GROUPS - 1) // 2)
                        for g in range(GROUPS):
                            ins = pe.matmul(M[g // 2][:, 256 * (g % 2):256 * (g % 2) + 256], QD[:, GROUPS * sl + g, P * qt:P * qt + P],
                                            KD[:, sl, :], start=True, stop=True)
                        ins.then_inc(sem("dsc_done"), 1)

                    slot_scores(0)
                    slot_scores(1)
                    for sl in range(SLOT_H):
                        if sl + 1 < SLOT_H:
                            slot_scores(2 * sl + 2)
                            slot_scores(2 * sl + 3)
                        pe.wait_ge(sem("dsm_ready"), 2 * sl + 2)
                        if sl >= 1:
                            pe.wait_ge(sem("dpt_ready"), sl)
                        for kt in range(2):
                            for qt in range(2):
                                ins = pe.transpose(M[2][:, 256 * kt + P * qt:256 * kt + P * qt + P], PD[:, sl % 2, qt, P * kt:P * kt + P], cst("ident"))
                        ins.then_inc(sem("dpt_done"), 1)
                        if p1 + sl < N_MIX2[l]:
                            mixing_panel(p1 + sl)
                        pe.wait_ge(sem("dpt_ready"), sl + 1)
                        if sl >= 1:
                            pe.wait_ge(sem("do_ready"), sl)
                        for kt in range(2):
                            ins = pe.matmul(M[3][:, 0:256], VD[:, kt, P * sl:P * sl + P], PTD[:, kt, :], start=(kt == 0), stop=(kt == 1))
                        ins.then_inc(sem("dpv_done"), 1)
                    pe.wait_ge(sem("do_ready"), SLOT_H)
                    pe.wait_ge(sem("dsc_read"), 2 * SLOT_H)
                pe.wait_ge(sem("mix2l_ready"), l + 1)
                for u in range(N_OUT):
                    half(s0 + N_MIX2[l] + u, "rr")
                w0 = s0 + N_MIX2[l] + N_OUT
                transposes(6 + 2 * l, X, lambda: pe.wait_ge(sem("x_ready"), 2 * l + 2))
                def head_scores(h):
                    evicted(pe, w0 + h)
                    if h >= 4:
                        pe.wait_ge(sem("keysc_ready"), PH * l + h - 3)
                    for tt in range(TT):
                        for side in range(2):
                            c = 256 * tt + P * side
                            ins = pe.matmul(M[h % 4][:, c:c + P], QP[:, 2 * h + side, P * tt:P * tt + P], SK[:, side, :], start=True, stop=True)
                    ins.then_inc(sem("keysc_done"), 1)

                pe.wait_ge(sem("keys_loaded"), 16 * (l + 1))
                for u in range(N_WQ):
                    half(w0 + u, "cc", inst=6 + 2 * l if u == 0 else None)
                    if u >= 1:
                        head_scores(u - 1)
                head_scores(PH - 1)
                d0 = w0 + N_WQ
                t0, s00 = (CHUNKS * STEPS) * l, PAIRS * l

                def expert_in(s, it=0):
                    i = d0 + u_at(s)
                    pe.wait_ge(lo_ready, i + 1 + it * 4)
                    if 2 <= s < AHEAD:
                        pe.wait_ge(sem("ahead_copied"), AHEAD * l + s - 1)
                    elif s >= AHEAD:
                        pe.wait_ge(sem("ge_ready"), s00 + s - 1 + it * 2)
                    wh, wl = (t[i % SLOTS][:].rearrange("p (k n) -> p k n", k=KT) for t in (HI, LO))
                    for c in range(2):
                        n = slice(P * c, P * c + P)
                        for k in range(KT):
                            ins = three(PS[s % 2][:, 256 * c:256 * c + 256], wh[:, k, n], wl[:, k, n], XH[:, k, :], XL[:, k, :], k == 0, k == KT - 1)
                    ins.then_inc(hp_used, 1)

                for s in range(AHEAD):
                    expert_in(s)
                pe.wait_ge(sem("keysc_ready"), 8 * l + 8)
                pe.wait_ge(sem("sel_ready"), l + 1)
                for c in range(3):
                    for tt in range(TT):
                        ins = pe.transpose(M[c // 2][:, 256 * (c % 2) + P * tt:256 * (c % 2) + P * tt + P], SEL[:, c, tt, :], cst("ident"))
                ins.then_inc(sem("selt_done"), 1)
                pe.wait_ge(sem("pf_ready"), l + 1)
                for n in range(4):
                    for j in range(4):
                        pe.matmul(M[n][:, P * j:P * j + P], cst("zero"), cst("zero"), start=(j == 0), stop=False, skip_group_check=True)
                def table(q, k, it=0, per=2):
                    n = t0 + STEPS * q + k
                    pe.wait_ge(sem("oa_ready"), n + 1 + it * per)
                    pe.wait_ge(sem("ob_ready"), n + 1 + it * per)
                    if n >= 2:
                        pe.wait_ge(sem("table_ready"), n - 1 + it * per)
                    oa, ob = (OA2, OB2) if q == 0 and k % 2 == 0 else (OA, OB)
                    for t in range(TPS):
                        for c in range(3):
                            ins = pe.matmul(PS[2 + k % 2][:, BC * t:BC * t + BC], oa[:, :, t], ob[:, c, :, t], start=(c == 0), stop=(c == 2))
                    ins.then_inc(sem("table_done"), 1)

                def expert_out(s, it=0):
                    i = d0 + v_at(s)
                    pe.wait_ge(lo_ready, i + 1 + it * 4)
                    pe.wait_ge(sem("al_ready"), s00 + s + 1 + it * 2)
                    vh, vl = (t[i % SLOTS][:].rearrange("p (b n) -> p b n", b=2) for t in (HI, LO))
                    for bi in range(2):
                        for tt in range(TT):
                            for n in range(2):
                                c = slice(512 * n, 512 * n + 512)
                                m = slice(256 * bi + P * tt, 256 * bi + P * tt + P)
                                ins = three(M[2 * tt + n][:], AH[s % 2][:, m], AL[s % 2][:, m], vh[:, bi, c], vl[:, bi, c], False, False, skip_group_check=True)
                    ins.then_inc(hp_used, 1)

                def dense_step(q, j, it=0):
                    s = STEPS * q + j
                    if AHEAD <= s + 1 < PAIRS:
                        expert_in(s + 1, it)
                    two = q == 0 and AHEAD - 1 <= j < STEPS - 1
                    if two:
                        table(1, 2 * (j - AHEAD + 1), it, 4)
                    elif 0 < q < CHUNKS - 1:
                        table(q + 1, j, it)
                    expert_out(s, it)
                    if two:
                        table(1, 2 * (j - AHEAD + 1) + 1, it, 4)

                for k in range(STEPS):
                    table(0, k)
                for j in range(AHEAD - 1):
                    dense_step(0, j)
                for q in range(CHUNKS):
                    j0 = AHEAD - 1 if q == 0 else 0
                    with pe.Fori(0, (STEPS - 1 - j0) // 2 - (q == 0)) as it:
                        for j in (j0, j0 + 1):
                            dense_step(q, j, it)
                    for j in range(STEPS - 3 if q == 0 else STEPS - 2, STEPS):
                        dense_step(q, j)
                for n in range(4):
                    ins = pe.matmul(M[n][:, 0:P], cst("zero"), cst("zero"), start=False, stop=True, skip_group_check=True)
                ins.then_inc(sem("f_done"), 1)



def _half_panels(w):
    n = w.shape[1]
    return w.reshape(KT, P, n // 256, 256).transpose(2, 1, 0, 3).reshape(n // 256, P, HP)


def _constants():
    c = np.zeros((P, N_CONST), np.float32)
    i = np.arange(P)

    def put(name, v):
        a, b = CONST[name]
        c[:, a:b] = v

    put("ident", np.eye(P))
    put("iota", i[None, :])
    put("blk", (i[:, None] // HEAD) == (i[None, :] // HEAD))
    put("ones", 1.0)
    rot = np.zeros((P, P))
    for m in range(P):
        if m % 32 < 16:
            rot[m + 16, m] = -1.0
        else:
            rot[m - 16, m] = 1.0
    put("rot", rot)
    tok = np.arange(TOK)
    inv = (np.float32(10000.0) ** (-np.arange(0, 32, 2, dtype=np.float32) / np.float32(32)))
    pos = np.where(((i % 64) // 32 == 0)[:, None], (tok // 64)[None, :], (tok % 64)[None, :]).astype(np.float32)
    ang = pos * inv[i % 16][:, None]
    put("cos", np.cos(ang))
    put("sin", np.sin(ang))
    put("chunkmask", (i[:, None] // CHUNK) == np.arange(8)[None, :])
    j = np.arange(16)
    for name, v in (("first", j == 0), ("notfirst", j > 0), ("last", j == 15), ("notlast", j < 15)):
        put(name, v)
    put("gscan", (np.arange(64) > 0))
    put("causal", (i % 64)[:, None] <= np.arange(64)[None, :])
    return c


def _order_in():
    sizes = [512, 128, 128, 256, 256, 256, 256, 256, 256, 256]
    at = np.concatenate([[0], np.cumsum(sizes)])
    qa, ka, va, qh, ih, ff, fb, gh, ac, gc = [np.arange(at[n], at[n + 1]) for n in range(10)]
    heads = qa.reshape(8, HEAD)
    q = np.concatenate([heads[[c, c + 4]].reshape(-1) for c in range(4)])
    return np.concatenate([ih, qh, ff, fb, gh, ac, gc, ka, va, q])


def _order_out():
    heads = np.arange(512).reshape(8, HEAD)
    return np.concatenate([heads[[c, c + 4]].reshape(-1) for c in range(4)] + [np.arange(512, 1024)])


def _columns(v):
    return v.reshape(v.shape[0], -1, P).transpose(0, 2, 1)


def layout_first(inp):
    f = lambda n: np.asarray(inp[n])
    parts = []
    wm = f("w_mem_kv_2")
    for l in range(DEPTH):
        parts.append(_half_panels(wm[l]))
    oi, oo = _order_in(), _order_out()
    for l in range(DEPTH):
        parts.append(_half_panels(f("w_in")[l][:, oi]))
        parts.append(_half_panels(f("w_out")[l][oo]))
        parts.append(_half_panels(f("w_mlp_in")[l]))
        for kc in range(4):
            parts.append(_half_panels(f("w_mlp_out")[l][1024 * kc:1024 * kc + 1024]))
    par = np.concatenate([
        _columns(f("norm_mix")), _columns(f("norm_mlp")),
        np.tile(f("q_norm"), (1, 2))[:, :, None], np.tile(f("k_norm"), (1, 2))[:, :, None],
        _columns(f("hgrn_norm")),
        f("conv_w").reshape(DEPTH, CONV_K, 2, P).transpose(0, 3, 2, 1).reshape(DEPTH, P, 62),
        _columns(f("conv_b")), _columns(f("conv_ln_g")), _columns(f("conv_ln_b"))], axis=2)
    lb = np.stack([f("hgrn_lb_fwd"), f("hgrn_lb_bwd")], 1).reshape(DEPTH, 2, 2, P).transpose(3, 0, 1, 2).reshape(P, 8)
    lb = np.concatenate([lb, np.zeros((P, 8), np.float32)], 1)
    return parts, par, lb


def layout_second(inp):
    f = lambda n: np.asarray(inp[n])
    parts = []
    qk = np.arange(GLA_H * GLA_K).reshape(GLA_H, GLA_K)
    wa = f("a_w_in_2")[0]
    n_qk, n_v = GLA_H * GLA_K, GLA_H * GLA_V
    gate0 = 2 * n_qk + 2 * n_v
    pad = np.zeros((D, 2 * GLA_H, P), np.float32)
    pad[:, :, :GLA_K] = wa[:, :2 * n_qk].reshape(D, 2 * GLA_H, GLA_K)
    pad[:, 0, GLA_K:GLA_K + 16] = wa[:, gate0:gate0 + 16]
    a_in = np.concatenate([pad.reshape(D, -1), wa[:, gate0 + 16:], wa[:, 2 * n_qk:gate0]], axis=1)
    wb, n_q = f("b_w_in_2")[0], GROUPS * SLOT_H * P
    b_in = np.concatenate([wb[:, n_q:], wb[:, :n_q].reshape(D, GROUPS, SLOT_H, P).transpose(0, 2, 1, 3).reshape(D, n_q)], axis=1)
    for l, w_in in enumerate([a_in, b_in]):
        if l > 0:
            parts.append(_half_panels(f("shared_w_kv_2")))
        parts.append(_half_panels(w_in))
        parts.append(_half_panels(f("w_out_2")[l]))
        parts.append(_half_panels(f("peer_w_q_2")[l]))
        u = f("peer_u_2")[l].reshape(KEYS, PAIRS, 2, KT, P).transpose(1, 4, 3, 2, 0).reshape(PAIRS, P, HP)
        v = f("peer_v_2")[l].reshape(KEYS, PAIRS, 2, D).transpose(1, 0, 2, 3).reshape(PAIRS, P, HP)
        dense = np.empty((2 * PAIRS, P, HP), np.float32)
        for s in range(PAIRS):
            dense[u_at(s)], dense[v_at(s)] = u[s], v[s]
        parts.append(dense)
    par2 = np.zeros((P, 16), np.float32)
    par2[:GLA_K, 0:GLA_H] = f("a_b_gate_2")[0].reshape(GLA_H, GLA_K).T
    par2[:, 4:10] = f("a_norm_g_2")[0].reshape(6, P).T
    rows = np.stack([np.stack([f(f"ln_{n}_g_2")[l], f(f"ln_{n}_b_2")[l]]) for l in range(DEPTH) for n in ("mix", "ffn")])
    keys = np.ascontiguousarray(f("peer_sub_keys_2").transpose(0, 3, 1, 2))
    return parts, par2, np.ascontiguousarray(f("a_w_gate2_2")[0]), rows, keys


def _dilated_mask():
    i, j = np.arange(TOK)[:, None], np.arange(TOK)[None, :]
    groups = [(i >= j) & (i - j <= w) & ((i - j) % d == 0) for w, d in ((128, 1), (512, 4), (2048, 16))]
    m = np.where(np.stack(groups, 1), 0.0, NEG).astype(np.float32)
    return np.ascontiguousarray(m.reshape(TT, P, GROUPS * TOK).transpose(1, 0, 2))


def kernel(**inputs):
    import concourse.bacc as _bacc
    from concourse.bass_utils import run_bass_kernel_spmd

    parts, par, lb = layout_first(inputs)
    more, par2, wg2, rows, keys = layout_second(inputs)
    f = lambda n: np.asarray(inputs[n])
    arrays = {"stream": np.concatenate(parts + more, 0), "x": f("x")[0], "mem": f("mem_2")[0], "consts": _constants(),
              "par": np.ascontiguousarray(par), "lb": np.ascontiguousarray(lb), "par2": par2, "wg2": wg2,
              "mask": _dilated_mask(), "rows": rows, "keys": keys}
    nc = _bacc.Bacc("TRN2", target_bir_lowering=False, num_devices=1)
    aps = {k: nc.dram_tensor(k, v.shape, F32, kind="ExternalInput").ap() for k, v in arrays.items()}
    out = nc.dram_tensor("out", (TOK, D), F32, kind="ExternalOutput").ap()
    build(nc, aps["stream"], aps["x"], aps["mem"], aps["consts"], aps["par"], aps["lb"], aps["par2"], aps["wg2"], aps["mask"],
          aps["rows"], aps["keys"], out)
    r = run_bass_kernel_spmd(nc, [arrays], core_ids=[0])
    return np.asarray(r.results[0]["out"]).reshape(1, TOK, D)
```
